# Optimizing a Trainium2 kernel written in Bass

```python
import jax, jax.numpy as jnp
from jax import lax
import numpy as np

D_MODEL = 1024
BATCH = 1
SEQ = 256
DEPTH = 1
DEC_BATCH = 1
DEC_SEQ = 32
PAST_LEN = 256

CHUNK = 64
EPS = 1e-6
D_POOL = D_MODEL // 2
POOL_WINDOWS = (2, 4, 8, 16)
POOL_GROUPS = len(POOL_WINDOWS)
POOL_GW = D_POOL // POOL_GROUPS
POOL_OUT_GW = D_MODEL // POOL_GROUPS
POOL_PAD = max(POOL_WINDOWS) - 1
D_CONV = D_MODEL // 2
CONV_WIDTH = 31
CONV_PAD = CONV_WIDTH - 1
N_EXPERTS = 32
TOP_K = 4
D_FF = D_MODEL
SWIGLU_LIMIT = 7.0
SWIGLU_ALPHA = 1.702
D_IN = D_POOL + 2 * D_CONV

kernel_name = "hybrid_pool_conformer_moe_stream_step"

def _rms_norm(x, g):
    xf = x.astype(jnp.float32)
    y = xf * lax.rsqrt(jnp.mean(xf * xf, axis=-1, keepdims=True) + EPS)
    return (y * g.astype(jnp.float32)).astype(x.dtype)

def _pool_mix(u, buf, pos0, pool_w, pool_scale):
    B, L, _ = u.shape
    full = jnp.concatenate([buf, u], axis=1)
    cs = jnp.cumsum(full.astype(jnp.float32), axis=1)
    cs = jnp.pad(cs, ((0, 0), (1, 0), (0, 0)))
    pos = pos0 + jnp.arange(L)
    outs = []
    for gi, w in enumerate(POOL_WINDOWS):
        seg = cs[:, :, gi * POOL_GW:(gi + 1) * POOL_GW]
        s = seg[:, POOL_PAD + 1:] - seg[:, POOL_PAD + 1 - w:POOL_PAD + 1 - w + L]
        cnt = jnp.minimum(pos + 1, w).astype(jnp.float32)
        mean = s / cnt[None, :, None]
        outs.append(mean - u[:, :, gi * POOL_GW:(gi + 1) * POOL_GW].astype(jnp.float32))
    pooled = jnp.stack(outs, axis=2).astype(u.dtype)
    y = jnp.einsum('blgc,gco->blgo', pooled, pool_w).reshape(B, L, D_MODEL)
    return y * pool_scale, full[:, -POOL_PAD:]

def _conv_mix(v, buf, conv_dw, conv_b, ln_g, ln_b, w_out_conv):
    a, g = v[..., :D_CONV], v[..., D_CONV:]
    u = a * jax.nn.sigmoid(g)
    full = jnp.concatenate([buf, u], axis=1)
    y = lax.conv_general_dilated(full, conv_dw[:, None, :], window_strides=(1,), padding='VALID',
                                 dimension_numbers=('NWC', 'WIO', 'NWC'),
                                 feature_group_count=D_CONV) + conv_b
    yf = y.astype(jnp.float32)
    mu = jnp.mean(yf, axis=-1, keepdims=True)
    var = jnp.mean(jnp.square(yf - mu), axis=-1, keepdims=True)
    yn = ((yf - mu) * lax.rsqrt(var + EPS) * ln_g + ln_b).astype(v.dtype)
    return jax.nn.silu(yn) @ w_out_conv, full[:, -CONV_PAD:]

def _moe(h, router_w, router_b, exp_w_gate, exp_b_gate, exp_w_up, exp_b_up, exp_w_down, exp_b_down):
    B, L, _ = h.shape
    t = h.reshape(B * L, D_MODEL)
    logits = (t @ router_w + router_b).astype(jnp.float32)
    top_vals, top_idx = lax.top_k(logits, TOP_K)
    top_w = jax.nn.softmax(top_vals, axis=-1)
    combine = jnp.sum(jax.nn.one_hot(top_idx, N_EXPERTS, dtype=jnp.float32) * top_w[..., None], axis=1)
    out = jnp.zeros((B * L, D_MODEL), jnp.float32)
    for e in range(N_EXPERTS):
        gt = jnp.minimum(t @ exp_w_gate[e] + exp_b_gate[e], SWIGLU_LIMIT)
        up = jnp.clip(t @ exp_w_up[e] + exp_b_up[e], -SWIGLU_LIMIT, SWIGLU_LIMIT)
        act = gt * jax.nn.sigmoid(SWIGLU_ALPHA * gt) * (up + 1.0)
        out = out + combine[:, e:e + 1] * (act @ exp_w_down[e] + exp_b_down[e]).astype(jnp.float32)
    return out.astype(h.dtype).reshape(B, L, D_MODEL)

def _layer(x, c, pool_buf, conv_buf, pos0, norm1_g, norm2_g, w_ada, b_ada, w_in, pool_w, pool_scale,
           conv_dw, conv_b, conv_ln_g, conv_ln_b, conv_w_out, gate_w, gate_b, w_out,
           router_w, router_b, exp_w_gate, exp_b_gate, exp_w_up, exp_b_up, exp_w_down, exp_b_down):
    B = x.shape[0]
    mod = (jax.nn.silu(c) @ w_ada + b_ada).reshape(B, 6, 1, D_MODEL)
    sh1, sc1, g1, sh2, sc2, g2 = mod[:, 0], mod[:, 1], mod[:, 2], mod[:, 3], mod[:, 4], mod[:, 5]
    h = _rms_norm(x, norm1_g) * (1.0 + sc1) + sh1
    proj = h @ w_in
    a, new_pool = _pool_mix(proj[..., :D_POOL], pool_buf, pos0, pool_w, pool_scale)
    b, new_conv = _conv_mix(proj[..., D_POOL:], conv_buf, conv_dw, conv_b, conv_ln_g, conv_ln_b, conv_w_out)
    gates = jax.nn.sigmoid(h @ gate_w + gate_b)
    merged = gates[..., :D_MODEL] * a + gates[..., D_MODEL:] * b
    x = x + g1 * (merged @ w_out)
    h2 = _rms_norm(x, norm2_g) * (1.0 + sc2) + sh2
    x = x + g2 * _moe(h2, router_w, router_b, exp_w_gate, exp_b_gate, exp_w_up, exp_b_up, exp_w_down, exp_b_down)
    return x, new_pool, new_conv

def setup_inputs(seed: int = 0) -> dict:
    key = jax.random.key(seed)
    ks = jax.random.split(key, 32)
    f32 = jnp.float32

    def nrm(k, shape, scale):
        return jax.random.normal(k, shape, f32) * scale

    D = D_MODEL
    return {
        "x_prompt": nrm(ks[0], (BATCH, SEQ, D), 1.0),
        "x_sample": nrm(ks[1], (DEC_BATCH, DEC_SEQ, D), 1.0),
        "state_pool": nrm(ks[2], (DEPTH, DEC_BATCH, POOL_PAD, D_POOL), 1.0),
        "state_conv": nrm(ks[3], (DEPTH, DEC_BATCH, CONV_PAD, D_CONV), 1.0),
        "c_prompt": nrm(ks[4], (BATCH, D), 1.0),
        "c_sample": nrm(ks[5], (DEC_BATCH, D), 1.0),
        "norm1_g": 1.0 + nrm(ks[6], (DEPTH, D), 0.02),
        "norm2_g": 1.0 + nrm(ks[7], (DEPTH, D), 0.02),
        "final_g": 1.0 + nrm(ks[8], (D,), 0.02),
        "w_ada": nrm(ks[9], (DEPTH, D, 6 * D), 0.3 * D ** -0.5),
        "b_ada": nrm(ks[10], (DEPTH, 6 * D), 0.02),
        "w_in": nrm(ks[11], (DEPTH, D, D_IN), D ** -0.5),
        "pool_w": nrm(ks[12], (DEPTH, POOL_GROUPS, POOL_GW, POOL_OUT_GW), POOL_GW ** -0.5),
        "pool_scale": 1.0 + nrm(ks[13], (DEPTH, D), 0.02),
        "conv_dw": nrm(ks[14], (DEPTH, CONV_WIDTH, D_CONV), CONV_WIDTH ** -0.5),
        "conv_b": nrm(ks[15], (DEPTH, D_CONV), 0.02),
        "conv_ln_g": 1.0 + nrm(ks[16], (DEPTH, D_CONV), 0.02),
        "conv_ln_b": nrm(ks[17], (DEPTH, D_CONV), 0.02),
        "conv_w_out": nrm(ks[18], (DEPTH, D_CONV, D), D_CONV ** -0.5),
        "gate_w": nrm(ks[19], (DEPTH, D, 2 * D), D ** -0.5),
        "gate_b": nrm(ks[20], (DEPTH, 2 * D), 0.02),
        "w_out": nrm(ks[21], (DEPTH, D, D), D ** -0.5),
        "router_w": nrm(ks[22], (DEPTH, D, N_EXPERTS), D ** -0.5),
        "router_b": nrm(ks[23], (DEPTH, N_EXPERTS), 0.01),
        "exp_w_gate": nrm(ks[24], (DEPTH, N_EXPERTS, D, D_FF), D ** -0.5),
        "exp_b_gate": nrm(ks[25], (DEPTH, N_EXPERTS, D_FF), 0.01),
        "exp_w_up": nrm(ks[26], (DEPTH, N_EXPERTS, D, D_FF), D ** -0.5),
        "exp_b_up": nrm(ks[27], (DEPTH, N_EXPERTS, D_FF), 0.01),
        "exp_w_down": nrm(ks[28], (DEPTH, N_EXPERTS, D_FF, D), D_FF ** -0.5),
        "exp_b_down": nrm(ks[29], (DEPTH, N_EXPERTS, D), 0.01),
    }

def reference(x_prompt, x_sample, state_pool, state_conv, c_prompt, c_sample,
              norm1_g, norm2_g, final_g, w_ada, b_ada, w_in, pool_w, pool_scale,
              conv_dw, conv_b, conv_ln_g, conv_ln_b, conv_w_out, gate_w, gate_b, w_out,
              router_w, router_b, exp_w_gate, exp_b_gate, exp_w_up, exp_b_up, exp_w_down, exp_b_down):
    xp, xs = x_prompt, x_sample
    Bp = x_prompt.shape[0]
    pool_p, conv_p, pool_s, conv_s = [], [], [], []
    for l in range(DEPTH):
        lp = (norm1_g[l], norm2_g[l], w_ada[l], b_ada[l], w_in[l], pool_w[l], pool_scale[l],
              conv_dw[l], conv_b[l], conv_ln_g[l], conv_ln_b[l], conv_w_out[l], gate_w[l], gate_b[l], w_out[l],
              router_w[l], router_b[l], exp_w_gate[l], exp_b_gate[l], exp_w_up[l], exp_b_up[l],
              exp_w_down[l], exp_b_down[l])
        zp = jnp.zeros((Bp, POOL_PAD, D_POOL), xp.dtype)
        zc = jnp.zeros((Bp, CONV_PAD, D_CONV), xp.dtype)
        xp, npp, ncp = _layer(xp, c_prompt, zp, zc, 0, *lp)
        xs, nps, ncs = _layer(xs, c_sample, state_pool[l], state_conv[l], PAST_LEN, *lp)
        pool_p.append(npp); conv_p.append(ncp); pool_s.append(nps); conv_s.append(ncs)
    y_prompt = _rms_norm(xp, final_g)
    y_sample = _rms_norm(xs, final_g)
    new_pool_prompt = jnp.stack(pool_p, axis=0)
    new_conv_prompt = jnp.stack(conv_p, axis=0)
    new_pool_sample = jnp.stack(pool_s, axis=0)
    new_conv_sample = jnp.stack(conv_s, axis=0)
    return (y_prompt, y_sample, new_pool_prompt, new_conv_prompt, new_pool_sample, new_conv_sample)


_drawn_inputs = setup_inputs


def setup_inputs(seed=0):
    import zlib

    import numpy as np

    out = dict(_drawn_inputs(seed))
    spreads = {}
    factors = {'state_pool': 3.946,
     'norm2_g': 4.665,
     'final_g': 8.887,
     'pool_scale': 7.116,
     'conv_b': 8.0,
     'conv_ln_g': 8.0,
     'conv_ln_b': 8.0,
     'gate_b': 8.0,
     'router_b': 4.356,
     'exp_b_gate': 31.609,
     'exp_b_up': 32.96,
     'exp_b_down': 64.0}
    for name, (base, spread) in spreads.items():
        noise = np.random.default_rng([zlib.crc32(name.encode()), seed]).standard_normal(out[name].shape)
        drawn = base * np.exp(spread * noise) if base else spread * noise
        out[name] = __import__('jax').numpy.asarray(drawn.astype(out[name].dtype))
    for name, factor in factors.items():
        out[name] = (out[name] * factor).astype(out[name].dtype)
    return out
```

```python
from contextlib import ExitStack

import concourse.bass as bass
from concourse import mybir

F32 = mybir.dt.float32
I32 = mybir.dt.int32
ALU = mybir.AluOpType
ACT = mybir.ActivationFunctionType
AX = mybir.AxisListType.X

P = 128
D = 1024
KD = D // P
NP_TOK, NS_TOK = 256, 32
TOK = NP_TOK + NS_TOK
TT = 3
ROWS = [P, P, NS_TOK]
EPS = 1e-6
WINDOWS = (2, 4, 8, 16)
POOL_PAD = max(WINDOWS) - 1
WIDTH = 31
CONV_PAD = WIDTH - 1
DC = D // 2
CT = DC // P
E = 32
TOPK = 4
LIMIT = 7.0
ALPHA = 1.702
SLOTS = 64
MAX_ROUNDS = -(-TOK // SLOTS)
HALF = 512
PSEG = [(POOL_PAD, 0, NP_TOK), (2 * POOL_PAD + NP_TOK, NP_TOK, NS_TOK)]
CSEG = [(CONV_PAD, 0, NP_TOK), (2 * CONV_PAD + NP_TOK, NP_TOK, NS_TOK)]
PEXT = TOK + 2 * POOL_PAD
CEXT = TOK + 2 * CONV_PAD
CW = CEXT - CONV_PAD

RING = 12
SLOT = 2 * D
PIECES = 12
FRONT = ([("ada", 0, k) for k in range(KD)] + [("in", c, 0) for c in (4, 2, 5, 3, 0, 1)]
         + [("gate", c, 0) for c in range(8)] + [("ada", b, k) for b in (1, 2) for k in range(KD)]
         + [("pool", 0, 0)] + [("conv", h, 0) for h in range(2)] + [("out", h, q) for h in range(2) for q in range(2)])
N_FRONT = len(FRONT)
F_END = -(-N_FRONT // RING) * RING
USES = [len([f for f in range(N_FRONT) if f % RING == s]) for s in range(RING)]
PAIRS = E // 2

C_N1, C_GB, C_PS, C_CB, C_LG, C_LB, C_CP, C_CS, N_COLS = 0, 8, 24, 32, 36, 40, 44, 52, 60


def build(nc, x_prompt, x_sample, state_pool, state_conv, c_prompt, c_sample, norm1_g, norm2_g, final_g,
          w_ada, b_ada, w_in, pool_w, pool_scale, conv_dw, conv_b, conv_ln_g, conv_ln_b, conv_w_out,
          gate_w, gate_b, w_out, router_w, router_b, exp_w_gate, exp_b_gate, exp_w_up, exp_b_up,
          exp_w_down, exp_b_down, y_prompt, y_sample, new_pool_p, new_conv_p, new_pool_s, new_conv_s):
    with ExitStack() as ctx:
        def sb(name, shape, dt=F32):
            return ctx.enter_context(nc.sbuf_tensor(name, shape, dt))

        def sem(name):
            return ctx.enter_context(nc.semaphore(name))

        ring = sb("ring", [P, RING, SLOT])
        x = sb("x", [P, TT, D])
        h2 = sb("h2", [P, TT, D])
        ident = sb("ident", [P, P])
        before = sb("before", [P, P])
        ones = sb("ones", [P, P])
        slot_no = sb("slot_no", [P, 2, SLOTS])
        pick = sb("pick", [P, 8, P])
        ada_sel = sb("ada_sel", [12, 12, 32])
        bada = sb("bada", [12, HALF])
        n2rows = sb("n2rows", [64, HALF])
        stage = sb("stage", [N_COLS, P])
        cols = sb("cols", [P, N_COLS])
        dwc = sb("dwc", [P, CT, 32])
        biases = sb("biases", [P, 2, D])
        rw = sb("rw", [P, KD, E])
        rb = sb("rb", [1, E])
        cT = sb("cT", [P, KD, 32])
        csig = sb("csig", [P, 16])
        shc = sb("shc", [P, 2 * KD])
        scc = sb("scc", [P, 2 * KD])
        invc = sb("invc", [P, CT, 16])
        stat = sb("stat", [P, 32])
        logit = sb("logit", [P, TT, E])
        rt = sb("rt", [P, 8, TT, E])
        top = sb("top", [P, TT, 8])
        routed = sb("routed", [P, 2, TT, E + 1])
        pairc = sb("pairc", [P, 2, 2 * TT, 2])
        nround = sb("nround", [P, 1], I32)
        npair = sb("npair", [P, 1], I32)
        arena = sb("arena", [P, 15088])

        def view(start, *shape):
            n = 1
            for s in shape:
                n *= s
            a = arena[:, start:start + n]
            if len(shape) == 2:
                a = a.rearrange("p (a b) -> p a b", b=shape[1])
            return a

        hT = view(0, KD, TOK)
        gates = view(2304, 2 * KD, TOK)
        merged = view(6912, KD, TOK)
        sig_g = view(6912, CT, TOK)
        up_ext = view(9216, CT, PEXT)
        pooled = view(10488, CT, TOK)
        wsum = view(11640, 2, PEXT)
        rows = view(12276, 3, HALF)
        tmp = view(13812, CT, CW)
        act_c = view(0, CT, TOK)
        slot_i = view(13812, 2, SLOTS).bitcast(I32)
        h2flat = h2[:, :, :].rearrange("p a b -> p (a b)")
        uc_ext = h2flat[:, 0:CT * CEXT].rearrange("p (a b) -> p a b", b=CEXT)
        yc = h2flat[:, CT * CEXT:CT * CEXT + CT * CW].rearrange("p (a b) -> p a b", b=CW)
        g1b = view(0, 2, D)
        a2b = view(2304, 2, D)
        sh2b = view(4352, 2, D)
        g2b = view(9216, 2, D)
        h2T = view(6912, KD, TOK)
        acc = view(2304, TT, D)
        xg = view(5376, HALF)
        xgT = view(5888, HALF)
        ohwT = view(6400, TT * P)
        gmin = view(0, HALF)
        gsig = view(512, HALF)
        ucl = view(1024, HALF)
        acts = view(1536, HALF)
        actT = view(6912, HALF)
        ysb = view(7424, HALF)
        oh = view(7936, 2 * TT, SLOTS)
        ohw = view(8320, 2 * TT, 2 * SLOTS)
        fgb = view(11640, D)
        wT = view(12664, TOK)
        bd_rows = view(13812, D)[0:E, :]
        bias_row = [biases[0:1, :, :], view(12952, 2, D)[0:1, :, :]]
        ybuf = h2

        bank = [ctx.enter_context(nc.psum_tensor(f"bank{i}", [P, HALF], F32)) for i in range(8)]

        slot_ld = [sem(f"slot_ld{s}") for s in range(RING)]
        piece_used = sem("piece_used")
        x_ld = sem("x_ld")
        c_ld = sem("c_ld")
        dw_ld = sem("dw_ld")
        st_ld = sem("st_ld")
        ada_ld = sem("ada_ld")
        n2_ld = sem("n2_ld")
        router_ld = sem("router_ld")
        bd_ld = sem("bd_ld")
        fg_ld = sem("fg_ld")
        bias_ld = [sem("bias_ld0"), sem("bias_ld1")]
        const = sem("const")
        chain_p = sem("chain_p")
        ssq = sem("ssq")
        chain_v = sem("chain_v")
        chain_a = sem("chain_a")
        xn_ready = sem("xn_ready")
        colT = sem("colT")
        cols_ready = sem("cols_ready")
        csig_ready = sem("csig_ready")
        cT_ready = sem("cT_ready")
        dwT = sem("dwT")
        dw_ready = sem("dw_ready")
        stT = sem("stT")
        hist_ready = sem("hist_ready")
        xT = sem("xT")
        xT_ev = sem("xT_ev")
        ada_mm = sem("ada_mm")
        rows_ready = sem("rows_ready")
        modT = sem("modT")
        mod_ready = sem("mod_ready")
        hT_ready = sem("hT_ready")
        in_mm = sem("in_mm")
        in_ev = sem("in_ev")
        sig_ready = sem("sig_ready")
        u_ready = sem("u_ready")
        pu_ready = sem("pu_ready")
        gate_mm = sem("gate_mm")
        gate_ev = sem("gate_ev")
        a2rows = sem("a2rows")
        outT = sem("outT")
        out_ev = sem("out_ev")
        pooled_ready = sem("pooled_ready")
        conv_step = sem("conv_step")
        mean_mm = sem("mean_mm")
        mean_ready = sem("mean_ready")
        cen_ready = sem("cen_ready")
        sq_ready = sem("sq_ready")
        zeroed = sem("zeroed")
        var_mm = sem("var_mm")
        std_ready = sem("std_ready")
        yn_ready = sem("yn_ready")
        zsig_ready = sem("zsig_ready")
        act_c_ready = sem("act_c_ready")
        pm_mm = sem("pm_mm")
        pm_ev = sem("pm_ev")
        cm_mm = sem("cm_mm")
        cm_ev = sem("cm_ev")
        merged_ready = sem("merged_ready")
        bc_mm = sem("bc_mm")
        bc_ev = sem("bc_ev")
        wo_mm = sem("wo_mm")
        wo_ev = sem("wo_ev")
        x2_ready = sem("x2_ready")
        ssq2 = sem("ssq2")
        sqrt_ready = sem("sqrt_ready")
        mean2 = sem("mean2")
        h2_ready = sem("h2_ready")
        h2T_mm = sem("h2T_mm")
        h2T_even = sem("h2T_even")
        h2T_odd = sem("h2T_odd")
        hist0_ready = sem("hist0_ready")
        logit_mm = sem("logit_mm")
        shifted = sem("shifted")
        exp_ready = sem("exp_ready")
        sel_ready = sem("sel_ready")
        rank_mm = sem("rank_mm")
        w_ready = sem("w_ready")
        wT_mm = sem("wT_mm")
        wT_ev = sem("wT_ev")
        accb_mm = sem("accb_mm")
        acc_init = sem("acc_init")
        rounds_ready = sem("rounds_ready")
        work_zero = sem("work_zero")
        oh_ready = sem("oh_ready")
        xg_mm = sem("xg_mm")
        xg_ev = sem("xg_ev")
        tpa_mm = sem("tpa_mm")
        tpa_ev = sem("tpa_ev")
        gate_done = sem("gate_done")
        gate_read = sem("gate_read")
        gsig_ready = sem("gsig_ready")
        up_done = sem("up_done")
        up_read = sem("up_read")
        gs_ready = sem("gs_ready")
        act_ready = sem("act_ready")
        actT_mm = sem("actT_mm")
        actT_ev = sem("actT_ev")
        y_mm = sem("y_mm")
        y_ev = sem("y_ev")
        scat_mm = sem("scat_mm")
        scat_add = sem("scat_add")
        cols_copied = sem("cols_copied")
        ssq3 = sem("ssq3")
        sqrt3 = sem("sqrt3")
        y_ready = sem("y_ready")
        stored = sem("stored")

        wada_v = w_ada[0].rearrange("(k p) n -> k p n", p=P)
        win_v = w_in[0].rearrange("(k p) n -> p k n", p=P)
        gate_v = gate_w[0].rearrange("(k p) n -> p k n", p=P)
        poolw_v = pool_w[0].rearrange("g c o -> c g o")
        convw_v = conv_w_out[0].rearrange("(k p) n -> p k n", p=P)
        wout_v = w_out[0].rearrange("(k p) n -> p k n", p=P)
        wg_v = exp_w_gate[0].rearrange("e (k p) n -> e p k n", p=P)
        wu_v = exp_w_up[0].rearrange("e (k p) n -> e p k n", p=P)
        wd_v = exp_w_down[0].rearrange("e (k p) n -> e p k n", p=P)

        def front_piece(f):
            kind, a, b = FRONT[f]
            slot = ring[:, f % RING, :]
            if kind == "ada":
                return wada_v[b][:, 4 * HALF * a:4 * HALF * (a + 1)], slot
            if kind in ("in", "gate"):
                src = win_v if kind == "in" else gate_v
                return src[:, :, 256 * a:256 * (a + 1)], slot.rearrange("p (k n) -> p k n", k=KD)
            if kind == "pool":
                return poolw_v, slot[:, 0:D].rearrange("p (k n) -> p k n", k=CT)
            if kind == "conv":
                return convw_v[:, :, HALF * a:HALF * (a + 1)], slot.rearrange("p (k n) -> p k n", k=CT)
            return (wout_v[:, 4 * b:4 * b + 4, HALF * a:HALF * (a + 1)], slot.rearrange("p (k n) -> p k n", k=4))

        def front_ready(eng, f):
            eng.wait_ge(slot_ld[f % RING], 16 * (f // RING + 1))

        first_of = {}
        for f, (kind, a, b) in enumerate(FRONT):
            first_of.setdefault((kind, a), f)

        pool_stage = [biases[0:POOL_PAD, 0, 0:DC], biases[0:CONV_PAD, 0, DC:D]]
        dw_stage = biases[0:WIDTH, 1, 0:DC]
        out_stage = [biases[0:POOL_PAD, 1, DC:D], biases[0:POOL_PAD, 1, 0:DC],
                     biases[0:CONV_PAD, 0, DC:D], biases[0:CONV_PAD, 0, 0:DC]]

        block = ctx.enter_context(nc.Block())

        @block.sync
        def _(sp):
            sp.dma_start(x[:, 0:2, :], x_prompt[0].rearrange("(t p) d -> p t d", p=P)).then_inc(x_ld, 16)
            sp.dma_start(x[0:NS_TOK, 2, :], x_sample[0]).then_inc(x_ld, 16)
            for f in range(N_FRONT):
                if f >= RING:
                    sp.wait_ge(piece_used, f - RING + 1)
                src, dst = front_piece(f)
                sp.dma_start(dst, src).then_inc(slot_ld[f % RING], 16)

            def expert(e, n, par):
                for i in range(PIECES):
                    sp.wait_ge(piece_used, n * PIECES + (F_END - PIECES + i + 1))
                    w = (wg_v, wu_v, wd_v)[i // 4]
                    sp.dma_start(ring[:, i, :].rearrange("p (k n) -> p k n", k=2),
                                 w[e][:, 2 * (i % 4):2 * (i % 4) + 2, :]).then_inc(slot_ld[i], 16)
                    if i == 0:
                        sp.wait_ge(up_done, n - 1)
                        sp.dma_start(bias_row[par][:, 0, :], exp_b_gate[0:1, e, :]).then_inc(bias_ld[par], 16)
                        sp.dma_start(bias_row[par][:, 1, :], exp_b_up[0:1, e, :]).then_inc(bias_ld[par], 16)

            def pieces_first(e):
                for i in range(PIECES):
                    last = max(f for f in range(N_FRONT) if f % RING == i)
                    sp.wait_ge(piece_used, last + 1)
                    w = (wg_v, wu_v, wd_v)[i // 4]
                    sp.dma_start(ring[:, i, :].rearrange("p (k n) -> p k n", k=2),
                                 w[e][:, 2 * (i % 4):2 * (i % 4) + 2, :]).then_inc(slot_ld[i], 16)
                sp.wait_ge(stored, 64)
                sp.wait_ge(acc_init, 2 * TT)
                sp.dma_start(bias_row[0][:, 0, :], exp_b_gate[0:1, e, :]).then_inc(bias_ld[0], 16)
                sp.dma_start(bias_row[0][:, 1, :], exp_b_up[0:1, e, :]).then_inc(bias_ld[0], 16)

            pieces_first(0)
            expert(1, 1, 1)
            with sp.Fori(1, PAIRS) as i:
                expert(i * 2, i * 2, 0)
                expert(i * 2 + 1, i * 2 + 1, 1)
            sp.wait_ge(rounds_ready, 1)
            rounds = sp.value_load(nround[0:1, 0:1], min_val=1, max_val=MAX_ROUNDS)
            with sp.If(rounds > 1):
                with sp.Fori(1, rounds) as r:
                    with sp.Fori(0, PAIRS) as i:
                        expert(i * 2, r * E + i * 2, 0)
                        expert(i * 2 + 1, r * E + i * 2 + 1, 1)
            sp.dma_start(fgb, final_g.rearrange("(a d) -> a d", a=1).broadcast_to([P, D])).then_inc(fg_ld, 16)
            for t in range(TT):
                sp.wait_ge(y_ready, t + 1)
                dst = y_sample[0] if t == 2 else y_prompt[0, P * t:P * (t + 1), :]
                sp.dma_start(dst, ybuf[0:ROWS[t], t, :]).then_inc(stored, 16)
            sp.wait_ge(stored, 16 * (4 + TT))

        @block.gpsimd
        def _(pool):
            g = nc.gpsimd
            n = [0]

            def step(ins):
                n[0] += 1
                ins.then_inc(chain_p, 1)
                pool.wait_ge(chain_p, n[0])

            step(g.memset(ident[:, :], 0.0))
            g.affine_select(out=ident[:, :], in_=ident[:, :], compare_op=ALU.not_equal, fill=1.0, base=0,
                            pattern=[[-1, P]], channel_multiplier=1).then_inc(const, 1)
            g.memset(ones[:, :], 1.0).then_inc(const, 1)
            g.memset(cT[:, :, :], 0.0).then_inc(const, 1)
            step(g.memset(ada_sel[:, :, :], 0.0))
            g.affine_select(out=ada_sel[:, :, :], in_=ada_sel[:, :, :], compare_op=ALU.not_equal, fill=1.0,
                            base=0, pattern=[[-1, 12], [0, 32]], channel_multiplier=1).then_inc(const, 1)
            g.memset(up_ext[:, :, 0:POOL_PAD], 0.0).then_inc(const, 1)
            step(g.memset(before[:, :], 1.0))
            g.affine_select(out=before[:, :], in_=before[:, :], compare_op=ALU.is_gt, fill=0.0, base=0,
                            pattern=[[1, P]], channel_multiplier=-1).then_inc(const, 1)
            step(g.memset(pick[:, :, :], 0.0))
            g.affine_select(out=pick[:, :, :].rearrange("p (j g) n -> p j g n", g=2),
                            in_=pick[:, :, :].rearrange("p (j g) n -> p j g n", g=2),
                            compare_op=ALU.not_equal, fill=1.0, base=0,
                            pattern=[[-32, 4], [-1, 2], [0, P]], channel_multiplier=1).then_inc(const, 1)
            step(g.iota(slot_i[:, :, :], pattern=[[0, 2], [1, SLOTS]], base=0, channel_multiplier=0))
            step(g.tensor_copy(slot_no[:, :, :], slot_i[:, :, :]))
            for w in range(CT):
                step(g.tensor_scalar(invc[:, w, :], slot_no[:, 0, 0:16], 1.0, float(WINDOWS[w]), ALU.add, ALU.min))
            g.memset(dwc[:, :, :], 0.0).then_inc(const, 1)
            for w in range(CT):
                pool.wait_ge(pu_ready, w + 1)
                if w == 0:
                    pool.wait_ge(hist_ready, 1)
                    pool.wait_ge(mod_ready, 2)
                src = up_ext[:, w, :]
                for d in range(w + 1):
                    lo = (1 << (d + 1)) - 1
                    dst = wsum[:, d % 2, :]
                    step(g.tensor_tensor(dst[:, lo:], src[:, lo:], src[:, lo - (1 << d):PEXT - (1 << d)], ALU.add))
                    src = dst
                step(g.tensor_tensor(pooled[:, w, 0:16], src[:, POOL_PAD:POOL_PAD + 16], invc[:, w, :], ALU.mult))
                step(g.tensor_scalar(pooled[:, w, 16:NP_TOK], src[:, POOL_PAD + 16:POOL_PAD + NP_TOK],
                                     1.0 / WINDOWS[w], None, ALU.mult))
                c0, t0, m = PSEG[1]
                step(g.tensor_scalar(pooled[:, w, t0:t0 + m], src[:, c0:c0 + m], 1.0 / WINDOWS[w], None, ALU.mult))
                for c0, t0, m in PSEG:
                    ins = g.tensor_tensor(pooled[:, w, t0:t0 + m], pooled[:, w, t0:t0 + m], up_ext[:, w, c0:c0 + m],
                                          ALU.subtract)
                    if t0 == 0:
                        step(ins)
                ins.then_inc(pooled_ready, 1)

        @block.scalar
        def _(act):
            a = nc.scalar
            small = [(C_N1, norm1_g[0], 8), (C_GB, gate_b[0], 16), (C_PS, pool_scale[0], 8), (C_CB, conv_b[0], 4),
                     (C_LG, conv_ln_g[0], 4), (C_LB, conv_ln_b[0], 4), (C_CP, c_prompt[0], 8), (C_CS, c_sample[0], 8)]
            for at, src, k in small:
                act.dma_start(stage[at:at + k, :], src.rearrange("(k p) -> k p", p=P)).then_inc(c_ld, 16)
            act.dma_start(bada[:, :], b_ada[0].rearrange("(k n) -> k n", n=HALF)).then_inc(ada_ld, 16)
            act.dma_start(pool_stage[0], state_pool[0, 0]).then_inc(st_ld, 16)
            act.dma_start(pool_stage[1], state_conv[0, 0]).then_inc(st_ld, 16)
            act.dma_start(dw_stage, conv_dw[0]).then_inc(dw_ld, 16)
            n2 = norm2_g[0].rearrange("(a j n) -> a j n", a=1, n=HALF)
            act.wait_ge(zeroed, 1)
            for j in range(2):
                for gg in range(2):
                    act.dma_start(n2rows[32 * j + gg:32 * j + gg + 1, :], n2[:, j, :]).then_inc(n2_ld, 16)
            act.dma_start(rw[:, :, :], router_w[0].rearrange("(k p) e -> p k e", p=P)).then_inc(router_ld, 16)
            act.dma_start(rb[:, :], router_b[0:1, :]).then_inc(router_ld, 16)

            act.wait_ge(x_ld, 32)
            for t in range(TT):
                r = ROWS[t]
                a.activation(view(2304 + D * t, D)[0:r, :], x[0:r, t, :], ACT.Square,
                             accum_out=stat[0:r, t:t + 1]).then_inc(ssq, 1)
            act.wait_ge(mean2, 1)
            a.activation(stat[:, 4:7], stat[:, 8:11], ACT.Sqrt).then_inc(sqrt_ready, 1)
            act.wait_ge(cols_ready, 1)
            a.activation(csig[:, :], cols[:, C_CP:C_CP + 16], ACT.Sigmoid).then_inc(csig_ready, 1)
            act.wait_ge(stT, 1)
            act.wait_ge(xn_ready, 3)
            act.wait_ge(xT, KD)
            a.activation(up_ext[:, :, NP_TOK + POOL_PAD:NP_TOK + 2 * POOL_PAD],
                         bank[6][:, 0:CT * 32].rearrange("p (c n) -> p c n", n=32)[:, :, 0:POOL_PAD],
                         ACT.Copy).then_inc(hist_ready, 1)
            a.activation(uc_ext[:, :, NP_TOK + CONV_PAD:NP_TOK + 2 * CONV_PAD],
                         bank[6][:, 128:128 + CT * 32].rearrange("p (c n) -> p c n", n=32)[:, :, 0:CONV_PAD],
                         ACT.Copy).then_inc(hist_ready, 1)
            act.wait_ge(ada_mm, 1)
            a.activation(rows[:, 0, :], bank[4][:, :], ACT.Copy).then_inc(rows_ready, 1)
            for n in range(12):
                if n in (0, 1, 4, 5):
                    c = n if n < 2 else n - 2
                    act.wait_ge(in_mm, n + 1)
                    ins = a.activation(sig_g[:, c, :], bank[n % 4][:, 0:TOK], ACT.Sigmoid)
                    ins.then_inc(sig_ready, 1)
                    act.wait_ge(sig_ready, c + 1)
                elif n >= 8:
                    act.wait_ge(in_mm, n + 1)
                    for c0, t0, m in PSEG:
                        ins = a.activation(up_ext[:, n - 8, c0:c0 + m], bank[n % 4][:, t0:t0 + m], ACT.Copy)
                    ins.then_inc(pu_ready, 1)
            for n in range(2 * KD):
                act.wait_ge(gate_mm, n + 1)
                a.activation(gates[:, n, :], bank[n % 4][:, 0:TOK], ACT.Sigmoid,
                             bias=cols[:, C_GB + n:C_GB + n + 1]).then_inc(gate_ev, 1)
            for b in (1, 2):
                act.wait_ge(ada_mm, b + 1)
                a.activation(rows[:, b, :], bank[4 + b - 1][:, :], ACT.Copy).then_inc(rows_ready, 1)
            for i in range(4):
                r = POOL_PAD if i < 2 else CONV_PAD
                act.wait_ge(outT, i + 1)
                a.activation(out_stage[i], bank[6 + i % 2][0:r, :], ACT.Copy).then_inc(out_ev, 1)
            for i, dst in enumerate((new_pool_p, new_pool_s, new_conv_p, new_conv_s)):
                act.wait_ge(out_ev, i + 1)
                act.dma_start(dst[0, 0], out_stage[i]).then_inc(stored, 16)
            act.wait_ge(mean_mm, 1)
            a.activation(view(11640, CW), bank[6][:, 0:CW], ACT.Copy, scale=1.0 / DC).then_inc(mean_ready, 1)
            act.wait_ge(cen_ready, 1)
            a.activation(tmp[:, :, :], yc[:, :, :], ACT.Square).then_inc(sq_ready, 1)
            act.wait_ge(var_mm, 1)
            act.wait_ge(chain_a, 1)
            a.activation(view(11640, CW), view(11640 + CW, CW), ACT.Sqrt).then_inc(std_ready, 1)
            act.wait_ge(yn_ready, 1)
            for c in range(CT):
                a.activation(tmp[:, c, :], yc[:, c, :], ACT.Sigmoid, scale=cols[:, C_LG + c:C_LG + c + 1],
                             bias=cols[:, C_LB + c:C_LB + c + 1]).then_inc(zsig_ready, 1)
            for i in range(16):
                which, gg, hh = i // 4, (i // 2) % 2, i % 2
                act.wait_ge(bc_mm, i + 1)
                if i == 0:
                    act.wait_ge(pm_ev, KD)
                    act.wait_ge(out_ev, 2)
                if which == 2:
                    act.wait_ge(merged_ready, KD)
                dst = (g2b, g1b, sh2b, a2b)[which]
                r = P if gg == 0 else NS_TOK
                a.activation(dst[0:r, gg, HALF * hh:HALF * (hh + 1)], bank[i % 4][0:r, :], ACT.Copy).then_inc(bc_ev, 1)
            for i in range(2 * TT):
                hh, t = i // TT, i % TT
                r = ROWS[t]
                act.wait_ge(x2_ready, i + 1)
                a.activation(h2[0:r, t, HALF * hh:HALF * (hh + 1)], x[0:r, t, HALF * hh:HALF * (hh + 1)], ACT.Square,
                             accum_out=stat[0:r, 12 + 3 * hh + t:13 + 3 * hh + t]).then_inc(ssq2, 1)
            act.dma_start(bd_rows, exp_b_down[0]).then_inc(bd_ld, 16)
            act.wait_ge(mean2, 2)
            a.activation(stat[:, 4:7], stat[:, 8:11], ACT.Sqrt).then_inc(sqrt_ready, 1)
            for k in range(1, KD, 2):
                act.wait_ge(h2T_mm, k + 1)
                a.activation(h2T[:, k, :], bank[k % 4][:, 0:TOK], ACT.Copy).then_inc(h2T_odd, 1)
            act.wait_ge(shifted, 1)
            a.activation(rt[:, 5, :, :], rt[:, 4, :, :], ACT.Exp).then_inc(exp_ready, 1)
            act.wait_ge(wT_mm, 1)
            a.activation(wT[0:E, :], bank[6][0:E, 0:TOK], ACT.Copy).then_inc(wT_ev, 1)
            for i in range(2 * TT):
                r = ROWS[i // 2]
                act.wait_ge(accb_mm, i + 1)
                a.activation(acc[0:r, i // 2, HALF * (i % 2):HALF * (i % 2 + 1)], bank[i % 4][0:r, :],
                             ACT.Copy).then_inc(acc_init, 1)

            act.wait_ge(xg_mm, 1)
            a.activation(xg, bank[0][:, :], ACT.Copy).then_inc(xg_ev, 1)
            act.wait_ge(tpa_mm, 1)
            a.activation(xgT, bank[1][:, :], ACT.Copy).then_inc(tpa_ev, 1)
            for free in (actT_ev, y_ev):
                act.sem_inc(free, 1)
            act.wait_ge(rounds_ready, 1)
            pairs = act.value_load(npair[0:1, 0:1], min_val=PAIRS, max_val=PAIRS * MAX_ROUNDS)
            with act.Fori(0, pairs) as i:
                for par in range(2):
                    n = i * 2 + par
                    act.wait_ge(gate_read, n + 2)
                    a.activation(gsig, gmin, ACT.Sigmoid, scale=ALPHA).then_inc(gsig_ready, 1)
                    act.wait_ge(xg_mm, n + 2)
                    a.activation(xg, bank[0][:, :], ACT.Copy).then_inc(xg_ev, 1)
                    act.wait_ge(tpa_mm, n * 2 + 2)
                    a.activation(ohwT, bank[1][:, 0:TT * P], ACT.Copy).then_inc(tpa_ev, 1)
                    act.wait_ge(actT_mm, n + 1)
                    a.activation(actT, bank[2][:, :], ACT.Copy).then_inc(actT_ev, 1)
                    act.wait_ge(tpa_mm, n * 2 + 3)
                    a.activation(xgT, bank[1][:, :], ACT.Copy).then_inc(tpa_ev, 1)
                    act.wait_ge(y_mm, n + 1)
                    a.activation(ysb, bank[5][:, :], ACT.Copy).then_inc(y_ev, 1)
            for t in range(TT):
                r = ROWS[t]
                act.wait_ge(ssq3, t + 1)
                a.activation(ring[0:r, t, 0:D], acc[0:r, t, :], ACT.Square,
                             accum_out=stat[0:r, 20 + t:21 + t]).then_inc(sqrt3, 1)
            act.wait_ge(mean2, 3)
            a.activation(stat[:, 4:7], stat[:, 8:11], ACT.Sqrt).then_inc(sqrt_ready, 1)

        @block.vector
        def _(dve):
            v = nc.vector
            n = [0]

            def step(ins):
                n[0] += 1
                ins.then_inc(chain_v, 1)
                dve.wait_ge(chain_v, n[0])

            def rstd(sums, count):
                ins = v.tensor_scalar(stat[:, 8:11], sums, 1.0 / D, EPS, ALU.mult, ALU.add)
                ins.then_inc(mean2, 1)
                dve.wait_ge(sqrt_ready, count)
                step(v.reciprocal(stat[:, 4:7], stat[:, 4:7]))

            step(v.memset(stat[:, :], 0.0))
            v.memset(n2rows[:, :], 0.0).then_inc(zeroed, 1)
            dve.wait_ge(ssq, TT)
            rstd(stat[:, 0:3], 1)
            for t in range(TT):
                r = ROWS[t]
                v.tensor_scalar(h2[0:r, t, :], x[0:r, t, :], stat[0:r, 4 + t:5 + t], None, ALU.mult).then_inc(xn_ready, 1)
            dve.wait_ge(colT, 1)
            v.tensor_copy(cols[:, :], bank[5][:, 0:N_COLS]).then_inc(cols_ready, 1)
            dve.wait_ge(csig_ready, 1)
            dve.wait_ge(cols_ready, 1)
            dve.wait_ge(const, 3)
            v.tensor_tensor(cT[:, :, 0:2], cols[:, C_CP:C_CP + 16].rearrange("p (g k) -> p k g", g=2),
                            csig[:, :].rearrange("p (g k) -> p k g", g=2), ALU.mult).then_inc(cT_ready, 1)
            dve.wait_ge(dwT, 1)
            dve.wait_ge(const, 8)
            v.tensor_copy(dwc[:, :, 0:WIDTH], bank[7][:, 0:CT * 32].rearrange("p (c n) -> p c n", n=32)[:, :, 0:WIDTH]) \
                .then_inc(dw_ready, 1)
            for k in range(KD):
                dve.wait_ge(xT, k + 1)
                v.tensor_copy(hT[:, k, :], bank[k % 4][:, 0:TOK]).then_inc(xT_ev, 1)
            v.memset(uc_ext[:, :, 0:CONV_PAD], 0.0).then_inc(hist0_ready, 1)
            v.reciprocal(invc[:, :, :], invc[:, :, :]).then_inc(mod_ready, 1)
            dve.wait_ge(modT, 1)
            modv = bank[7][:, :].rearrange("p (r j m) -> p j r m", r=4, m=32)
            four = "p (j r g) -> p j r g"
            step(v.tensor_copy(shc[:, :].rearrange(four, j=2, g=2), modv[:, 0:2, :, 0:2]))
            step(v.tensor_copy(scc[:, :].rearrange(four, j=2, g=2), modv[:, 2:4, :, 0:2]))
            for gg in range(2):
                s = scc[:, :].rearrange("p (k g) -> p g k", g=2)[:, gg, :]
                ins = v.scalar_tensor_tensor(out=s, in0=s, scalar=1.0, in1=cols[:, C_N1:C_N1 + KD],
                                             op0=ALU.add, op1=ALU.mult)
                step(ins) if gg == 0 else ins.then_inc(mod_ready, 1)
            dve.wait_ge(mod_ready, 2)
            dve.wait_ge(xT_ev, KD)
            for k in range(KD):
                for gg, (t0, m) in enumerate(((0, NP_TOK), (NP_TOK, NS_TOK))):
                    ins = v.tensor_scalar(hT[:, k, t0:t0 + m], hT[:, k, t0:t0 + m], scc[:, 2 * k + gg:2 * k + gg + 1],
                                          shc[:, 2 * k + gg:2 * k + gg + 1], ALU.mult, ALU.add)
                ins.then_inc(hT_ready, 1)
            dve.wait_ge(hist_ready, 2)
            dve.wait_ge(hist0_ready, 1)
            steps = [0]

            def glu(tiles):
                for c in tiles:
                    m_in = c + 2 if c < 2 else c + 4
                    dve.wait_ge(in_mm, m_in + 1)
                    dve.wait_ge(sig_ready, c + 1)
                    for c0, t0, m in CSEG:
                        ins = v.tensor_tensor(uc_ext[:, c, c0:c0 + m], bank[m_in % 4][:, t0:t0 + m],
                                              sig_g[:, c, t0:t0 + m], ALU.mult)
                    ins.then_inc(u_ready, 1)

            def conv(tiles):
                for k in range(WIDTH):
                    for c in tiles:
                        if k:
                            dve.wait_ge(conv_step, steps[0] - 1)
                        tap = dwc[:, c, k:k + 1]
                        if k == 0:
                            ins = v.tensor_scalar(yc[:, c, :], uc_ext[:, c, 0:CW], tap, cols[:, C_CB + c:C_CB + c + 1],
                                                  ALU.mult, ALU.add)
                        else:
                            ins = v.scalar_tensor_tensor(out=yc[:, c, :], in0=uc_ext[:, c, k:k + CW], scalar=tap,
                                                         in1=yc[:, c, :], op0=ALU.mult, op1=ALU.add)
                        ins.then_inc(conv_step, 1)
                        steps[0] += 1

            glu((0, 1))
            glu((2, 3))
            dve.wait_ge(u_ready, 4)
            dve.wait_ge(dw_ready, 1)
            conv((0, 1))
            conv((2, 3))
            dve.wait_ge(rows_ready, 3)
            dve.wait_ge(n2_ld, 64)
            v.scalar_tensor_tensor(out=rows[0:64, 2, :], in0=rows[0:64, 2, :], scalar=1.0, in1=n2rows[:, :],
                                   op0=ALU.add, op1=ALU.mult).then_inc(a2rows, 1)
            dve.wait_ge(gate_ev, 2 * KD)
            for m in range(KD):
                dve.wait_ge(pm_mm, m + 1)
                v.scalar_tensor_tensor(out=merged[:, m, :], in0=bank[m % 4][:, 0:TOK],
                                       scalar=cols[:, C_PS + m:C_PS + m + 1], in1=gates[:, m, :],
                                       op0=ALU.mult, op1=ALU.mult).then_inc(pm_ev, 1)
            dve.wait_ge(mean_ready, 1)
            for c in range(CT):
                ins = v.tensor_tensor(yc[:, c, :], yc[:, c, :], view(11640, CW), ALU.subtract)
            ins.then_inc(cen_ready, 1)
            dve.wait_ge(var_mm, 1)
            v.tensor_scalar(view(11640 + CW, CW), bank[7][:, 0:CW], 1.0 / DC, EPS, ALU.mult, ALU.add).then_inc(chain_a, 1)
            dve.wait_ge(std_ready, 1)
            step(v.reciprocal(view(11640, CW), view(11640, CW)))
            for c in range(CT):
                ins = v.tensor_tensor(yc[:, c, :], yc[:, c, :], view(11640, CW), ALU.mult)
            ins.then_inc(yn_ready, 1)
            dve.wait_ge(yn_ready, 1)
            dve.wait_ge(zsig_ready, CT)
            for c in range(CT):
                ins = v.tensor_scalar(yc[:, c, :], yc[:, c, :], cols[:, C_LG + c:C_LG + c + 1],
                                      cols[:, C_LB + c:C_LB + c + 1], ALU.mult, ALU.add)
                step(ins)
            for c in range(CT):
                for (c0, t0, m) in ((0, 0, NP_TOK), (NP_TOK + CONV_PAD, NP_TOK, NS_TOK)):
                    step(v.tensor_tensor(act_c[:, c, t0:t0 + m], yc[:, c, c0:c0 + m], tmp[:, c, c0:c0 + m], ALU.mult))
            v.memset(h2[:, 2, :], 0.0).then_inc(act_c_ready, 1)
            dve.wait_ge(pm_ev, KD)
            for m in range(KD):
                dve.wait_ge(cm_mm, m + 1)
                v.tensor_tensor(gates[:, KD + m, :], bank[m % 4][:, 0:TOK], gates[:, KD + m, :], ALU.mult).then_inc(cm_ev, 1)
                dve.wait_ge(cm_ev, m + 1)
                v.tensor_tensor(merged[:, m, :], merged[:, m, :], gates[:, KD + m, :], ALU.add).then_inc(merged_ready, 1)
            dve.wait_ge(bc_ev, 8)
            for i in range(2 * TT):
                hh, t = i // TT, i % TT
                r, gg = ROWS[t], t // 2
                cs = slice(HALF * hh, HALF * (hh + 1))
                dve.wait_ge(wo_mm, i + 1)
                v.tensor_tensor(view(13812 + HALF * (i % 2), HALF)[0:r, :], bank[4 + i % 4][0:r, :], g1b[0:r, gg, cs], ALU.mult).then_inc(wo_ev, 1)
                dve.wait_ge(wo_ev, i + 1)
                v.tensor_tensor(x[0:r, t, cs], x[0:r, t, cs], view(13812 + HALF * (i % 2), HALF)[0:r, :], ALU.add).then_inc(x2_ready, 1)
            dve.wait_ge(ssq2, 2 * TT)
            step(v.tensor_tensor(stat[:, 0:3], stat[:, 12:15], stat[:, 15:18], ALU.add))
            rstd(stat[:, 0:3], 2)
            dve.wait_ge(bc_ev, 16)
            for t in range(TT):
                r, gg = ROWS[t], t // 2
                step(v.scalar_tensor_tensor(out=h2[0:r, t, :], in0=x[0:r, t, :], scalar=stat[0:r, 4 + t:5 + t],
                                            in1=a2b[0:r, gg, :], op0=ALU.mult, op1=ALU.mult))
                v.tensor_tensor(h2[0:r, t, :], h2[0:r, t, :], sh2b[0:r, gg, :], ALU.add).then_inc(h2_ready, 1)
            for k in range(0, KD, 2):
                dve.wait_ge(h2T_mm, k + 1)
                v.tensor_copy(h2T[:, k, :], bank[k % 4][:, 0:TOK]).then_inc(h2T_even, 1)

            def wide(ap):
                return ap.broadcast_to([P, TT, E])

            step(v.memset(logit[:, :, :], 0.0))
            dve.wait_ge(logit_mm, 1)
            v.tensor_copy(logit[:, 0:2, :], bank[4][:, 0:2 * E].rearrange("p (t e) -> p t e", e=E))
            step(v.tensor_copy(logit[0:NS_TOK, 2, :], bank[4][0:NS_TOK, 2 * E:3 * E]))
            for t in range(TT):
                ins = v.max(top[:, t, :], logit[:, t, :])
            step(ins)
            v.tensor_tensor(rt[:, 4, :, :], logit[:, :, :], wide(top[:, :, 0:1]), ALU.subtract).then_inc(shifted, 1)
            v.tensor_tensor(rt[:, 0, :, :], logit[:, :, :], wide(top[:, :, 3:4]), ALU.is_gt)
            step(v.tensor_tensor(rt[:, 1, :, :], logit[:, :, :], wide(top[:, :, 3:4]), ALU.is_equal))
            v.tensor_copy(rt[:, 2, :, :], rt[:, 1, :, :])
            step(v.tensor_reduce(stat[:, 24:27], rt[:, 0, :, :], AX, ALU.add))
            src = 2
            for d in (1, 2, 4, 8, 16):
                dst = 3 if src == 2 else 2
                v.tensor_copy(rt[:, dst, :, 0:d], rt[:, src, :, 0:d])
                step(v.tensor_tensor(rt[:, dst, :, d:E], rt[:, src, :, d:E], rt[:, src, :, 0:E - d], ALU.add))
                src = dst
            for t in range(TT):
                ins = v.tensor_scalar(rt[:, 6, t, :], rt[:, src, t, :], stat[:, 24 + t:25 + t], float(TOPK), ALU.add, ALU.is_le)
            step(ins)
            step(v.tensor_tensor(rt[:, 6, :, :], rt[:, 6, :, :], rt[:, 1, :, :], ALU.mult))
            v.tensor_tensor(rt[:, 7, :, :], rt[:, 6, :, :], rt[:, 0, :, :], ALU.add).then_inc(sel_ready, 1)
            dve.wait_ge(sel_ready, 1)
            dve.wait_ge(exp_ready, 1)
            step(v.tensor_tensor(rt[:, 5, :, :], rt[:, 5, :, :], rt[:, 7, :, :], ALU.mult))
            step(v.tensor_reduce(stat[:, 24:27], rt[:, 5, :, :], AX, ALU.add))
            step(v.reciprocal(stat[:, 27:30], stat[:, 24:27]))
            for t in range(TT):
                ins = v.tensor_scalar(routed[:, 1, t, 0:E], rt[:, 5, t, :], stat[:, 27 + t:28 + t], None, ALU.mult)
            ins.then_inc(w_ready, 1)
            dve.wait_ge(w_ready, 1)
            v.tensor_copy(routed[:, 1, :, E:E + 1], routed[:, 1, :, 0:1])
            dve.wait_ge(rank_mm, 1)
            step(v.memset(rt[:, 0, :, :], 0.0))
            step(v.tensor_copy(rt[:, 0, 0:2, :], bank[5][:, 0:2 * E].rearrange("p (t e) -> p t e", e=E)))
            step(v.tensor_copy(rt[0:NS_TOK, 0, 2, :], bank[5][0:NS_TOK, 2 * E:3 * E]))
            step(v.scalar_tensor_tensor(out=rt[:, 0, :, :], in0=rt[:, 0, :, :], scalar=1.0, in1=rt[:, 7, :, :],
                                        op0=ALU.add, op1=ALU.mult))
            step(v.tensor_scalar(routed[:, 0, :, 0:E], rt[:, 0, :, :], -1.0, None, ALU.add))
            step(v.tensor_reduce(stat[:, 30:31], bank[5][:, 3 * E:4 * E], AX, ALU.max))
            step(v.tensor_scalar(stat[:, 31:32], stat[:, 30:31], float(SLOTS), 1.0, ALU.is_gt, ALU.add))
            for m in range(2, MAX_ROUNDS):
                step(v.tensor_scalar(stat[:, 29:30], stat[:, 30:31], float(m * SLOTS), None, ALU.is_gt))
                step(v.tensor_tensor(stat[:, 31:32], stat[:, 31:32], stat[:, 29:30], ALU.add))
            step(v.tensor_copy(nround[:, :], stat[:, 31:32]))
            v.tensor_scalar(npair[:, :], stat[:, 31:32], float(PAIRS), None, ALU.mult).then_inc(rounds_ready, 1)
            dve.wait_ge(rounds_ready, 1)

            def one_hots(par, cs):
                for t in range(TT):
                    rank = pairc[:, cs, t, par:par + 1]
                    v.tensor_scalar(oh[:, TT * par + t, :], slot_no[:, 0, :], rank, None, ALU.is_equal)
                    ins = v.tensor_scalar(ohw[:, TT * par + t, :], slot_no[:, :, :].rearrange("p a b -> p (a b)"), rank,
                                          pairc[:, cs, TT + t, par:par + 1], ALU.is_equal, ALU.mult)
                ins.then_inc(oh_ready, 1)

            for free in (gate_read, up_read, scat_add):
                dve.sem_inc(free, 1)
            dve.wait_ge(wT_mm, 1)
            dve.wait_ge(acc_init, 2 * TT)
            v.memset(ohwT, 0.0).then_inc(work_zero, 1)
            v.memset(ysb, 0.0).then_inc(work_zero, 1)
            step(v.tensor_copy(pairc[:, 1, :, :], routed[:, :, :, :].rearrange("p a t e -> p (a t) e")[:, :, 0:2]))
            one_hots(0, 1)
            rounds = dve.value_load(nround[0:1, 0:1], min_val=1, max_val=MAX_ROUNDS)

            def add_back(t, count):
                r = ROWS[t]
                dve.wait_ge(scat_mm, count)
                for hh in range(2):
                    cs = slice(HALF * hh, HALF * (hh + 1))
                    ins = v.tensor_tensor(acc[0:r, t, cs], acc[0:r, t, cs], bank[6 + hh][0:r, :], ALU.add)
                ins.then_inc(scat_add, 1)

            with dve.Fori(0, rounds) as r:
                dve.wait_ge(shifted, r * 2 + 1)
                v.tensor_scalar(routed[:, 0, :, E:E + 1], routed[:, 0, :, 0:1], float(SLOTS), None, ALU.subtract) \
                    .then_inc(shifted, 1)
                with dve.Fori(0, PAIRS) as i:
                    dve.wait_ge(shifted, r * 2 + 2)
                    v.tensor_copy(pairc[:, 0, :, :], routed[:, :, :, :].rearrange("p a t e -> p (a t) e")
                                  [:, :, bass.ds(i * 2 + 1, 2)]).then_inc(cols_copied, 1)
                    for par in range(2):
                        n_e = r * E + i * 2 + par
                        if par == 0:
                            dve.wait_ge(cols_copied, r * PAIRS + i + 1)
                        dve.wait_ge(xg_mm, n_e + 1)
                        dve.wait_ge(tpa_mm, n_e * 2 + 1)
                        one_hots_next = 1 - par
                        for t in range(TT):
                            rank = pairc[:, 0, t, par:par + 1]
                            v.tensor_scalar(oh[:, TT * one_hots_next + t, :], slot_no[:, 0, :], rank, None, ALU.is_equal)
                            ins = v.tensor_scalar(ohw[:, TT * one_hots_next + t, :],
                                                  slot_no[:, :, :].rearrange("p a b -> p (a b)"), rank,
                                                  pairc[:, 0, TT + t, par:par + 1], ALU.is_equal, ALU.mult)
                        ins.then_inc(oh_ready, 1)
                        dve.wait_ge(gate_done, n_e + 1)
                        v.tensor_scalar(gmin, bank[3][:, :], LIMIT, None, ALU.min).then_inc(gate_read, 1)
                        add_back(0, n_e * 3 + 1)
                        dve.wait_ge(gsig_ready, n_e + 1)
                        dve.wait_ge(gate_read, n_e + 2)
                        v.tensor_tensor(gsig, gmin, gsig, ALU.mult).then_inc(gs_ready, 1)
                        add_back(1, n_e * 3 + 2)
                        dve.wait_ge(up_done, n_e + 1)
                        v.tensor_scalar(ucl, bank[4][:, :], LIMIT, -LIMIT, ALU.min, ALU.max).then_inc(up_read, 1)
                        dve.wait_ge(up_read, n_e + 2)
                        dve.wait_ge(gs_ready, n_e + 1)
                        v.scalar_tensor_tensor(out=acts, in0=ucl, scalar=1.0, in1=gsig,
                                               op0=ALU.add, op1=ALU.mult).then_inc(act_ready, 1)
                        add_back(2, n_e * 3 + 3)
                v.tensor_scalar(routed[:, 0, :, 0:E], routed[:, 0, :, 0:E], float(SLOTS), None, ALU.subtract) \
                    .then_inc(shifted, 1)

            for t in range(TT):
                add_back(t, rounds * (3 * E) + (t + 1))
            dve.wait_ge(scat_add, rounds * (3 * E) + 4)
            for t in range(TT):
                r = ROWS[t]
                step(v.tensor_tensor(acc[0:r, t, :], acc[0:r, t, :], g2b[0:r, t // 2, :], ALU.mult))
                v.tensor_tensor(acc[0:r, t, :], acc[0:r, t, :], x[0:r, t, :], ALU.add).then_inc(ssq3, 1)
            dve.wait_ge(ssq3, TT)
            dve.wait_ge(sqrt3, TT)
            rstd(stat[:, 20:23], 3)
            dve.wait_ge(fg_ld, 16)
            for t in range(TT):
                r = ROWS[t]
                v.scalar_tensor_tensor(out=ybuf[0:r, t, :], in0=acc[0:r, t, :], scalar=stat[0:r, 4 + t:5 + t],
                                       in1=fgb[0:r, :], op0=ALU.mult, op1=ALU.mult).then_inc(y_ready, 1)

        @block.tensor
        def _(pe):
            mm, tr = nc.tensor.matmul, nc.tensor.transpose

            pe.wait_ge(const, 4)
            pe.wait_ge(c_ld, 16 * 8)
            tr(bank[5][:, 0:N_COLS], stage[:, :], ident[0:N_COLS, 0:N_COLS]).then_inc(colT, 1)
            pe.wait_ge(dw_ld, 16)
            for c in range(CT):
                ins = tr(bank[7][:, 32 * c:32 * c + WIDTH], dw_stage[:, P * c:P * (c + 1)], ident[0:WIDTH, 0:WIDTH])
            ins.then_inc(dwT, 1)
            pe.wait_ge(st_ld, 32)
            for c in range(CT):
                tr(bank[6][:, 32 * c:32 * c + POOL_PAD], pool_stage[0][:, P * c:P * (c + 1)], ident[0:POOL_PAD, 0:POOL_PAD])
            for c in range(CT):
                ins = tr(bank[6][:, 128 + 32 * c:128 + 32 * c + CONV_PAD], pool_stage[1][:, P * c:P * (c + 1)],
                         ident[0:CONV_PAD, 0:CONV_PAD])
            ins.then_inc(stT, 1)

            def transposes(src, k, done):
                for t in range(TT):
                    r = ROWS[t]
                    ins = tr(bank[k % 4][:, P * t:P * t + r], src[0:r, t, P * k:P * (k + 1)], ident[0:r, 0:r])
                ins.then_inc(done, 1)

            pe.wait_ge(xn_ready, TT)
            for k in range(KD):
                if k >= 4:
                    pe.wait_ge(xT_ev, k - 3)
                transposes(h2, k, xT)

            def modulation(b, out):
                f0 = first_of[("ada", b)]
                for k in range(KD):
                    front_ready(pe, f0 + k)
                    for j in range(4):
                        ins = mm(out[32 * j:32 * j + 32, :], cT[:, k, :], ring[:, (f0 + k) % RING, HALF * j:HALF * (j + 1)],
                                 start=(k == 0), stop=False, skip_group_check=True)
                    ins.then_inc(piece_used, 1)
                for j in range(4):
                    ins = mm(out[32 * j:32 * j + 32, :], ada_sel[:, 4 * b + j, :], bada[:, :], start=False, stop=True,
                             skip_group_check=True)
                ins.then_inc(ada_mm, 1)

            pe.wait_ge(cT_ready, 1)
            pe.wait_ge(ada_ld, 16)
            modulation(0, bank[4])
            pe.wait_ge(rows_ready, 1)
            pe.wait_ge(dw_ready, 1)
            for r in range(4):
                ins = tr(bank[7][:, P * r:P * (r + 1)], rows[:, 0, P * r:P * (r + 1)], ident[:, :])
            ins.then_inc(modT, 1)

            pe.wait_ge(xT_ev, KD)
            for n in range(12):
                f = first_of[("in", (4, 2, 5, 3, 0, 1)[n // 2])]
                w = front_piece(f)[1]
                front_ready(pe, f)
                if n >= 4:
                    m = n - 4
                    if m in (0, 1, 4, 5):
                        pe.wait_ge(sig_ready, (m if m < 2 else m - 2) + 1)
                    elif m < 8:
                        pe.wait_ge(u_ready, (m - 2 if m < 4 else m - 4) + 1)
                for k in range(KD):
                    if n == 0:
                        pe.wait_ge(hT_ready, k + 1)
                    ins = mm(bank[n % 4][:, 0:TOK], w[:, k, P * (n % 2):P * (n % 2 + 1)], hT[:, k, :],
                             start=(k == 0), stop=(k == KD - 1))
                ins.then_inc(in_mm, 1)
                if n % 2:
                    pe.wait_ge(in_mm, n + 1)
                    pe.sem_inc(piece_used, 1)
            for n in range(2 * KD):
                f = first_of[("gate", n // 2)]
                w = front_piece(f)[1]
                front_ready(pe, f)
                if n < 4:
                    pe.wait_ge(pu_ready, n + 1)
                else:
                    pe.wait_ge(gate_ev, n - 3)
                for k in range(KD):
                    ins = mm(bank[n % 4][:, 0:TOK], w[:, k, P * (n % 2):P * (n % 2 + 1)], hT[:, k, :],
                             start=(k == 0), stop=(k == KD - 1))
                ins.then_inc(gate_mm, 1)
                if n % 2:
                    pe.wait_ge(gate_mm, n + 1)
                    pe.sem_inc(piece_used, 1)
            modulation(1, bank[4])
            modulation(2, bank[5])
            pe.wait_ge(hist_ready, 2)
            pe.wait_ge(mod_ready, 2)
            pe.wait_ge(u_ready, 4)
            for i, (src, c0, r) in enumerate(((up_ext, POOL_PAD + NP_TOK - POOL_PAD, POOL_PAD),
                                              (up_ext, PEXT - POOL_PAD, POOL_PAD),
                                              (uc_ext, CONV_PAD + NP_TOK - CONV_PAD, CONV_PAD),
                                              (uc_ext, CEXT - CONV_PAD, CONV_PAD))):
                if i >= 2:
                    pe.wait_ge(out_ev, i - 1)
                for c in range(CT):
                    ins = tr(bank[6 + i % 2][0:r, P * c:P * (c + 1)], src[:, c, c0:c0 + r], ident[:, :])
                ins.then_inc(outT, 1)
            f = first_of[("pool", 0)]
            w = front_piece(f)[1]
            front_ready(pe, f)
            for m in range(KD):
                pe.wait_ge(pooled_ready, m // 2 + 1)
                if m >= 4:
                    pe.wait_ge(pm_ev, m - 3)
                else:
                    pe.wait_ge(gate_ev, 2 * KD - 3 + m)
                ins = mm(bank[m % 4][:, 0:TOK], w[:, m // 2, P * (m % 2):P * (m % 2 + 1)], pooled[:, m // 2, :],
                         start=True, stop=True)
                ins.then_inc(pm_mm, 1)
            pe.wait_ge(pm_mm, KD)
            pe.sem_inc(piece_used, 1)

            pe.wait_ge(conv_step, CT * WIDTH)
            pe.wait_ge(out_ev, 4)
            for c in range(CT):
                ins = mm(bank[6][:, 0:CW], ones[:, :], yc[:, c, :], start=(c == 0), stop=(c == CT - 1))
            ins.then_inc(mean_mm, 1)
            pe.wait_ge(sq_ready, 1)
            for c in range(CT):
                ins = mm(bank[7][:, 0:CW], ones[:, :], tmp[:, c, :], start=(c == 0), stop=(c == CT - 1))
            ins.then_inc(var_mm, 1)
            pe.wait_ge(act_c_ready, 1)
            pe.wait_ge(pm_ev, KD)
            for m in range(KD):
                f = first_of[("conv", m // 4)]
                w = front_piece(f)[1]
                front_ready(pe, f)
                if m >= 4:
                    pe.wait_ge(cm_ev, m - 3)
                for c in range(CT):
                    ins = mm(bank[m % 4][:, 0:TOK], w[:, c, P * (m % 4):P * (m % 4 + 1)], act_c[:, c, :],
                             start=(c == 0), stop=(c == CT - 1))
                ins.then_inc(cm_mm, 1)
                if m % 4 == 3:
                    pe.wait_ge(cm_mm, m + 1)
                    pe.sem_inc(piece_used, 1)
            pe.wait_ge(const, 8)
            pe.wait_ge(rows_ready, 3)
            pe.wait_ge(a2rows, 1)
            for i in range(16):
                which, gg, hh = i // 4, (i // 2) % 2, i % 2
                b, j = ((2, 2), (1, 0), (1, 2), (2, 0))[which]
                if i >= 4:
                    pe.wait_ge(bc_ev, i - 3)
                else:
                    pe.wait_ge(cm_ev, 5 + i)
                mm(bank[i % 4][:, :], pick[:, 2 * (j + hh) + gg, :], rows[:, b, :], start=True, stop=True) \
                    .then_inc(bc_mm, 1)
            pe.wait_ge(merged_ready, KD)
            for hh in range(2):
                for q in range(2):
                    f = first_of[("out", hh)] + q
                    w = front_piece(f)[1]
                    front_ready(pe, f)
                    for t in range(TT):
                        i = hh * TT + t
                        r = ROWS[t]
                        if i >= 4 and q == 0:
                            pe.wait_ge(wo_ev, i - 3)
                        for k in range(4):
                            ins = mm(bank[4 + i % 4][0:r, :], merged[:, 4 * q + k, P * t:P * t + r], w[:, k, :],
                                     start=(q == 0 and k == 0), stop=(q == 1 and k == 3), skip_group_check=True)
                        if q == 1:
                            ins.then_inc(wo_mm, 1)
                    if q == 0:
                        ins.then_inc(piece_used, 1)
                    else:
                        pe.wait_ge(wo_mm, i + 1)
                        pe.sem_inc(piece_used, 1 if hh == 0 else 1 + F_END - N_FRONT)
            pe.wait_ge(h2_ready, TT)
            for k in range(KD):
                if k >= 4:
                    pe.wait_ge((h2T_even, h2T_odd)[k % 2], k // 2 - 1)
                else:
                    pe.wait_ge(bc_ev, 13 + k)
                transposes(h2, k, h2T_mm)
            pe.wait_ge(h2T_even, KD // 2)
            pe.wait_ge(h2T_odd, KD // 2)
            pe.wait_ge(router_ld, 32)
            for t in range(TT):
                r = ROWS[t]
                out = bank[4][0:r, E * t:E * (t + 1)]
                for k in range(KD):
                    mm(out, h2T[:, k, P * t:P * t + r], rw[:, k, :], start=(k == 0), stop=False)
                ins = mm(out, ones[0:1, 0:r], rb[:, :], start=False, stop=True)
            ins.then_inc(logit_mm, 1)
            pe.wait_ge(sel_ready, 1)
            for t in range(TT):
                r = ROWS[t]
                out = bank[5][0:r, E * t:E * (t + 1)]
                for s in range(t):
                    mm(out, ones[:, 0:r], rt[:, 7, s, :], start=(s == 0), stop=False)
                mm(out, before[0:r, 0:r], rt[0:r, 7, t, :], start=(t == 0), stop=True)
            for s in range(TT):
                ins = mm(bank[5][:, 3 * E:4 * E], ones[0:ROWS[s], :], rt[0:ROWS[s], 7, s, :], start=(s == 0), stop=(s == 2))
            ins.then_inc(rank_mm, 1)
            pe.wait_ge(w_ready, 1)
            for t in range(TT):
                r = ROWS[t]
                ins = tr(bank[6][0:E, P * t:P * t + r], routed[0:r, 1, t, 0:E], ident[0:r, 0:r])
            ins.then_inc(wT_mm, 1)
            pe.wait_ge(wT_ev, 1)
            pe.wait_ge(bd_ld, 16)
            for i in range(2 * TT):
                r = ROWS[i // 2]
                if i >= 4:
                    pe.wait_ge(acc_init, i - 3)
                mm(bank[i % 4][0:r, :], wT[0:E, P * (i // 2):P * (i // 2) + r],
                   bd_rows[:, HALF * (i % 2):HALF * (i % 2 + 1)], start=True, stop=True).then_inc(accb_mm, 1)
            pe.wait_ge(acc_init, 2 * TT)

            def gather(par, n_next):
                pe.wait_ge(oh_ready, n_next + 1)
                if not isinstance(n_next, int):
                    pe.wait_ge(xg_ev, n_next)
                for t in range(TT):
                    for hh in range(2):
                        ins = mm(bank[0][64 * hh:64 * hh + 64, :], oh[:, TT * par + t, :],
                                 h2[:, t, HALF * hh:HALF * (hh + 1)], start=(t == 0), stop=(t == TT - 1),
                                 skip_group_check=True)
                ins.then_inc(xg_mm, 1)

            def turn_tokens(n_next):
                pe.wait_ge(xg_ev, n_next + 1)
                if not isinstance(n_next, int):
                    pe.wait_ge(tpa_ev, n_next * 2)
                for j in range(4):
                    ins = tr(bank[1][:, P * j:P * (j + 1)], xg[:, P * j:P * (j + 1)], ident[:, :])
                ins.then_inc(tpa_mm, 1)

            def product(out, lhs, n, c0, done, scatter_mid=None):
                for k in range(KD):
                    s = c0 + k // 2
                    if k % 2 == 0:
                        pe.wait_ge(slot_ld[s], (n + (USES[s] + 1)) * 16)
                    for hh in range(2):
                        ins = mm(out[64 * hh:64 * hh + 64, :], lhs(k),
                                 ring[:, s, D * (k % 2) + HALF * hh:D * (k % 2) + HALF * (hh + 1)],
                                 start=(done is y_mm and k == 0), stop=(done is y_mm and k == KD - 1) or k == KD - 1,
                                 skip_group_check=True)
                    if k % 2 and k != KD - 1:
                        ins.then_inc(piece_used, 1)
                    if k == 3 and scatter_mid:
                        scatter_mid()
                ins.then_inc(done, 1)

            def bias(out, row, par):
                for hh in range(2):
                    mm(out[64 * hh:64 * hh + 64, :], ones[0:1, 0:SLOTS],
                       bias_row[par][:, row, HALF * hh:HALF * (hh + 1)], start=True, stop=False, skip_group_check=True)

            def half_of(buf, k):
                return buf[:, P * (k % 4) + 64 * (k // 4):P * (k % 4) + 64 * (k // 4) + 64]

            def scatter(t, group):
                if not isinstance(group, int):
                    pe.wait_ge(scat_add, group + 1)
                for hh in range(2):
                    ins = mm(bank[6 + hh][:, :], ohwT[64 * hh:64 * hh + 64, P * t:P * (t + 1)],
                             ysb[64 * hh:64 * hh + 64, :], start=True, stop=True)
                ins.then_inc(scat_mm, 1)

            gather(0, 0)
            turn_tokens(0)
            pe.wait_ge(work_zero, 2)
            pe.wait_ge(rounds_ready, 1)
            pairs = pe.value_load(npair[0:1, 0:1], min_val=PAIRS, max_val=PAIRS * MAX_ROUNDS)
            with pe.Fori(0, pairs) as i:
                for par in range(2):
                    n = i * 2 + par
                    pe.wait_ge(tpa_ev, n * 2 + 1)
                    pe.wait_ge(gate_read, n + 1)
                    pe.wait_ge(bias_ld[par], i * 32 + 32)
                    bias(bank[3], 0, par)
                    product(bank[3], lambda k: half_of(xgT, k), n, 0, gate_done)
                    pe.wait_ge(gate_done, n + 1)
                    pe.sem_inc(piece_used, 1)
                    pe.wait_ge(y_ev, n + 1)
                    scatter(0, n * 3)
                    pe.wait_ge(up_read, n + 1)
                    bias(bank[4], 1, par)
                    product(bank[4], lambda k: half_of(xgT, k), n, 4, up_done, lambda: scatter(1, n * 3 + 1))
                    pe.wait_ge(up_done, n + 1)
                    pe.sem_inc(piece_used, 1)
                    scatter(2, n * 3 + 2)
                    gather(1 - par, n + 1)
                    pe.wait_ge(tpa_ev, n * 2 + 1)
                    for t in range(TT):
                        ins = tr(bank[1][:, P * t:P * (t + 1)], ohw[:, TT * par + t, :], ident[:, :])
                    ins.then_inc(tpa_mm, 1)
                    pe.wait_ge(act_ready, n + 1)
                    pe.wait_ge(actT_ev, n + 1)
                    for j in range(4):
                        ins = tr(bank[2][:, P * j:P * (j + 1)], acts[:, P * j:P * (j + 1)], ident[:, :])
                    ins.then_inc(actT_mm, 1)
                    turn_tokens(n + 1)
                    pe.wait_ge(actT_ev, n + 2)
                    pe.wait_ge(y_ev, n + 1)
                    product(bank[5], lambda k: half_of(actT, k), n, 8, y_mm)
                    pe.wait_ge(y_mm, n + 1)
                    pe.sem_inc(piece_used, 1)
            pe.wait_ge(y_ev, pairs * 2 + 1)
            for t in range(TT):
                scatter(t, pairs * 6 + t)


_INS = ["x_prompt", "x_sample", "state_pool", "state_conv", "c_prompt", "c_sample", "norm1_g", "norm2_g", "final_g",
        "w_ada", "b_ada", "w_in", "pool_w", "pool_scale", "conv_dw", "conv_b", "conv_ln_g", "conv_ln_b", "conv_w_out",
        "gate_w", "gate_b", "w_out", "router_w", "router_b", "exp_w_gate", "exp_b_gate", "exp_w_up", "exp_b_up",
        "exp_w_down", "exp_b_down"]
_OUTS = [(1, 256, 1024), (1, 32, 1024), (1, 1, 15, 512), (1, 1, 30, 512), (1, 1, 15, 512), (1, 1, 30, 512)]


def kernel(**inputs):
    import numpy as _np
    import concourse.bacc as _bacc
    from concourse import mybir as _mybir
    from concourse.bass_utils import run_bass_kernel_spmd as _run

    nc = _bacc.Bacc("TRN2", target_bir_lowering=False, num_devices=1)
    arrays, args = {}, []
    for name in _INS:
        a = _np.ascontiguousarray(inputs[name])
        arrays[f"in_{name}"] = a
        args.append(nc.dram_tensor(f"in_{name}", a.shape, _mybir.dt.from_np(a.dtype), kind="ExternalInput").ap())
    for i, shape in enumerate(_OUTS):
        args.append(nc.dram_tensor(f"out_{i}", shape, _mybir.dt.float32, kind="ExternalOutput").ap())
    build(nc, *args)
    r = _run(nc, [arrays], core_ids=[0])
    return tuple(r.results[0][f"out_{i}"] for i in range(len(_OUTS)))
```

```python
from contextlib import ExitStack

import concourse.bass as bass
from concourse import mybir

F32 = mybir.dt.float32
I32 = mybir.dt.int32
ALU = mybir.AluOpType
ACT = mybir.ActivationFunctionType
AX = mybir.AxisListType.X

P = 128
D = 1024
KD = D // P
NP_TOK, NS_TOK = 256, 32
TOK = NP_TOK + NS_TOK
TT = 3
ROWS = [P, P, NS_TOK]
EPS = 1e-6
WINDOWS = (2, 4, 8, 16)
POOL_PAD = max(WINDOWS) - 1
WIDTH = 31
CONV_PAD = WIDTH - 1
DC = D // 2
CT = DC // P
E = 32
TOPK = 4
LIMIT = 7.0
ALPHA = 1.702
SLOTS = 64
MAX_ITEMS_E = -(-TOK // SLOTS)
MAX_ITEMS = E + TOPK * TOK // SLOTS
N_TAB = MAX_ITEMS + 2
HALF = 512
PSEG = [(POOL_PAD, 0, NP_TOK), (2 * POOL_PAD + NP_TOK, NP_TOK, NS_TOK)]
CSEG = [(CONV_PAD, 0, NP_TOK), (2 * CONV_PAD + NP_TOK, NP_TOK, NS_TOK)]
PEXT = TOK + 2 * POOL_PAD
CEXT = TOK + 2 * CONV_PAD
CW = CEXT - CONV_PAD

RING = 12
SLOT = 2 * D
PIECES = 12
FRONT = ([("ada", 0, k) for k in range(KD)] + [("in", c, 0) for c in (4, 2, 5, 3, 0, 1)]
         + [("gate", c, 0) for c in range(8)] + [("ada", b, k) for b in (1, 2) for k in range(KD)]
         + [("pool", 0, 0)] + [("conv", h, 0) for h in range(2)] + [("out", h, q) for h in range(2) for q in range(2)])
N_FRONT = len(FRONT)
F_END = -(-N_FRONT // RING) * RING
USES = [len([f for f in range(N_FRONT) if f % RING == s]) for s in range(RING)]

C_N1, C_GB, C_PS, C_CB, C_LG, C_LB, C_CP, C_CS, N_COLS = 0, 8, 24, 32, 36, 40, 44, 52, 60


def build(nc, x_prompt, x_sample, state_pool, state_conv, c_prompt, c_sample, norm1_g, norm2_g, final_g,
          w_ada, b_ada, w_in, pool_w, pool_scale, conv_dw, conv_b, conv_ln_g, conv_ln_b, conv_w_out,
          gate_w, gate_b, w_out, router_w, router_b, exp_w_gate, exp_b_gate, exp_w_up, exp_b_up,
          exp_w_down, exp_b_down, y_prompt, y_sample, new_pool_p, new_conv_p, new_pool_s, new_conv_s):
    with ExitStack() as ctx:
        def sb(name, shape, dt=F32):
            return ctx.enter_context(nc.sbuf_tensor(name, shape, dt))

        def sem(name):
            return ctx.enter_context(nc.semaphore(name))

        ring = sb("ring", [P, RING, SLOT])
        x = sb("x", [P, TT, D])
        h2 = sb("h2", [P, TT, D])
        ident = sb("ident", [P, P])
        before = sb("before", [P, P])
        ones = sb("ones", [P, P])
        slot_no = sb("slot_no", [P, 2, SLOTS])
        pick = sb("pick", [P, 8, P])
        ada_sel = sb("ada_sel", [12, 12, 32])
        bada = sb("bada", [12, HALF])
        n2rows = sb("n2rows", [64, HALF])
        stage = sb("stage", [N_COLS, P])
        cols = sb("cols", [P, N_COLS])
        dwc = sb("dwc", [P, CT, 32])
        biases = sb("biases", [P, 2, D])
        rw = sb("rw", [P, KD, E])
        rb = sb("rb", [1, E])
        cT = sb("cT", [P, KD, 32])
        csig = sb("csig", [P, 16])
        shc = sb("shc", [P, 2 * KD])
        scc = sb("scc", [P, 2 * KD])
        invc = sb("invc", [P, CT, 16])
        stat = sb("stat", [P, 32])
        logit = sb("logit", [P, TT, E])
        rt = sb("rt", [P, 8, TT, E])
        top = sb("top", [P, TT, 8])
        routed = sb("routed", [P, 2, TT, E + 1])
        item_col = sb("item_col", [P, 2, TT])
        base = sb("base", [P, 2, E + 1])
        base_i = sb("base_i", [1, E + 1], I32)
        owner = rt[:, 3, :, :].rearrange("p t e -> p (t e)")[:, 0:N_TAB]
        owner_i = sb("owner_i", [1, 2, N_TAB], I32)
        first = sb("first", [P, N_TAB])
        arena = sb("arena", [P, 15088])

        def view(start, *shape):
            n = 1
            for s in shape:
                n *= s
            a = arena[:, start:start + n]
            if len(shape) == 2:
                a = a.rearrange("p (a b) -> p a b", b=shape[1])
            return a

        hT = view(0, KD, TOK)
        gates = view(2304, 2 * KD, TOK)
        merged = view(6912, KD, TOK)
        sig_g = view(6912, CT, TOK)
        up_ext = view(9216, CT, PEXT)
        pooled = view(10488, CT, TOK)
        wsum = view(11640, 2, PEXT)
        rows = view(12276, 3, HALF)
        tmp = view(13812, CT, CW)
        act_c = view(0, CT, TOK)
        slot_i = view(13812, 2, SLOTS).bitcast(I32)
        h2flat = h2[:, :, :].rearrange("p a b -> p (a b)")
        uc_ext = h2flat[:, 0:CT * CEXT].rearrange("p (a b) -> p a b", b=CEXT)
        yc = h2flat[:, CT * CEXT:CT * CEXT + CT * CW].rearrange("p (a b) -> p a b", b=CW)
        g1b = view(0, 2, D)
        a2b = view(2304, 2, D)
        sh2b = view(4352, 2, D)
        g2b = view(9216, 2, D)
        h2T = view(6912, KD, TOK)
        acc = view(2304, TT, D)
        xg = view(5376, HALF)
        xgT = view(5888, HALF)
        ohwT = view(6400, TT * P)
        gmin = view(0, HALF)
        gsig = view(512, HALF)
        ucl = view(1024, HALF)
        acts = view(1536, HALF)
        actT = view(6912, HALF)
        ysb = view(7424, HALF)
        oh = view(7936, TT, SLOTS)
        ohw = view(8320, TT, 2 * SLOTS)
        cmp = view(0, N_TAB, E)
        fgb = view(11640, D)
        wT = view(12664, TOK)
        bd_rows = view(13812, D)[0:E, :]
        bias_row = biases[0:1, :, :]
        ybuf = h2

        bank = [ctx.enter_context(nc.psum_tensor(f"bank{i}", [P, HALF], F32)) for i in range(8)]

        slot_ld = [sem(f"slot_ld{s}") for s in range(RING)]
        piece_used = sem("piece_used")
        x_ld = sem("x_ld")
        c_ld = sem("c_ld")
        dw_ld = sem("dw_ld")
        st_ld = sem("st_ld")
        ada_ld = sem("ada_ld")
        n2_ld = sem("n2_ld")
        router_ld = sem("router_ld")
        bd_ld = sem("bd_ld")
        fg_ld = sem("fg_ld")
        bias_ld = sem("bias_ld")
        weights_ready = sem("weights_ready")
        const = sem("const")
        chain_p = sem("chain_p")
        ssq = sem("ssq")
        chain_v = sem("chain_v")
        chain_a = sem("chain_a")
        xn_ready = sem("xn_ready")
        colT = sem("colT")
        cols_ready = sem("cols_ready")
        csig_ready = sem("csig_ready")
        cT_ready = sem("cT_ready")
        dwT = sem("dwT")
        dw_ready = sem("dw_ready")
        stT = sem("stT")
        hist_ready = sem("hist_ready")
        xT = sem("xT")
        xT_ev = sem("xT_ev")
        ada_mm = sem("ada_mm")
        rows_ready = sem("rows_ready")
        modT = sem("modT")
        mod_ready = sem("mod_ready")
        hT_ready = sem("hT_ready")
        in_mm = sem("in_mm")
        in_ev = sem("in_ev")
        sig_ready = sem("sig_ready")
        u_ready = sem("u_ready")
        pu_ready = sem("pu_ready")
        gate_mm = sem("gate_mm")
        gate_ev = sem("gate_ev")
        a2rows = sem("a2rows")
        outT = sem("outT")
        out_ev = sem("out_ev")
        pooled_ready = sem("pooled_ready")
        conv_step = sem("conv_step")
        mean_mm = sem("mean_mm")
        mean_ready = sem("mean_ready")
        cen_ready = sem("cen_ready")
        sq_ready = sem("sq_ready")
        zeroed = sem("zeroed")
        var_mm = sem("var_mm")
        std_ready = sem("std_ready")
        yn_ready = sem("yn_ready")
        zsig_ready = sem("zsig_ready")
        act_c_ready = sem("act_c_ready")
        pm_mm = sem("pm_mm")
        pm_ev = sem("pm_ev")
        cm_mm = sem("cm_mm")
        cm_ev = sem("cm_ev")
        merged_ready = sem("merged_ready")
        bc_mm = sem("bc_mm")
        bc_ev = sem("bc_ev")
        wo_mm = sem("wo_mm")
        wo_ev = sem("wo_ev")
        x2_ready = sem("x2_ready")
        ssq2 = sem("ssq2")
        sqrt_ready = sem("sqrt_ready")
        mean2 = sem("mean2")
        h2_ready = sem("h2_ready")
        h2T_mm = sem("h2T_mm")
        h2T_even = sem("h2T_even")
        h2T_odd = sem("h2T_odd")
        hist0_ready = sem("hist0_ready")
        logit_mm = sem("logit_mm")
        shifted = sem("shifted")
        exp_ready = sem("exp_ready")
        sel_ready = sem("sel_ready")
        rank_mm = sem("rank_mm")
        w_ready = sem("w_ready")
        wT_mm = sem("wT_mm")
        wT_ev = sem("wT_ev")
        accb_mm = sem("accb_mm")
        acc_init = sem("acc_init")
        base_ready = sem("base_ready")
        owner_ready = sem("owner_ready")
        work_zero = sem("work_zero")
        oh_ready = sem("oh_ready")
        ohw_ready = sem("ohw_ready")
        xg_mm = sem("xg_mm")
        xg_ev = sem("xg_ev")
        tpa_mm = sem("tpa_mm")
        tpa_ev = sem("tpa_ev")
        gate_done = sem("gate_done")
        gate_read = sem("gate_read")
        gsig_ready = sem("gsig_ready")
        up_done = sem("up_done")
        up_read = sem("up_read")
        gs_ready = sem("gs_ready")
        act_ready = sem("act_ready")
        actT_mm = sem("actT_mm")
        actT_ev = sem("actT_ev")
        y_mm = sem("y_mm")
        y_ev = sem("y_ev")
        scat_mm = sem("scat_mm")
        scat_add = sem("scat_add")
        col_ready = sem("col_ready")
        ssq3 = sem("ssq3")
        sqrt3 = sem("sqrt3")
        y_ready = sem("y_ready")
        stored = sem("stored")

        wada_v = w_ada[0].rearrange("(k p) n -> k p n", p=P)
        win_v = w_in[0].rearrange("(k p) n -> p k n", p=P)
        gate_v = gate_w[0].rearrange("(k p) n -> p k n", p=P)
        poolw_v = pool_w[0].rearrange("g c o -> c g o")
        convw_v = conv_w_out[0].rearrange("(k p) n -> p k n", p=P)
        wout_v = w_out[0].rearrange("(k p) n -> p k n", p=P)
        wg_v = exp_w_gate[0].rearrange("e (k p) n -> e p k n", p=P)
        wu_v = exp_w_up[0].rearrange("e (k p) n -> e p k n", p=P)
        wd_v = exp_w_down[0].rearrange("e (k p) n -> e p k n", p=P)

        def front_piece(f):
            kind, a, b = FRONT[f]
            slot = ring[:, f % RING, :]
            if kind == "ada":
                return wada_v[b][:, 4 * HALF * a:4 * HALF * (a + 1)], slot
            if kind in ("in", "gate"):
                src = win_v if kind == "in" else gate_v
                return src[:, :, 256 * a:256 * (a + 1)], slot.rearrange("p (k n) -> p k n", k=KD)
            if kind == "pool":
                return poolw_v, slot[:, 0:D].rearrange("p (k n) -> p k n", k=CT)
            if kind == "conv":
                return convw_v[:, :, HALF * a:HALF * (a + 1)], slot.rearrange("p (k n) -> p k n", k=CT)
            return (wout_v[:, 4 * b:4 * b + 4, HALF * a:HALF * (a + 1)], slot.rearrange("p (k n) -> p k n", k=4))

        def front_ready(eng, f):
            eng.wait_ge(slot_ld[f % RING], 16 * (f // RING + 1))

        first_of = {}
        for f, (kind, a, b) in enumerate(FRONT):
            first_of.setdefault((kind, a), f)

        pool_stage = [biases[0:POOL_PAD, 0, 0:DC], biases[0:CONV_PAD, 0, DC:D]]
        dw_stage = biases[0:WIDTH, 1, 0:DC]
        out_stage = [biases[0:POOL_PAD, 1, DC:D], biases[0:POOL_PAD, 1, 0:DC],
                     biases[0:CONV_PAD, 0, DC:D], biases[0:CONV_PAD, 0, 0:DC]]

        block = ctx.enter_context(nc.Block())

        @block.sync
        def _(sp):
            sp.dma_start(x[:, 0:2, :], x_prompt[0].rearrange("(t p) d -> p t d", p=P)).then_inc(x_ld, 16)
            sp.dma_start(x[0:NS_TOK, 2, :], x_sample[0]).then_inc(x_ld, 16)
            for f in range(N_FRONT):
                if f >= RING:
                    sp.wait_ge(piece_used, f - RING + 1)
                src, dst = front_piece(f)
                sp.dma_start(dst, src).then_inc(slot_ld[f % RING], 16)

            def expert(e, last_use):
                for i in range(PIECES):
                    sp.wait_ge(piece_used, last_use(i))
                    w = (wg_v, wu_v, wd_v)[i // 4]
                    sp.dma_start(ring[:, i, :].rearrange("p (k n) -> p k n", k=2),
                                 w[e][:, 2 * (i % 4):2 * (i % 4) + 2, :]).then_inc(slot_ld[i], 16)

            expert(0, lambda i: max(f for f in range(N_FRONT) if f % RING == i) + 1)
            sp.wait_ge(base_ready, 1)
            with sp.Fori(1, E) as e:
                at = sp.value_load(base_i[0:1, bass.ds(e, 1)], min_val=1, max_val=MAX_ITEMS)
                expert(e, lambda i: at * PIECES + (F_END - PIECES + i + 1))
            sp.dma_start(fgb, final_g.rearrange("(a d) -> a d", a=1).broadcast_to([P, D])).then_inc(fg_ld, 16)
            for t in range(TT):
                sp.wait_ge(y_ready, t + 1)
                dst = y_sample[0] if t == 2 else y_prompt[0, P * t:P * (t + 1), :]
                sp.dma_start(dst, ybuf[0:ROWS[t], t, :]).then_inc(stored, 16)
            sp.wait_ge(stored, 16 * (4 + TT))

        @block.gpsimd
        def _(pool):
            g = nc.gpsimd
            n = [0]

            def step(ins):
                n[0] += 1
                ins.then_inc(chain_p, 1)
                pool.wait_ge(chain_p, n[0])

            step(g.memset(ident[:, :], 0.0))
            g.affine_select(out=ident[:, :], in_=ident[:, :], compare_op=ALU.not_equal, fill=1.0, base=0,
                            pattern=[[-1, P]], channel_multiplier=1).then_inc(const, 1)
            g.memset(ones[:, :], 1.0).then_inc(const, 1)
            g.memset(cT[:, :, :], 0.0).then_inc(const, 1)
            step(g.memset(ada_sel[:, :, :], 0.0))
            g.affine_select(out=ada_sel[:, :, :], in_=ada_sel[:, :, :], compare_op=ALU.not_equal, fill=1.0,
                            base=0, pattern=[[-1, 12], [0, 32]], channel_multiplier=1).then_inc(const, 1)
            g.memset(up_ext[:, :, 0:POOL_PAD], 0.0).then_inc(const, 1)
            step(g.memset(before[:, :], 1.0))
            g.affine_select(out=before[:, :], in_=before[:, :], compare_op=ALU.is_gt, fill=0.0, base=0,
                            pattern=[[1, P]], channel_multiplier=-1).then_inc(const, 1)
            step(g.memset(pick[:, :, :], 0.0))
            g.affine_select(out=pick[:, :, :].rearrange("p (j g) n -> p j g n", g=2),
                            in_=pick[:, :, :].rearrange("p (j g) n -> p j g n", g=2),
                            compare_op=ALU.not_equal, fill=1.0, base=0,
                            pattern=[[-32, 4], [-1, 2], [0, P]], channel_multiplier=1).then_inc(const, 1)
            step(g.iota(slot_i[:, :, :], pattern=[[0, 2], [1, SLOTS]], base=0, channel_multiplier=0))
            step(g.tensor_copy(slot_no[:, :, :], slot_i[:, :, :]))
            for w in range(CT):
                step(g.tensor_scalar(invc[:, w, :], slot_no[:, 0, 0:16], 1.0, float(WINDOWS[w]), ALU.add, ALU.min))
            g.memset(dwc[:, :, :], 0.0).then_inc(const, 1)
            for w in range(CT):
                pool.wait_ge(pu_ready, w + 1)
                if w == 0:
                    pool.wait_ge(hist_ready, 1)
                    pool.wait_ge(mod_ready, 2)
                src = up_ext[:, w, :]
                for d in range(w + 1):
                    lo = (1 << (d + 1)) - 1
                    dst = wsum[:, d % 2, :]
                    step(g.tensor_tensor(dst[:, lo:], src[:, lo:], src[:, lo - (1 << d):PEXT - (1 << d)], ALU.add))
                    src = dst
                step(g.tensor_tensor(pooled[:, w, 0:16], src[:, POOL_PAD:POOL_PAD + 16], invc[:, w, :], ALU.mult))
                step(g.tensor_scalar(pooled[:, w, 16:NP_TOK], src[:, POOL_PAD + 16:POOL_PAD + NP_TOK],
                                     1.0 / WINDOWS[w], None, ALU.mult))
                c0, t0, m = PSEG[1]
                step(g.tensor_scalar(pooled[:, w, t0:t0 + m], src[:, c0:c0 + m], 1.0 / WINDOWS[w], None, ALU.mult))
                for c0, t0, m in PSEG:
                    ins = g.tensor_tensor(pooled[:, w, t0:t0 + m], pooled[:, w, t0:t0 + m], up_ext[:, w, c0:c0 + m],
                                          ALU.subtract)
                    if t0 == 0:
                        step(ins)
                ins.then_inc(pooled_ready, 1)

            pool.wait_ge(owner_ready, 1)
            items = pool.value_load(base_i[0:1, E:E + 1], min_val=E, max_val=MAX_ITEMS)
            with pool.Fori(0, items) as n_i:
                e = pool.value_load(owner_i[0:1, 0, bass.ds(n_i, 1)], min_val=0, max_val=E - 1)
                for i in range(PIECES):
                    pool.wait_ge(slot_ld[i], (e + (USES[i] + 1)) * 16)
                    pool.sem_inc(weights_ready, 1)

        @block.scalar
        def _(act):
            a = nc.scalar
            small = [(C_N1, norm1_g[0], 8), (C_GB, gate_b[0], 16), (C_PS, pool_scale[0], 8), (C_CB, conv_b[0], 4),
                     (C_LG, conv_ln_g[0], 4), (C_LB, conv_ln_b[0], 4), (C_CP, c_prompt[0], 8), (C_CS, c_sample[0], 8)]
            for at, src, k in small:
                act.dma_start(stage[at:at + k, :], src.rearrange("(k p) -> k p", p=P)).then_inc(c_ld, 16)
            act.dma_start(bada[:, :], b_ada[0].rearrange("(k n) -> k n", n=HALF)).then_inc(ada_ld, 16)
            act.dma_start(pool_stage[0], state_pool[0, 0]).then_inc(st_ld, 16)
            act.dma_start(pool_stage[1], state_conv[0, 0]).then_inc(st_ld, 16)
            act.dma_start(dw_stage, conv_dw[0]).then_inc(dw_ld, 16)
            n2 = norm2_g[0].rearrange("(a j n) -> a j n", a=1, n=HALF)
            act.wait_ge(zeroed, 1)
            for j in range(2):
                for gg in range(2):
                    act.dma_start(n2rows[32 * j + gg:32 * j + gg + 1, :], n2[:, j, :]).then_inc(n2_ld, 16)
            act.dma_start(rw[:, :, :], router_w[0].rearrange("(k p) e -> p k e", p=P)).then_inc(router_ld, 16)
            act.dma_start(rb[:, :], router_b[0:1, :]).then_inc(router_ld, 16)

            act.wait_ge(x_ld, 32)
            for t in range(TT):
                r = ROWS[t]
                a.activation(view(2304 + D * t, D)[0:r, :], x[0:r, t, :], ACT.Square,
                             accum_out=stat[0:r, t:t + 1]).then_inc(ssq, 1)
            act.wait_ge(mean2, 1)
            a.activation(stat[:, 4:7], stat[:, 8:11], ACT.Sqrt).then_inc(sqrt_ready, 1)
            act.wait_ge(cols_ready, 1)
            a.activation(csig[:, :], cols[:, C_CP:C_CP + 16], ACT.Sigmoid).then_inc(csig_ready, 1)
            act.wait_ge(stT, 1)
            act.wait_ge(xn_ready, 3)
            act.wait_ge(xT, KD)
            a.activation(up_ext[:, :, NP_TOK + POOL_PAD:NP_TOK + 2 * POOL_PAD],
                         bank[6][:, 0:CT * 32].rearrange("p (c n) -> p c n", n=32)[:, :, 0:POOL_PAD],
                         ACT.Copy).then_inc(hist_ready, 1)
            a.activation(uc_ext[:, :, NP_TOK + CONV_PAD:NP_TOK + 2 * CONV_PAD],
                         bank[6][:, 128:128 + CT * 32].rearrange("p (c n) -> p c n", n=32)[:, :, 0:CONV_PAD],
                         ACT.Copy).then_inc(hist_ready, 1)
            act.wait_ge(ada_mm, 1)
            a.activation(rows[:, 0, :], bank[4][:, :], ACT.Copy).then_inc(rows_ready, 1)
            for n in range(12):
                if n in (0, 1, 4, 5):
                    c = n if n < 2 else n - 2
                    act.wait_ge(in_mm, n + 1)
                    ins = a.activation(sig_g[:, c, :], bank[n % 4][:, 0:TOK], ACT.Sigmoid)
                    ins.then_inc(sig_ready, 1)
                    act.wait_ge(sig_ready, c + 1)
                elif n >= 8:
                    act.wait_ge(in_mm, n + 1)
                    for c0, t0, m in PSEG:
                        ins = a.activation(up_ext[:, n - 8, c0:c0 + m], bank[n % 4][:, t0:t0 + m], ACT.Copy)
                    ins.then_inc(pu_ready, 1)
            for n in range(2 * KD):
                act.wait_ge(gate_mm, n + 1)
                a.activation(gates[:, n, :], bank[n % 4][:, 0:TOK], ACT.Sigmoid,
                             bias=cols[:, C_GB + n:C_GB + n + 1]).then_inc(gate_ev, 1)
            for b in (1, 2):
                act.wait_ge(ada_mm, b + 1)
                a.activation(rows[:, b, :], bank[4 + b - 1][:, :], ACT.Copy).then_inc(rows_ready, 1)
            for i in range(4):
                r = POOL_PAD if i < 2 else CONV_PAD
                act.wait_ge(outT, i + 1)
                a.activation(out_stage[i], bank[6 + i % 2][0:r, :], ACT.Copy).then_inc(out_ev, 1)
            for i, dst in enumerate((new_pool_p, new_pool_s, new_conv_p, new_conv_s)):
                act.wait_ge(out_ev, i + 1)
                act.dma_start(dst[0, 0], out_stage[i]).then_inc(stored, 16)
            act.wait_ge(mean_mm, 1)
            a.activation(view(11640, CW), bank[6][:, 0:CW], ACT.Copy, scale=1.0 / DC).then_inc(mean_ready, 1)
            act.wait_ge(cen_ready, 1)
            a.activation(tmp[:, :, :], yc[:, :, :], ACT.Square).then_inc(sq_ready, 1)
            act.wait_ge(var_mm, 1)
            act.wait_ge(chain_a, 1)
            a.activation(view(11640, CW), view(11640 + CW, CW), ACT.Sqrt).then_inc(std_ready, 1)
            act.wait_ge(yn_ready, 1)
            for c in range(CT):
                a.activation(tmp[:, c, :], yc[:, c, :], ACT.Sigmoid, scale=cols[:, C_LG + c:C_LG + c + 1],
                             bias=cols[:, C_LB + c:C_LB + c + 1]).then_inc(zsig_ready, 1)
            for i in range(16):
                which, gg, hh = i // 4, (i // 2) % 2, i % 2
                act.wait_ge(bc_mm, i + 1)
                if i == 0:
                    act.wait_ge(pm_ev, KD)
                    act.wait_ge(out_ev, 2)
                if which == 2:
                    act.wait_ge(merged_ready, KD)
                dst = (g2b, g1b, sh2b, a2b)[which]
                r = P if gg == 0 else NS_TOK
                a.activation(dst[0:r, gg, HALF * hh:HALF * (hh + 1)], bank[i % 4][0:r, :], ACT.Copy).then_inc(bc_ev, 1)
            for i in range(2 * TT):
                hh, t = i // TT, i % TT
                r = ROWS[t]
                act.wait_ge(x2_ready, i + 1)
                a.activation(h2[0:r, t, HALF * hh:HALF * (hh + 1)], x[0:r, t, HALF * hh:HALF * (hh + 1)], ACT.Square,
                             accum_out=stat[0:r, 12 + 3 * hh + t:13 + 3 * hh + t]).then_inc(ssq2, 1)
            act.dma_start(bd_rows, exp_b_down[0]).then_inc(bd_ld, 16)
            act.wait_ge(mean2, 2)
            a.activation(stat[:, 4:7], stat[:, 8:11], ACT.Sqrt).then_inc(sqrt_ready, 1)
            for k in range(1, KD, 2):
                act.wait_ge(h2T_mm, k + 1)
                a.activation(h2T[:, k, :], bank[k % 4][:, 0:TOK], ACT.Copy).then_inc(h2T_odd, 1)
            act.wait_ge(shifted, 1)
            a.activation(rt[:, 5, :, :], rt[:, 4, :, :], ACT.Exp).then_inc(exp_ready, 1)
            act.wait_ge(wT_mm, 1)
            a.activation(wT[0:E, :], bank[6][0:E, 0:TOK], ACT.Copy).then_inc(wT_ev, 1)
            for i in range(2 * TT):
                r = ROWS[i // 2]
                act.wait_ge(accb_mm, i + 1)
                a.activation(acc[0:r, i // 2, HALF * (i % 2):HALF * (i % 2 + 1)], bank[i % 4][0:r, :],
                             ACT.Copy).then_inc(acc_init, 1)

            act.wait_ge(xg_mm, 1)
            a.activation(xg, bank[0][:, :], ACT.Copy).then_inc(xg_ev, 1)
            act.wait_ge(tpa_mm, 1)
            a.activation(xgT, bank[1][:, :], ACT.Copy).then_inc(tpa_ev, 1)
            for free in (actT_ev, y_ev):
                act.sem_inc(free, 1)
            act.wait_ge(stored, 64)
            for j, src in enumerate((exp_b_gate, exp_b_up)):
                act.dma_start(bias_row[:, j, :], src[0:1, 0, :]).then_inc(bias_ld, 16)
            act.wait_ge(owner_ready, 1)
            items = act.value_load(base_i[0:1, E:E + 1], min_val=E, max_val=MAX_ITEMS)
            with act.Fori(0, items) as n:
                nxt = act.value_load(owner_i[0:1, 1, bass.ds(n + 1, 1)], min_val=0, max_val=E - 1)
                act.wait_ge(gate_read, n + 2)
                a.activation(gsig, gmin, ACT.Sigmoid, scale=ALPHA).then_inc(gsig_ready, 1)
                act.wait_ge(xg_mm, n + 2)
                a.activation(xg, bank[0][:, :], ACT.Copy).then_inc(xg_ev, 1)
                act.wait_ge(up_done, n + 1)
                for j, src in enumerate((exp_b_gate, exp_b_up)):
                    act.dma_start(bias_row[:, j, :], src[0:1, bass.ds(nxt, 1), :].rearrange("a e d -> a (e d)")) \
                        .then_inc(bias_ld, 16)
                act.wait_ge(tpa_mm, n * 2 + 2)
                a.activation(ohwT, bank[1][:, 0:TT * P], ACT.Copy).then_inc(tpa_ev, 1)
                act.wait_ge(actT_mm, n + 1)
                a.activation(actT, bank[2][:, :], ACT.Copy).then_inc(actT_ev, 1)
                act.wait_ge(tpa_mm, n * 2 + 3)
                a.activation(xgT, bank[1][:, :], ACT.Copy).then_inc(tpa_ev, 1)
                act.wait_ge(y_mm, n + 1)
                a.activation(ysb, bank[5][:, :], ACT.Copy).then_inc(y_ev, 1)
            act.wait_ge(bias_ld, items * 32 + 32)
            for t in range(TT):
                r = ROWS[t]
                act.wait_ge(ssq3, t + 1)
                a.activation(ring[0:r, t, 0:D], acc[0:r, t, :], ACT.Square,
                             accum_out=stat[0:r, 20 + t:21 + t]).then_inc(sqrt3, 1)
            act.wait_ge(mean2, 3)
            a.activation(stat[:, 4:7], stat[:, 8:11], ACT.Sqrt).then_inc(sqrt_ready, 1)

        @block.vector
        def _(dve):
            v = nc.vector
            n = [0]

            def step(ins):
                n[0] += 1
                ins.then_inc(chain_v, 1)
                dve.wait_ge(chain_v, n[0])

            def rstd(sums, count):
                ins = v.tensor_scalar(stat[:, 8:11], sums, 1.0 / D, EPS, ALU.mult, ALU.add)
                ins.then_inc(mean2, 1)
                dve.wait_ge(sqrt_ready, count)
                step(v.reciprocal(stat[:, 4:7], stat[:, 4:7]))

            step(v.memset(stat[:, :], 0.0))
            v.memset(n2rows[:, :], 0.0).then_inc(zeroed, 1)
            dve.wait_ge(ssq, TT)
            rstd(stat[:, 0:3], 1)
            for t in range(TT):
                r = ROWS[t]
                v.tensor_scalar(h2[0:r, t, :], x[0:r, t, :], stat[0:r, 4 + t:5 + t], None, ALU.mult).then_inc(xn_ready, 1)
            dve.wait_ge(colT, 1)
            v.tensor_copy(cols[:, :], bank[5][:, 0:N_COLS]).then_inc(cols_ready, 1)
            dve.wait_ge(csig_ready, 1)
            dve.wait_ge(cols_ready, 1)
            dve.wait_ge(const, 3)
            v.tensor_tensor(cT[:, :, 0:2], cols[:, C_CP:C_CP + 16].rearrange("p (g k) -> p k g", g=2),
                            csig[:, :].rearrange("p (g k) -> p k g", g=2), ALU.mult).then_inc(cT_ready, 1)
            dve.wait_ge(dwT, 1)
            dve.wait_ge(const, 8)
            v.tensor_copy(dwc[:, :, 0:WIDTH], bank[7][:, 0:CT * 32].rearrange("p (c n) -> p c n", n=32)[:, :, 0:WIDTH]) \
                .then_inc(dw_ready, 1)
            for k in range(KD):
                dve.wait_ge(xT, k + 1)
                v.tensor_copy(hT[:, k, :], bank[k % 4][:, 0:TOK]).then_inc(xT_ev, 1)
            v.memset(uc_ext[:, :, 0:CONV_PAD], 0.0).then_inc(hist0_ready, 1)
            v.reciprocal(invc[:, :, :], invc[:, :, :]).then_inc(mod_ready, 1)
            dve.wait_ge(modT, 1)
            modv = bank[7][:, :].rearrange("p (r j m) -> p j r m", r=4, m=32)
            four = "p (j r g) -> p j r g"
            step(v.tensor_copy(shc[:, :].rearrange(four, j=2, g=2), modv[:, 0:2, :, 0:2]))
            step(v.tensor_copy(scc[:, :].rearrange(four, j=2, g=2), modv[:, 2:4, :, 0:2]))
            for gg in range(2):
                s = scc[:, :].rearrange("p (k g) -> p g k", g=2)[:, gg, :]
                ins = v.scalar_tensor_tensor(out=s, in0=s, scalar=1.0, in1=cols[:, C_N1:C_N1 + KD],
                                             op0=ALU.add, op1=ALU.mult)
                step(ins) if gg == 0 else ins.then_inc(mod_ready, 1)
            dve.wait_ge(mod_ready, 2)
            dve.wait_ge(xT_ev, KD)
            for k in range(KD):
                for gg, (t0, m) in enumerate(((0, NP_TOK), (NP_TOK, NS_TOK))):
                    ins = v.tensor_scalar(hT[:, k, t0:t0 + m], hT[:, k, t0:t0 + m], scc[:, 2 * k + gg:2 * k + gg + 1],
                                          shc[:, 2 * k + gg:2 * k + gg + 1], ALU.mult, ALU.add)
                ins.then_inc(hT_ready, 1)
            dve.wait_ge(hist_ready, 2)
            dve.wait_ge(hist0_ready, 1)
            steps = [0]

            def glu(tiles):
                for c in tiles:
                    m_in = c + 2 if c < 2 else c + 4
                    dve.wait_ge(in_mm, m_in + 1)
                    dve.wait_ge(sig_ready, c + 1)
                    for c0, t0, m in CSEG:
                        ins = v.tensor_tensor(uc_ext[:, c, c0:c0 + m], bank[m_in % 4][:, t0:t0 + m],
                                              sig_g[:, c, t0:t0 + m], ALU.mult)
                    ins.then_inc(u_ready, 1)

            def conv(tiles):
                for k in range(WIDTH):
                    for c in tiles:
                        if k:
                            dve.wait_ge(conv_step, steps[0] - 1)
                        tap = dwc[:, c, k:k + 1]
                        if k == 0:
                            ins = v.tensor_scalar(yc[:, c, :], uc_ext[:, c, 0:CW], tap, cols[:, C_CB + c:C_CB + c + 1],
                                                  ALU.mult, ALU.add)
                        else:
                            ins = v.scalar_tensor_tensor(out=yc[:, c, :], in0=uc_ext[:, c, k:k + CW], scalar=tap,
                                                         in1=yc[:, c, :], op0=ALU.mult, op1=ALU.add)
                        ins.then_inc(conv_step, 1)
                        steps[0] += 1

            glu((0, 1))
            glu((2, 3))
            dve.wait_ge(u_ready, 4)
            dve.wait_ge(dw_ready, 1)
            conv((0, 1))
            conv((2, 3))
            dve.wait_ge(rows_ready, 3)
            dve.wait_ge(n2_ld, 64)
            v.scalar_tensor_tensor(out=rows[0:64, 2, :], in0=rows[0:64, 2, :], scalar=1.0, in1=n2rows[:, :],
                                   op0=ALU.add, op1=ALU.mult).then_inc(a2rows, 1)
            dve.wait_ge(gate_ev, 2 * KD)
            for m in range(KD):
                dve.wait_ge(pm_mm, m + 1)
                v.scalar_tensor_tensor(out=merged[:, m, :], in0=bank[m % 4][:, 0:TOK],
                                       scalar=cols[:, C_PS + m:C_PS + m + 1], in1=gates[:, m, :],
                                       op0=ALU.mult, op1=ALU.mult).then_inc(pm_ev, 1)
            dve.wait_ge(mean_ready, 1)
            for c in range(CT):
                ins = v.tensor_tensor(yc[:, c, :], yc[:, c, :], view(11640, CW), ALU.subtract)
            ins.then_inc(cen_ready, 1)
            dve.wait_ge(var_mm, 1)
            v.tensor_scalar(view(11640 + CW, CW), bank[7][:, 0:CW], 1.0 / DC, EPS, ALU.mult, ALU.add).then_inc(chain_a, 1)
            dve.wait_ge(std_ready, 1)
            step(v.reciprocal(view(11640, CW), view(11640, CW)))
            for c in range(CT):
                ins = v.tensor_tensor(yc[:, c, :], yc[:, c, :], view(11640, CW), ALU.mult)
            ins.then_inc(yn_ready, 1)
            dve.wait_ge(yn_ready, 1)
            dve.wait_ge(zsig_ready, CT)
            for c in range(CT):
                ins = v.tensor_scalar(yc[:, c, :], yc[:, c, :], cols[:, C_LG + c:C_LG + c + 1],
                                      cols[:, C_LB + c:C_LB + c + 1], ALU.mult, ALU.add)
                step(ins)
            for c in range(CT):
                for (c0, t0, m) in ((0, 0, NP_TOK), (NP_TOK + CONV_PAD, NP_TOK, NS_TOK)):
                    step(v.tensor_tensor(act_c[:, c, t0:t0 + m], yc[:, c, c0:c0 + m], tmp[:, c, c0:c0 + m], ALU.mult))
            v.memset(h2[:, 2, :], 0.0).then_inc(act_c_ready, 1)
            dve.wait_ge(pm_ev, KD)
            for m in range(KD):
                dve.wait_ge(cm_mm, m + 1)
                v.tensor_tensor(gates[:, KD + m, :], bank[m % 4][:, 0:TOK], gates[:, KD + m, :], ALU.mult).then_inc(cm_ev, 1)
                dve.wait_ge(cm_ev, m + 1)
                v.tensor_tensor(merged[:, m, :], merged[:, m, :], gates[:, KD + m, :], ALU.add).then_inc(merged_ready, 1)
            dve.wait_ge(bc_ev, 8)
            for i in range(2 * TT):
                hh, t = i // TT, i % TT
                r, gg = ROWS[t], t // 2
                cs = slice(HALF * hh, HALF * (hh + 1))
                dve.wait_ge(wo_mm, i + 1)
                v.tensor_tensor(view(13812 + HALF * (i % 2), HALF)[0:r, :], bank[4 + i % 4][0:r, :], g1b[0:r, gg, cs], ALU.mult).then_inc(wo_ev, 1)
                dve.wait_ge(wo_ev, i + 1)
                v.tensor_tensor(x[0:r, t, cs], x[0:r, t, cs], view(13812 + HALF * (i % 2), HALF)[0:r, :], ALU.add).then_inc(x2_ready, 1)
            dve.wait_ge(ssq2, 2 * TT)
            step(v.tensor_tensor(stat[:, 0:3], stat[:, 12:15], stat[:, 15:18], ALU.add))
            rstd(stat[:, 0:3], 2)
            dve.wait_ge(bc_ev, 16)
            for t in range(TT):
                r, gg = ROWS[t], t // 2
                step(v.scalar_tensor_tensor(out=h2[0:r, t, :], in0=x[0:r, t, :], scalar=stat[0:r, 4 + t:5 + t],
                                            in1=a2b[0:r, gg, :], op0=ALU.mult, op1=ALU.mult))
                v.tensor_tensor(h2[0:r, t, :], h2[0:r, t, :], sh2b[0:r, gg, :], ALU.add).then_inc(h2_ready, 1)
            for k in range(0, KD, 2):
                dve.wait_ge(h2T_mm, k + 1)
                v.tensor_copy(h2T[:, k, :], bank[k % 4][:, 0:TOK]).then_inc(h2T_even, 1)

            def wide(ap):
                return ap.broadcast_to([P, TT, E])

            step(v.memset(logit[:, :, :], 0.0))
            dve.wait_ge(logit_mm, 1)
            v.tensor_copy(logit[:, 0:2, :], bank[4][:, 0:2 * E].rearrange("p (t e) -> p t e", e=E))
            step(v.tensor_copy(logit[0:NS_TOK, 2, :], bank[4][0:NS_TOK, 2 * E:3 * E]))
            for t in range(TT):
                ins = v.max(top[:, t, :], logit[:, t, :])
            step(ins)
            v.tensor_tensor(rt[:, 4, :, :], logit[:, :, :], wide(top[:, :, 0:1]), ALU.subtract).then_inc(shifted, 1)
            v.tensor_tensor(rt[:, 0, :, :], logit[:, :, :], wide(top[:, :, 3:4]), ALU.is_gt)
            step(v.tensor_tensor(rt[:, 1, :, :], logit[:, :, :], wide(top[:, :, 3:4]), ALU.is_equal))
            v.tensor_copy(rt[:, 2, :, :], rt[:, 1, :, :])
            step(v.tensor_reduce(stat[:, 24:27], rt[:, 0, :, :], AX, ALU.add))
            src = 2
            for d in (1, 2, 4, 8, 16):
                dst = 3 if src == 2 else 2
                v.tensor_copy(rt[:, dst, :, 0:d], rt[:, src, :, 0:d])
                step(v.tensor_tensor(rt[:, dst, :, d:E], rt[:, src, :, d:E], rt[:, src, :, 0:E - d], ALU.add))
                src = dst
            for t in range(TT):
                ins = v.tensor_scalar(rt[:, 6, t, :], rt[:, src, t, :], stat[:, 24 + t:25 + t], float(TOPK), ALU.add, ALU.is_le)
            step(ins)
            step(v.tensor_tensor(rt[:, 6, :, :], rt[:, 6, :, :], rt[:, 1, :, :], ALU.mult))
            v.tensor_tensor(rt[:, 7, :, :], rt[:, 6, :, :], rt[:, 0, :, :], ALU.add).then_inc(sel_ready, 1)
            dve.wait_ge(sel_ready, 1)
            dve.wait_ge(exp_ready, 1)
            step(v.tensor_tensor(rt[:, 5, :, :], rt[:, 5, :, :], rt[:, 7, :, :], ALU.mult))
            step(v.tensor_reduce(stat[:, 24:27], rt[:, 5, :, :], AX, ALU.add))
            step(v.reciprocal(stat[:, 27:30], stat[:, 24:27]))
            for t in range(TT):
                ins = v.tensor_scalar(routed[:, 1, t, 0:E], rt[:, 5, t, :], stat[:, 27 + t:28 + t], None, ALU.mult)
            ins.then_inc(w_ready, 1)
            dve.wait_ge(w_ready, 1)
            v.memset(routed[:, 1, :, E:E + 1], 0.0)
            v.memset(routed[:, 0, :, E:E + 1], -1.0)
            dve.wait_ge(rank_mm, 1)
            step(v.memset(rt[:, 0, :, :], 0.0))
            step(v.tensor_copy(rt[:, 0, 0:2, :], bank[5][:, 0:2 * E].rearrange("p (t e) -> p t e", e=E)))
            step(v.tensor_copy(rt[0:NS_TOK, 0, 2, :], bank[5][0:NS_TOK, 2 * E:3 * E]))
            step(v.scalar_tensor_tensor(out=rt[:, 0, :, :], in0=rt[:, 0, :, :], scalar=1.0, in1=rt[:, 7, :, :],
                                        op0=ALU.add, op1=ALU.mult))
            step(v.tensor_scalar(routed[:, 0, :, 0:E], rt[:, 0, :, :], -1.0, None, ALU.add))
            step(v.tensor_copy(rt[:, 1, 0, :], bank[5][:, 3 * E:4 * E]))
            step(v.tensor_scalar(rt[:, 2, 0, :], rt[:, 1, 0, :], float(SLOTS), 1.0, ALU.is_gt, ALU.add))
            for m in range(2, MAX_ITEMS_E):
                step(v.scalar_tensor_tensor(out=rt[:, 2, 0, :], in0=rt[:, 1, 0, :], scalar=float(m * SLOTS),
                                            in1=rt[:, 2, 0, :], op0=ALU.is_gt, op1=ALU.add))
            v.memset(base[:, :, 0:1], 0.0)
            step(v.tensor_copy(base[:, 1, 1:E + 1], rt[:, 2, 0, :]))
            src = 1
            for d in (1, 2, 4, 8, 16):
                v.tensor_copy(base[:, 1 - src, 1:1 + d], base[:, src, 1:1 + d])
                step(v.tensor_tensor(base[:, 1 - src, 1 + d:], base[:, src, 1 + d:], base[:, src, 1:E + 1 - d], ALU.add))
                src = 1 - src
            base_f = base[:, src, :]
            v.tensor_copy(base_i[:, :], base_f[0:1, :]).then_inc(base_ready, 1)

            both = slot_no[:, :, :].rearrange("p a b -> p (a b)")

            def one_hot():
                for t in range(TT):
                    ins = v.tensor_scalar(oh[:, t, :], slot_no[:, 0, :], item_col[:, 0, t:t + 1], None, ALU.is_equal)
                ins.then_inc(oh_ready, 1)

            for free in (gate_read, up_read, scat_add):
                dve.sem_inc(free, 1)
            dve.wait_ge(wT_mm, 1)
            dve.wait_ge(acc_init, 2 * TT)
            v.memset(ohwT, 0.0).then_inc(work_zero, 1)
            v.memset(ysb, 0.0).then_inc(work_zero, 1)
            step(v.tensor_copy(item_col[:, :, :], routed[:, :, :, 0]))
            one_hot()
            item_no = slot_no[:, 0, 0:N_TAB].unsqueeze(2).broadcast_to([P, N_TAB, E])
            ends = base_f[:, 1:E + 1].unsqueeze(1).broadcast_to([P, N_TAB, E])
            step(v.tensor_tensor(cmp, item_no, ends, ALU.is_ge))
            step(v.tensor_reduce(owner, cmp, AX, ALU.add))
            step(v.tensor_tensor(cmp, cmp, ends, ALU.mult))
            step(v.tensor_reduce(first[:, :], cmp, AX, ALU.max))
            step(v.tensor_tensor(first[:, :], slot_no[:, 0, 0:N_TAB], first[:, :], ALU.subtract))
            step(v.tensor_scalar(first[:, :], first[:, :], float(SLOTS), None, ALU.mult))
            v.tensor_copy(owner_i[:, 0, :], owner[0:1, :])
            v.tensor_scalar(owner_i[:, 1, :], owner[0:1, :], float(E - 1), None, ALU.min).then_inc(owner_ready, 1)
            dve.wait_ge(owner_ready, 1)
            items = dve.value_load(base_i[0:1, E:E + 1], min_val=E, max_val=MAX_ITEMS)

            def add_back(t, count):
                r = ROWS[t]
                dve.wait_ge(scat_mm, count)
                for hh in range(2):
                    cs = slice(HALF * hh, HALF * (hh + 1))
                    ins = v.tensor_tensor(acc[0:r, t, cs], acc[0:r, t, cs], bank[6 + hh][0:r, :], ALU.add)
                ins.then_inc(scat_add, 1)

            with dve.Fori(0, items) as n_e:
                nxt = dve.value_load(owner_i[0:1, 0, bass.ds(n_e + 1, 1)], min_val=0, max_val=E)
                dve.wait_ge(tpa_mm, n_e * 2 + 1)
                for t in range(TT):
                    ins = v.tensor_scalar(ohw[:, t, :], both, item_col[:, 0, t:t + 1], item_col[:, 1, t:t + 1],
                                          ALU.is_equal, ALU.mult)
                ins.then_inc(ohw_ready, 1)
                dve.wait_ge(ohw_ready, n_e + 1)
                v.tensor_scalar(item_col[:, 0, :].unsqueeze(2), routed[:, 0, :, bass.ds(nxt, 1)],
                                first[:, bass.ds(n_e + 1, 1)], None, ALU.subtract)
                v.tensor_copy(item_col[:, 1, :].unsqueeze(2), routed[:, 1, :, bass.ds(nxt, 1)]).then_inc(col_ready, 1)
                dve.wait_ge(col_ready, n_e + 1)
                dve.wait_ge(xg_mm, n_e + 1)
                one_hot()
                dve.wait_ge(gate_done, n_e + 1)
                v.tensor_scalar(gmin, bank[3][:, :], LIMIT, None, ALU.min).then_inc(gate_read, 1)
                add_back(0, n_e * 3 + 1)
                dve.wait_ge(gsig_ready, n_e + 1)
                dve.wait_ge(gate_read, n_e + 2)
                v.tensor_tensor(gsig, gmin, gsig, ALU.mult).then_inc(gs_ready, 1)
                add_back(1, n_e * 3 + 2)
                dve.wait_ge(up_done, n_e + 1)
                v.tensor_scalar(ucl, bank[4][:, :], LIMIT, -LIMIT, ALU.min, ALU.max).then_inc(up_read, 1)
                dve.wait_ge(up_read, n_e + 2)
                dve.wait_ge(gs_ready, n_e + 1)
                v.scalar_tensor_tensor(out=acts, in0=ucl, scalar=1.0, in1=gsig,
                                       op0=ALU.add, op1=ALU.mult).then_inc(act_ready, 1)
                add_back(2, n_e * 3 + 3)

            for t in range(TT):
                add_back(t, items * 3 + (t + 1))
            dve.wait_ge(scat_add, items * 3 + 4)
            for t in range(TT):
                r = ROWS[t]
                step(v.tensor_tensor(acc[0:r, t, :], acc[0:r, t, :], g2b[0:r, t // 2, :], ALU.mult))
                v.tensor_tensor(acc[0:r, t, :], acc[0:r, t, :], x[0:r, t, :], ALU.add).then_inc(ssq3, 1)
            dve.wait_ge(ssq3, TT)
            dve.wait_ge(sqrt3, TT)
            rstd(stat[:, 20:23], 3)
            dve.wait_ge(fg_ld, 16)
            for t in range(TT):
                r = ROWS[t]
                v.scalar_tensor_tensor(out=ybuf[0:r, t, :], in0=acc[0:r, t, :], scalar=stat[0:r, 4 + t:5 + t],
                                       in1=fgb[0:r, :], op0=ALU.mult, op1=ALU.mult).then_inc(y_ready, 1)

        @block.tensor
        def _(pe):
            mm, tr = nc.tensor.matmul, nc.tensor.transpose

            pe.wait_ge(const, 4)
            pe.wait_ge(c_ld, 16 * 8)
            tr(bank[5][:, 0:N_COLS], stage[:, :], ident[0:N_COLS, 0:N_COLS]).then_inc(colT, 1)
            pe.wait_ge(dw_ld, 16)
            for c in range(CT):
                ins = tr(bank[7][:, 32 * c:32 * c + WIDTH], dw_stage[:, P * c:P * (c + 1)], ident[0:WIDTH, 0:WIDTH])
            ins.then_inc(dwT, 1)
            pe.wait_ge(st_ld, 32)
            for c in range(CT):
                tr(bank[6][:, 32 * c:32 * c + POOL_PAD], pool_stage[0][:, P * c:P * (c + 1)], ident[0:POOL_PAD, 0:POOL_PAD])
            for c in range(CT):
                ins = tr(bank[6][:, 128 + 32 * c:128 + 32 * c + CONV_PAD], pool_stage[1][:, P * c:P * (c + 1)],
                         ident[0:CONV_PAD, 0:CONV_PAD])
            ins.then_inc(stT, 1)

            def transposes(src, k, done):
                for t in range(TT):
                    r = ROWS[t]
                    ins = tr(bank[k % 4][:, P * t:P * t + r], src[0:r, t, P * k:P * (k + 1)], ident[0:r, 0:r])
                ins.then_inc(done, 1)

            pe.wait_ge(xn_ready, TT)
            for k in range(KD):
                if k >= 4:
                    pe.wait_ge(xT_ev, k - 3)
                transposes(h2, k, xT)

            def modulation(b, out):
                f0 = first_of[("ada", b)]
                for k in range(KD):
                    front_ready(pe, f0 + k)
                    for j in range(4):
                        ins = mm(out[32 * j:32 * j + 32, :], cT[:, k, :], ring[:, (f0 + k) % RING, HALF * j:HALF * (j + 1)],
                                 start=(k == 0), stop=False, skip_group_check=True)
                    ins.then_inc(piece_used, 1)
                for j in range(4):
                    ins = mm(out[32 * j:32 * j + 32, :], ada_sel[:, 4 * b + j, :], bada[:, :], start=False, stop=True,
                             skip_group_check=True)
                ins.then_inc(ada_mm, 1)

            pe.wait_ge(cT_ready, 1)
            pe.wait_ge(ada_ld, 16)
            modulation(0, bank[4])
            pe.wait_ge(rows_ready, 1)
            pe.wait_ge(dw_ready, 1)
            for r in range(4):
                ins = tr(bank[7][:, P * r:P * (r + 1)], rows[:, 0, P * r:P * (r + 1)], ident[:, :])
            ins.then_inc(modT, 1)

            pe.wait_ge(xT_ev, KD)
            for n in range(12):
                f = first_of[("in", (4, 2, 5, 3, 0, 1)[n // 2])]
                w = front_piece(f)[1]
                front_ready(pe, f)
                if n >= 4:
                    m = n - 4
                    if m in (0, 1, 4, 5):
                        pe.wait_ge(sig_ready, (m if m < 2 else m - 2) + 1)
                    elif m < 8:
                        pe.wait_ge(u_ready, (m - 2 if m < 4 else m - 4) + 1)
                for k in range(KD):
                    if n == 0:
                        pe.wait_ge(hT_ready, k + 1)
                    ins = mm(bank[n % 4][:, 0:TOK], w[:, k, P * (n % 2):P * (n % 2 + 1)], hT[:, k, :],
                             start=(k == 0), stop=(k == KD - 1))
                ins.then_inc(in_mm, 1)
                if n % 2:
                    pe.wait_ge(in_mm, n + 1)
                    pe.sem_inc(piece_used, 1)
            for n in range(2 * KD):
                f = first_of[("gate", n // 2)]
                w = front_piece(f)[1]
                front_ready(pe, f)
                if n < 4:
                    pe.wait_ge(pu_ready, n + 1)
                else:
                    pe.wait_ge(gate_ev, n - 3)
                for k in range(KD):
                    ins = mm(bank[n % 4][:, 0:TOK], w[:, k, P * (n % 2):P * (n % 2 + 1)], hT[:, k, :],
                             start=(k == 0), stop=(k == KD - 1))
                ins.then_inc(gate_mm, 1)
                if n % 2:
                    pe.wait_ge(gate_mm, n + 1)
                    pe.sem_inc(piece_used, 1)
            modulation(1, bank[4])
            modulation(2, bank[5])
            pe.wait_ge(hist_ready, 2)
            pe.wait_ge(mod_ready, 2)
            pe.wait_ge(u_ready, 4)
            for i, (src, c0, r) in enumerate(((up_ext, POOL_PAD + NP_TOK - POOL_PAD, POOL_PAD),
                                              (up_ext, PEXT - POOL_PAD, POOL_PAD),
                                              (uc_ext, CONV_PAD + NP_TOK - CONV_PAD, CONV_PAD),
                                              (uc_ext, CEXT - CONV_PAD, CONV_PAD))):
                if i >= 2:
                    pe.wait_ge(out_ev, i - 1)
                for c in range(CT):
                    ins = tr(bank[6 + i % 2][0:r, P * c:P * (c + 1)], src[:, c, c0:c0 + r], ident[:, :])
                ins.then_inc(outT, 1)
            f = first_of[("pool", 0)]
            w = front_piece(f)[1]
            front_ready(pe, f)
            for m in range(KD):
                pe.wait_ge(pooled_ready, m // 2 + 1)
                if m >= 4:
                    pe.wait_ge(pm_ev, m - 3)
                else:
                    pe.wait_ge(gate_ev, 2 * KD - 3 + m)
                ins = mm(bank[m % 4][:, 0:TOK], w[:, m // 2, P * (m % 2):P * (m % 2 + 1)], pooled[:, m // 2, :],
                         start=True, stop=True)
                ins.then_inc(pm_mm, 1)
            pe.wait_ge(pm_mm, KD)
            pe.sem_inc(piece_used, 1)

            pe.wait_ge(conv_step, CT * WIDTH)
            pe.wait_ge(out_ev, 4)
            for c in range(CT):
                ins = mm(bank[6][:, 0:CW], ones[:, :], yc[:, c, :], start=(c == 0), stop=(c == CT - 1))
            ins.then_inc(mean_mm, 1)
            pe.wait_ge(sq_ready, 1)
            for c in range(CT):
                ins = mm(bank[7][:, 0:CW], ones[:, :], tmp[:, c, :], start=(c == 0), stop=(c == CT - 1))
            ins.then_inc(var_mm, 1)
            pe.wait_ge(act_c_ready, 1)
            pe.wait_ge(pm_ev, KD)
            for m in range(KD):
                f = first_of[("conv", m // 4)]
                w = front_piece(f)[1]
                front_ready(pe, f)
                if m >= 4:
                    pe.wait_ge(cm_ev, m - 3)
                for c in range(CT):
                    ins = mm(bank[m % 4][:, 0:TOK], w[:, c, P * (m % 4):P * (m % 4 + 1)], act_c[:, c, :],
                             start=(c == 0), stop=(c == CT - 1))
                ins.then_inc(cm_mm, 1)
                if m % 4 == 3:
                    pe.wait_ge(cm_mm, m + 1)
                    pe.sem_inc(piece_used, 1)
            pe.wait_ge(const, 8)
            pe.wait_ge(rows_ready, 3)
            pe.wait_ge(a2rows, 1)
            for i in range(16):
                which, gg, hh = i // 4, (i // 2) % 2, i % 2
                b, j = ((2, 2), (1, 0), (1, 2), (2, 0))[which]
                if i >= 4:
                    pe.wait_ge(bc_ev, i - 3)
                else:
                    pe.wait_ge(cm_ev, 5 + i)
                mm(bank[i % 4][:, :], pick[:, 2 * (j + hh) + gg, :], rows[:, b, :], start=True, stop=True) \
                    .then_inc(bc_mm, 1)
            pe.wait_ge(merged_ready, KD)
            for hh in range(2):
                for q in range(2):
                    f = first_of[("out", hh)] + q
                    w = front_piece(f)[1]
                    front_ready(pe, f)
                    for t in range(TT):
                        i = hh * TT + t
                        r = ROWS[t]
                        if i >= 4 and q == 0:
                            pe.wait_ge(wo_ev, i - 3)
                        for k in range(4):
                            ins = mm(bank[4 + i % 4][0:r, :], merged[:, 4 * q + k, P * t:P * t + r], w[:, k, :],
                                     start=(q == 0 and k == 0), stop=(q == 1 and k == 3), skip_group_check=True)
                        if q == 1:
                            ins.then_inc(wo_mm, 1)
                    if q == 0:
                        ins.then_inc(piece_used, 1)
                    else:
                        pe.wait_ge(wo_mm, i + 1)
                        pe.sem_inc(piece_used, 1 if hh == 0 else F_END - N_FRONT)
            pe.wait_ge(h2_ready, TT)
            for k in range(KD):
                if k >= 4:
                    pe.wait_ge((h2T_even, h2T_odd)[k % 2], k // 2 - 1)
                else:
                    pe.wait_ge(bc_ev, 13 + k)
                transposes(h2, k, h2T_mm)
            pe.wait_ge(h2T_even, KD // 2)
            pe.wait_ge(h2T_odd, KD // 2)
            pe.wait_ge(router_ld, 32)
            for t in range(TT):
                r = ROWS[t]
                out = bank[4][0:r, E * t:E * (t + 1)]
                for k in range(KD):
                    mm(out, h2T[:, k, P * t:P * t + r], rw[:, k, :], start=(k == 0), stop=False)
                ins = mm(out, ones[0:1, 0:r], rb[:, :], start=False, stop=True)
            ins.then_inc(logit_mm, 1)
            pe.wait_ge(sel_ready, 1)
            for t in range(TT):
                r = ROWS[t]
                out = bank[5][0:r, E * t:E * (t + 1)]
                for s in range(t):
                    mm(out, ones[:, 0:r], rt[:, 7, s, :], start=(s == 0), stop=False)
                mm(out, before[0:r, 0:r], rt[0:r, 7, t, :], start=(t == 0), stop=True)
            for s in range(TT):
                ins = mm(bank[5][:, 3 * E:4 * E], ones[0:ROWS[s], :], rt[0:ROWS[s], 7, s, :], start=(s == 0), stop=(s == 2))
            ins.then_inc(rank_mm, 1)
            pe.wait_ge(w_ready, 1)
            for t in range(TT):
                r = ROWS[t]
                ins = tr(bank[6][0:E, P * t:P * t + r], routed[0:r, 1, t, 0:E], ident[0:r, 0:r])
            ins.then_inc(wT_mm, 1)
            pe.wait_ge(wT_ev, 1)
            pe.wait_ge(bd_ld, 16)
            for i in range(2 * TT):
                r = ROWS[i // 2]
                if i >= 4:
                    pe.wait_ge(acc_init, i - 3)
                mm(bank[i % 4][0:r, :], wT[0:E, P * (i // 2):P * (i // 2) + r],
                   bd_rows[:, HALF * (i % 2):HALF * (i % 2 + 1)], start=True, stop=True).then_inc(accb_mm, 1)
            pe.wait_ge(acc_init, 2 * TT)

            def gather(n_next):
                pe.wait_ge(oh_ready, n_next + 1)
                if not isinstance(n_next, int):
                    pe.wait_ge(xg_ev, n_next)
                for t in range(TT):
                    for hh in range(2):
                        ins = mm(bank[0][64 * hh:64 * hh + 64, :], oh[:, t, :],
                                 h2[:, t, HALF * hh:HALF * (hh + 1)], start=(t == 0), stop=(t == TT - 1),
                                 skip_group_check=True)
                ins.then_inc(xg_mm, 1)

            def turn_tokens(n_next):
                pe.wait_ge(xg_ev, n_next + 1)
                if not isinstance(n_next, int):
                    pe.wait_ge(tpa_ev, n_next * 2)
                for j in range(4):
                    ins = tr(bank[1][:, P * j:P * (j + 1)], xg[:, P * j:P * (j + 1)], ident[:, :])
                ins.then_inc(tpa_mm, 1)

            def product(out, lhs, n_i, c0, done, scatter_mid=None):
                for k in range(KD):
                    s = c0 + k // 2
                    if k % 2 == 0:
                        pe.wait_ge(weights_ready, n_i * PIECES + (s + 1))
                    for hh in range(2):
                        ins = mm(out[64 * hh:64 * hh + 64, :], lhs(k),
                                 ring[:, s, D * (k % 2) + HALF * hh:D * (k % 2) + HALF * (hh + 1)],
                                 start=(done is y_mm and k == 0), stop=(done is y_mm and k == KD - 1) or k == KD - 1,
                                 skip_group_check=True)
                    if k % 2 and k != KD - 1:
                        ins.then_inc(piece_used, 1)
                    if k == 3 and scatter_mid:
                        scatter_mid()
                ins.then_inc(done, 1)

            def bias(out, row, before_used=None):
                for hh in range(2):
                    ins = mm(out[64 * hh:64 * hh + 64, :], ones[0:1, 0:SLOTS],
                             bias_row[:, row, HALF * hh:HALF * (hh + 1)], start=True, stop=False, skip_group_check=True)
                    if hh == 0 and before_used:
                        ins.then_inc(before_used, 1)

            def half_of(buf, k):
                return buf[:, P * (k % 4) + 64 * (k // 4):P * (k % 4) + 64 * (k // 4) + 64]

            def scatter(t, group, before_used=None):
                if not isinstance(group, int):
                    pe.wait_ge(scat_add, group + 1)
                for hh in range(2):
                    ins = mm(bank[6 + hh][:, :], ohwT[64 * hh:64 * hh + 64, P * t:P * (t + 1)],
                             ysb[64 * hh:64 * hh + 64, :], start=True, stop=True)
                    if hh == 0 and before_used:
                        ins.then_inc(before_used, 1)
                ins.then_inc(scat_mm, 1)

            gather(0)
            turn_tokens(0)
            pe.wait_ge(work_zero, 2)
            pe.wait_ge(base_ready, 1)

            items = pe.value_load(base_i[0:1, E:E + 1], min_val=E, max_val=MAX_ITEMS)
            with pe.Fori(0, items) as n:
                pe.wait_ge(tpa_ev, n * 2 + 1)
                pe.wait_ge(gate_read, n + 1)
                pe.wait_ge(bias_ld, n * 32 + 32)
                bias(bank[3], 0, piece_used)
                product(bank[3], lambda k: half_of(xgT, k), n, 0, gate_done)
                pe.wait_ge(y_ev, n + 1)
                scatter(0, n * 3, piece_used)
                pe.wait_ge(up_read, n + 1)
                bias(bank[4], 1)
                product(bank[4], lambda k: half_of(xgT, k), n, 4, up_done, lambda: scatter(1, n * 3 + 1))
                scatter(2, n * 3 + 2, piece_used)
                gather(n + 1)
                pe.wait_ge(tpa_ev, n * 2 + 1)
                pe.wait_ge(ohw_ready, n + 1)
                for t in range(TT):
                    ins = tr(bank[1][:, P * t:P * (t + 1)], ohw[:, t, :], ident[:, :])
                ins.then_inc(tpa_mm, 1)
                pe.wait_ge(act_ready, n + 1)
                pe.wait_ge(actT_ev, n + 1)
                for j in range(4):
                    ins = tr(bank[2][:, P * j:P * (j + 1)], acts[:, P * j:P * (j + 1)], ident[:, :])
                ins.then_inc(actT_mm, 1)
                turn_tokens(n + 1)
                pe.wait_ge(actT_ev, n + 2)
                pe.wait_ge(y_ev, n + 1)
                product(bank[5], lambda k: half_of(actT, k), n, 8, y_mm)
            pe.wait_ge(y_ev, items + 1)
            for t in range(TT):
                scatter(t, items * 3 + t)


_INS = ["x_prompt", "x_sample", "state_pool", "state_conv", "c_prompt", "c_sample", "norm1_g", "norm2_g", "final_g",
        "w_ada", "b_ada", "w_in", "pool_w", "pool_scale", "conv_dw", "conv_b", "conv_ln_g", "conv_ln_b", "conv_w_out",
        "gate_w", "gate_b", "w_out", "router_w", "router_b", "exp_w_gate", "exp_b_gate", "exp_w_up", "exp_b_up",
        "exp_w_down", "exp_b_down"]
_OUTS = [(1, 256, 1024), (1, 32, 1024), (1, 1, 15, 512), (1, 1, 30, 512), (1, 1, 15, 512), (1, 1, 30, 512)]


def kernel(**inputs):
    import numpy as _np
    import concourse.bacc as _bacc
    from concourse import mybir as _mybir
    from concourse.bass_utils import run_bass_kernel_spmd as _run

    nc = _bacc.Bacc("TRN2", target_bir_lowering=False, num_devices=1)
    arrays, args = {}, []
    for name in _INS:
        a = _np.ascontiguousarray(inputs[name])
        arrays[f"in_{name}"] = a
        args.append(nc.dram_tensor(f"in_{name}", a.shape, _mybir.dt.from_np(a.dtype), kind="ExternalInput").ap())
    for i, shape in enumerate(_OUTS):
        args.append(nc.dram_tensor(f"out_{i}", shape, _mybir.dt.float32, kind="ExternalOutput").ap())
    build(nc, *args)
    r = _run(nc, [arrays], core_ids=[0])
    return tuple(r.results[0][f"out_{i}"] for i in range(len(_OUTS)))
```

```python
from contextlib import ExitStack

import concourse.bass as bass
from concourse import mybir

F32 = mybir.dt.float32
I32 = mybir.dt.int32
ALU = mybir.AluOpType
ACT = mybir.ActivationFunctionType
AX = mybir.AxisListType.X

P = 128
D = 1024
KD = D // P
NP_TOK, NS_TOK = 256, 32
TOK = NP_TOK + NS_TOK
TT = 3
ROWS = [P, P, NS_TOK]
EPS = 1e-6
WINDOWS = (2, 4, 8, 16)
POOL_PAD = max(WINDOWS) - 1
WIDTH = 31
CONV_PAD = WIDTH - 1
DC = D // 2
CT = DC // P
E = 32
TOPK = 4
LIMIT = 7.0
FAR = 3.4028234e38
ALPHA = 1.702
SLOTS = 64
MAX_ITEMS_E = -(-TOK // SLOTS)
MAX_ITEMS = E + TOPK * TOK // SLOTS
N_TAB = MAX_ITEMS + 2
HALF = 512
PSEG = [(POOL_PAD, 0, NP_TOK), (2 * POOL_PAD + NP_TOK, NP_TOK, NS_TOK)]
CSEG = [(CONV_PAD, 0, NP_TOK), (2 * CONV_PAD + NP_TOK, NP_TOK, NS_TOK)]
PEXT = TOK + 2 * POOL_PAD
CEXT = TOK + 2 * CONV_PAD
CW = CEXT - CONV_PAD

RING = 12
SLOT = 2 * D
PIECES = 12
FRONT = ([("ada", 0, k) for k in range(KD)] + [("in", c, 0) for c in (4, 2, 5, 3, 0, 1)]
         + [piece for c in range(8)
            for piece in (("gate", c, 0), ("ada", 1 + c // 4, 2 * c % 8), ("ada", 1 + c // 4, 2 * c % 8 + 1))]
         + [("pool", 0, 0)] + [("conv", h, 0) for h in range(2)] + [("out", q, h) for h in range(2) for q in range(2)])
N_FRONT = len(FRONT)
F_END = -(-N_FRONT // RING) * RING
USES = [len([f for f in range(N_FRONT) if f % RING == s]) for s in range(RING)]

CONV_SPLIT = 18
STATES_AT, MEAN_AT, VAR_AT = (1, 2), 5, 7
LAST_ORDER = (0, 1, 2)
OUT_ORDER = (0, 2, 1)
WO_BANK = ((4, 5), (7, 4), (6, 6))
H2T_BANK = ((0, 1), (0, 1), (2, 3))

C_N1, C_GB, C_PS, C_CB, C_LG, C_LB, N_COLS = 0, 8, 24, 32, 36, 40, 44


def build(nc, x_prompt, x_sample, state_pool, state_conv, c_prompt, c_sample, norm1_g, norm2_g, final_g,
          w_ada, b_ada, w_in, pool_w, pool_scale, conv_dw, conv_b, conv_ln_g, conv_ln_b, conv_w_out,
          gate_w, gate_b, w_out, router_w, router_b, exp_w_gate, exp_b_gate, exp_w_up, exp_b_up,
          exp_w_down, exp_b_down, y_prompt, y_sample, new_pool_p, new_conv_p, new_pool_s, new_conv_s):
    with ExitStack() as ctx:
        def sb(name, shape, dt=F32):
            return ctx.enter_context(nc.sbuf_tensor(name, shape, dt))

        def sem(name):
            return ctx.enter_context(nc.semaphore(name))

        ring = sb("ring", [P, RING, SLOT])
        x = sb("x", [P, TT, D])
        h2 = sb("h2", [P, TT, D])
        ident = sb("ident", [P, P])
        before = sb("before", [P, P])
        ones = sb("ones", [P, P])
        slot_no = sb("slot_no", [P, 2, SLOTS])
        ada_sel = sb("ada_sel", [12, 12, 32])
        bada = sb("bada", [12, HALF])
        n2rows = sb("n2rows", [64, HALF])
        stage = sb("stage", [N_COLS, P])
        c_stage = sb("c_stage", [2 * KD, P])
        c_cols = sb("c_cols", [P, 2 * KD])
        cols = sb("cols", [P, N_COLS])
        dwc = sb("dwc", [P, CT, 32])
        biases = sb("biases", [P, 2, D])
        rw = sb("rw", [P, KD, E])
        rb = sb("rb", [1, E])
        cT = sb("cT", [P, KD, 32])
        csig = sb("csig", [P, 16])
        shc = sb("shc", [P, 2 * KD])
        scc = sb("scc", [P, 2 * KD])
        invc = sb("invc", [P, CT, 16])
        stat = sb("stat", [P, 32])
        logit = sb("logit", [P, TT, E])
        rt = sb("rt", [P, 8, TT, E])
        top = sb("top", [P, TT, 8])
        routed = sb("routed", [P, 2, TT, E + 1])
        item_col = sb("item_col", [P, 2, TT])
        base = sb("base", [P, 2, E + 1])
        base_i = sb("base_i", [1, E + 1], I32)
        owner = rt[:, 3, :, :].rearrange("p t e -> p (t e)")[:, 0:N_TAB]
        owner_i = sb("owner_i", [1, N_TAB], I32)
        part_no = sb("part_no", [E, SLOTS])
        mine = sb("mine", [E, SLOTS])
        first = sb("first", [P, N_TAB])
        arena = sb("arena", [P, 15088])

        def view(start, *shape):
            n = 1
            for s in shape:
                n *= s
            a = arena[:, start:start + n]
            if len(shape) == 2:
                a = a.rearrange("p (a b) -> p a b", b=shape[1])
            return a

        hT = view(0, KD, TOK)
        gates = view(2304, 2 * KD, TOK)
        merged = view(6912, KD, TOK)
        sig_g = view(6912, CT, TOK)
        up_ext = view(9216, CT, PEXT)
        pooled = view(10488, CT, TOK)
        wsum = view(11640, 2, PEXT)
        rows = view(12276, 3, HALF)
        tmp = view(13812, CT, CW)
        act_c = view(9216, CT, TOK)
        slot_i = view(13812, 2, SLOTS).bitcast(I32)
        part_i = view(13812 + 2 * SLOTS, SLOTS).bitcast(I32)[0:E, :]
        h2flat = h2[:, :, :].rearrange("p a b -> p (a b)")
        uc_ext = h2flat[:, 0:CT * CEXT].rearrange("p (a b) -> p a b", b=CEXT)
        yc = h2flat[:, CT * CEXT:CT * CEXT + CT * CW].rearrange("p (a b) -> p a b", b=CW)
        g1b = view(0, 2, D)
        a2b = view(2304, 2, D)
        sh2b = view(4352, 2, D)
        g2b = view(9216, 2, D)
        acc = view(2304, TT, D)
        xg = view(5376, HALF)
        xgT = view(5888, HALF)
        ohwT = view(6400, TT * P)
        gmin = view(0, HALF)
        gsig = view(512, HALF)
        ucl = view(1024, HALF)
        acts = view(1536, HALF)
        actT = view(6912, HALF)
        ysb = view(7424, HALF)
        oh = view(7936, TT, SLOTS)
        ohw = view(8320, TT, 2 * SLOTS)
        cmp = view(0, N_TAB, E)
        fgb = view(11640, D)
        bias_table = biases[0:E, :, :]
        ybuf = h2
        h2T = biases[:, :, :].rearrange("p a b -> p (a b)").rearrange("p (k n) -> p k n", k=KD)
        h2T_s = cT
        ln_mean, ln_var = view(6912, CW), view(6912 + CW, CW)

        bank = [ctx.enter_context(nc.psum_tensor(f"bank{i}", [P, HALF], F32)) for i in range(8)]

        slot_ld = [sem(f"slot_ld{s}") for s in range(RING)]
        piece_used = sem("piece_used")
        x_ld = sem("x_ld")
        c_ld = sem("c_ld")
        cols_ld = sem("cols_ld")
        cT1 = sem("cT1")
        c_cols_ready = sem("c_cols_ready")
        dw_ld = sem("dw_ld")
        st_ld = sem("st_ld")
        ada_ld = sem("ada_ld")
        n2_ld = sem("n2_ld")
        router_ld = sem("router_ld")
        bd_ld = sem("bd_ld")
        fg_ld = sem("fg_ld")
        bias_ld = sem("bias_ld")
        weights_ready = sem("weights_ready")
        const = sem("const")
        chain_p = sem("chain_p")
        ssq = sem("ssq")
        chain_v = sem("chain_v")
        chain_a = sem("chain_a")
        xn_ready = sem("xn_ready")
        colT = sem("colT")
        cols_ready = sem("cols_ready")
        csig_ready = sem("csig_ready")
        cT_ready = sem("cT_ready")
        dwT = sem("dwT")
        dw_ready = sem("dw_ready")
        stT = sem("stT")
        hist_ready = sem("hist_ready")
        xT = sem("xT")
        xT_ev = sem("xT_ev")
        ada_mm = sem("ada_mm")
        rows_ready = sem("rows_ready")
        modT = sem("modT")
        mod_ready = sem("mod_ready")
        hT_ready = sem("hT_ready")
        in_mm = sem("in_mm")
        sig_ready = sem("sig_ready")
        u_ready = sem("u_ready")
        pu_ready = sem("pu_ready")
        gate_mm = sem("gate_mm")
        gate_ev = sem("gate_ev")
        a2rows = sem("a2rows")
        outT = sem("outT")
        out_ev = sem("out_ev")
        pooled_ready = sem("pooled_ready")
        conv_step = sem("conv_step")
        mean_mm = sem("mean_mm")
        mean_ready = sem("mean_ready")
        cen_ready = sem("cen_ready")
        sq_ready = sem("sq_ready")
        zeroed = sem("zeroed")
        var_mm = sem("var_mm")
        std_ready = sem("std_ready")
        yn_ready = sem("yn_ready")
        zsig_ready = sem("zsig_ready")
        act_c_ready = sem("act_c_ready")
        pm_mm = sem("pm_mm")
        pm_ev = sem("pm_ev")
        cm_mm = sem("cm_mm")
        cm_ev = sem("cm_ev")
        merged_ready = sem("merged_ready")
        h2_zero = sem("h2_zero")
        spread_ld = [sem("g1_ld"), sem("sh2_a2_ld"), sem("g2_ld")]
        rows_out = [sem("rows_out1"), sem("rows_out2")]
        wo_mm = sem("wo_mm")
        wo_ev = sem("wo_ev")
        x_part = sem("x_part")
        x2_ready = sem("x2_ready")
        ssq2 = sem("ssq2")
        sqrt_ready = sem("sqrt_ready")
        mean2 = sem("mean2")
        h2_ready = sem("h2_ready")
        h2T_mm = sem("h2T_mm")
        h2T_ev = [sem("h2T_ev0"), sem("h2T_ev1")]
        hist0_ready = sem("hist0_ready")
        logit_mm = sem("logit_mm")
        shifted = sem("shifted")
        exp_ready = sem("exp_ready")
        sel_ready = sem("sel_ready")
        rank_mm = sem("rank_mm")
        w_ready = sem("w_ready")
        base_ready = sem("base_ready")
        owner_ready = sem("owner_ready")
        work_zero = sem("work_zero")
        acc_zero = sem("acc_zero")
        oh_ready = sem("oh_ready")
        ohw_ready = sem("ohw_ready")
        xg_mm = sem("xg_mm")
        xg_ev = sem("xg_ev")
        xgT_mm = sem("xgT_mm")
        xgT_ev = sem("xgT_ev")
        ohwT_mm = sem("ohwT_mm")
        ohwT_ev = sem("ohwT_ev")
        mine_ready = sem("mine_ready")
        gate_done = sem("gate_done")
        gate_read = sem("gate_read")
        gsig_ready = sem("gsig_ready")
        up_done = sem("up_done")
        up_read = sem("up_read")
        gs_ready = sem("gs_ready")
        act_ready = sem("act_ready")
        actT_mm = sem("actT_mm")
        actT_ev = sem("actT_ev")
        y_mm = sem("y_mm")
        y_ev = sem("y_ev")
        scat_mm = sem("scat_mm")
        scat_add = sem("scat_add")
        col_ready = sem("col_ready")
        ssq3 = sem("ssq3")
        u_mul = sem("u_mul")
        u_done = sem("u_done")
        last_mm = sem("last_mm")
        last_mul = sem("last_mul")
        x3_ready = sem("x3_ready")
        y_ready = sem("y_ready")
        stored = sem("stored")

        mod_rows = nc.dram_tensor("mod_rows", (2, 2, 2 * D), F32, kind="Internal").ap()

        wada_v = w_ada[0].rearrange("(k p) n -> k p n", p=P)
        win_v = w_in[0].rearrange("(k p) n -> p k n", p=P)
        gate_v = gate_w[0].rearrange("(k p) n -> p k n", p=P)
        poolw_v = pool_w[0].rearrange("g c o -> c g o")
        convw_v = conv_w_out[0].rearrange("(k p) n -> p k n", p=P)
        wout_v = w_out[0].rearrange("(k p) n -> p k n", p=P)
        wg_v = exp_w_gate[0].rearrange("e (k p) n -> e p k n", p=P)
        wu_v = exp_w_up[0].rearrange("e (k p) n -> e p k n", p=P)
        wd_v = exp_w_down[0].rearrange("e (k p) n -> e p k n", p=P)

        def front_piece(f):
            kind, a, b = FRONT[f]
            slot = ring[:, f % RING, :]
            if kind == "ada":
                return wada_v[b][:, 4 * HALF * a:4 * HALF * (a + 1)], slot
            if kind in ("in", "gate"):
                src = win_v if kind == "in" else gate_v
                return src[:, :, 256 * a:256 * (a + 1)], slot.rearrange("p (k n) -> p k n", k=KD)
            if kind == "pool":
                return poolw_v, slot[:, 0:D].rearrange("p (k n) -> p k n", k=CT)
            if kind == "conv":
                return convw_v[:, :, HALF * a:HALF * (a + 1)], slot.rearrange("p (k n) -> p k n", k=CT)
            return (wout_v[:, 4 * a:4 * a + 4, HALF * b:HALF * (b + 1)], slot.rearrange("p (k n) -> p k n", k=4))

        def front_ready(eng, f):
            eng.wait_ge(slot_ld[f % RING], 16 * (f // RING + 1))

        first_of = {}
        for f, (kind, a, b) in enumerate(FRONT):
            first_of.setdefault((kind, a), f)
        ada_piece = {(a, b): f for f, (kind, a, b) in enumerate(FRONT) if kind == "ada"}

        pool_stage = [biases[0:POOL_PAD, 0, 0:DC], biases[0:CONV_PAD, 0, DC:D]]
        dw_stage = biases[0:WIDTH, 1, 0:DC]
        out_stage = [biases[0:POOL_PAD, 1, DC:D], biases[0:POOL_PAD, 1, 0:DC],
                     biases[0:CONV_PAD, 0, DC:D], biases[0:CONV_PAD, 0, 0:DC]]

        def last_bank(t, hh):
            return bank[5][32 * hh:32 * hh + 32, :] if t == 2 else bank[(6, 3)[t] + hh][:, :]

        def turned(eng, i, t, half):
            eng.wait_ge(h2T_mm, 2 * i + 1 + half)
            r = ROWS[t]
            src = bank[H2T_BANK[t][half]][:, 0:4 * r].rearrange("p (k n) -> p k n", n=r)
            dst = h2T_s[:, 4 * half:4 * half + 4, :] if t == 2 else h2T[:, 4 * half:4 * half + 4, P * t:P * (t + 1)]
            if half == 0:
                nc.scalar.activation(dst, src, ACT.Copy).then_inc(h2T_ev[0], 1)
            else:
                nc.vector.tensor_copy(dst, src).then_inc(h2T_ev[1], 1)

        block = ctx.enter_context(nc.Block())

        @block.sync
        def _(sp):
            sp.dma_start(x[:, 0:2, :], x_prompt[0].rearrange("(t p) d -> p t d", p=P)).then_inc(x_ld, 16)
            sp.dma_start(x[0:NS_TOK, 2, :], x_sample[0]).then_inc(x_ld, 16)
            for f in range(N_FRONT):
                if f >= RING:
                    sp.wait_ge(piece_used, f - RING + 1)
                src, dst = front_piece(f)
                sp.dma_start(dst, src).then_inc(slot_ld[f % RING], 16)

            def expert(e, last_use):
                for i in range(PIECES):
                    sp.wait_ge(piece_used, last_use(i))
                    w = (wg_v, wu_v, wd_v)[i // 4]
                    sp.dma_start(ring[:, i, :].rearrange("p (k n) -> p k n", k=2),
                                 w[e][:, 2 * (i % 4):2 * (i % 4) + 2, :]).then_inc(slot_ld[i], 16)

            expert(0, lambda i: max(f for f in range(N_FRONT) if f % RING == i) + 1)
            sp.wait_ge(base_ready, 1)
            with sp.Fori(1, E) as e:
                at = sp.value_load(base_i[0:1, bass.ds(e, 1)], min_val=1, max_val=MAX_ITEMS)
                expert(e, lambda i: at * PIECES + (F_END - PIECES + i + 1))
            sp.dma_start(fgb, final_g.rearrange("(a d) -> a d", a=1).broadcast_to([P, D])).then_inc(fg_ld, 16)
            for i, t in enumerate(LAST_ORDER):
                sp.wait_ge(y_ready, i + 1)
                dst = y_sample[0] if t == 2 else y_prompt[0, P * t:P * (t + 1), :]
                sp.dma_start(dst, ybuf[0:ROWS[t], t, :]).then_inc(stored, 16)
            sp.wait_ge(stored, 16 * (4 + TT))

        @block.gpsimd
        def _(pool):
            g = nc.gpsimd
            n = [0]

            def step(ins):
                n[0] += 1
                ins.then_inc(chain_p, 1)
                pool.wait_ge(chain_p, n[0])

            step(g.memset(ident[:, :], 0.0))
            g.affine_select(out=ident[:, :], in_=ident[:, :], compare_op=ALU.not_equal, fill=1.0, base=0,
                            pattern=[[-1, P]], channel_multiplier=1).then_inc(const, 1)
            g.memset(ones[:, :], 1.0).then_inc(const, 1)
            g.memset(cT[:, :, :], 0.0).then_inc(const, 1)
            step(g.memset(ada_sel[:, :, :], 0.0))
            g.affine_select(out=ada_sel[:, :, :], in_=ada_sel[:, :, :], compare_op=ALU.not_equal, fill=1.0,
                            base=0, pattern=[[-1, 12], [0, 32]], channel_multiplier=1).then_inc(const, 1)
            g.memset(up_ext[:, :, 0:POOL_PAD], 0.0).then_inc(const, 1)
            step(g.memset(before[:, :], 1.0))
            g.affine_select(out=before[:, :], in_=before[:, :], compare_op=ALU.is_gt, fill=0.0, base=0,
                            pattern=[[1, P]], channel_multiplier=-1).then_inc(const, 1)
            step(g.iota(slot_i[:, :, :], pattern=[[0, 2], [1, SLOTS]], base=0, channel_multiplier=0))
            step(g.tensor_copy(slot_no[:, :, :], slot_i[:, :, :]))
            step(g.iota(part_i, pattern=[[0, SLOTS]], base=0, channel_multiplier=1))
            step(g.tensor_copy(part_no[:, :], part_i))
            for w in range(CT):
                step(g.tensor_scalar(invc[:, w, :], slot_no[:, 0, 0:16], 1.0, float(WINDOWS[w]), ALU.add, ALU.min))
            g.memset(dwc[:, :, :], 0.0).then_inc(const, 1)
            for w in range(CT):
                pool.wait_ge(pu_ready, w + 1)
                if w == 0:
                    pool.wait_ge(hist_ready, 1)
                    pool.wait_ge(mod_ready, 2)
                src = up_ext[:, w, :]
                for d in range(w + 1):
                    lo = (1 << (d + 1)) - 1
                    dst = wsum[:, d % 2, :]
                    step(g.tensor_tensor(dst[:, lo:], src[:, lo:], src[:, lo - (1 << d):PEXT - (1 << d)], ALU.add))
                    src = dst
                step(g.tensor_tensor(pooled[:, w, 0:16], src[:, POOL_PAD:POOL_PAD + 16], invc[:, w, :], ALU.mult))
                step(g.tensor_scalar(pooled[:, w, 16:NP_TOK], src[:, POOL_PAD + 16:POOL_PAD + NP_TOK],
                                     1.0 / WINDOWS[w], None, ALU.mult))
                c0, t0, m = PSEG[1]
                step(g.tensor_scalar(pooled[:, w, t0:t0 + m], src[:, c0:c0 + m], 1.0 / WINDOWS[w], None, ALU.mult))
                for c0, t0, m in PSEG:
                    ins = g.tensor_tensor(pooled[:, w, t0:t0 + m], pooled[:, w, t0:t0 + m], up_ext[:, w, c0:c0 + m],
                                          ALU.subtract)
                    if t0 == 0:
                        step(ins)
                ins.then_inc(pooled_ready, 1)

            pool.wait_ge(wo_mm, 5)
            g.memset(ysb, 0.0).then_inc(work_zero, 1)
            g.memset(ohw, 0.0).then_inc(work_zero, 1)
            pool.wait_ge(h2_ready, TT)
            g.memset(acc, 0.0).then_inc(acc_zero, 1)
            pool.wait_ge(base_ready, 1)
            items = pool.value_load(base_i[0:1, E:E + 1], min_val=E, max_val=MAX_ITEMS)
            for i in range(PIECES):
                pool.wait_ge(slot_ld[i], (USES[i] + 1) * 16)
                pool.sem_inc(weights_ready, 1)
            pool.wait_ge(owner_ready, 1)
            with pool.Fori(1, items) as n_i:
                e = pool.value_load(owner_i[0:1, bass.ds(n_i, 1)], min_val=0, max_val=E - 1)
                for i in range(PIECES):
                    pool.wait_ge(slot_ld[i], (e + (USES[i] + 1)) * 16)
                    pool.sem_inc(weights_ready, 1)

        @block.scalar
        def _(act):
            a = nc.scalar
            for at, src in ((0, c_prompt[0]), (KD, c_sample[0])):
                act.dma_start(c_stage[at:at + KD, :], src.rearrange("(k p) -> k p", p=P)).then_inc(c_ld, 16)
            small = [(C_N1, norm1_g[0], 8), (C_GB, gate_b[0], 16), (C_PS, pool_scale[0], 8), (C_CB, conv_b[0], 4),
                     (C_LG, conv_ln_g[0], 4), (C_LB, conv_ln_b[0], 4)]
            for at, src, k in small:
                act.dma_start(stage[at:at + k, :], src.rearrange("(k p) -> k p", p=P)).then_inc(cols_ld, 16)
            act.dma_start(bada[:, :], b_ada[0].rearrange("(k n) -> k n", n=HALF)).then_inc(ada_ld, 16)
            act.dma_start(dw_stage, conv_dw[0]).then_inc(dw_ld, 16)
            act.dma_start(pool_stage[0], state_pool[0, 0]).then_inc(st_ld, 16)
            act.dma_start(pool_stage[1], state_conv[0, 0]).then_inc(st_ld, 16)
            act.wait_ge(c_cols_ready, 1)
            a.activation(csig[:, :], c_cols[:, :], ACT.Sigmoid).then_inc(csig_ready, 1)
            n2 = norm2_g[0].rearrange("(a j n) -> a j n", a=1, n=HALF)
            act.wait_ge(zeroed, 1)
            for j in range(2):
                for gg in range(2):
                    act.dma_start(n2rows[32 * j + gg:32 * j + gg + 1, :], n2[:, j, :]).then_inc(n2_ld, 16)
            act.dma_start(rw[:, :, :], router_w[0].rearrange("(k p) e -> p k e", p=P)).then_inc(router_ld, 16)
            act.dma_start(rb[:, :], router_b[0:1, :]).then_inc(router_ld, 16)

            act.wait_ge(x_ld, 32)
            for t in range(TT):
                r = ROWS[t]
                a.activation(view(2304 + D * t, D)[0:r, :], x[0:r, t, :], ACT.Square,
                             accum_out=stat[0:r, t:t + 1]).then_inc(ssq, 1)
            act.wait_ge(mean2, 1)
            a.activation(stat[:, 4:7], stat[:, 8:11], ACT.Sqrt).then_inc(sqrt_ready, 1)
            act.wait_ge(ada_mm, 1)
            a.activation(rows[:, 0, :], bank[4][:, :], ACT.Copy).then_inc(rows_ready, 1)
            act.wait_ge(stT, 1)
            act.wait_ge(xn_ready, 3)
            act.wait_ge(xT, KD)
            a.activation(up_ext[:, :, NP_TOK + POOL_PAD:NP_TOK + 2 * POOL_PAD],
                         bank[6][:, 0:CT * 32].rearrange("p (c n) -> p c n", n=32)[:, :, 0:POOL_PAD],
                         ACT.Copy).then_inc(hist_ready, 1)
            a.activation(uc_ext[:, :, NP_TOK + CONV_PAD:NP_TOK + 2 * CONV_PAD],
                         bank[6][:, 128:128 + CT * 32].rearrange("p (c n) -> p c n", n=32)[:, :, 0:CONV_PAD],
                         ACT.Copy).then_inc(hist_ready, 1)
            for n in range(12):
                if n in (0, 1, 4, 5):
                    c = n if n < 2 else n - 2
                    act.wait_ge(in_mm, n + 1)
                    ins = a.activation(sig_g[:, c, :], bank[n % 4][:, 0:TOK], ACT.Sigmoid)
                    ins.then_inc(sig_ready, 1)
                    act.wait_ge(sig_ready, c + 1)
                elif n >= 8:
                    act.wait_ge(in_mm, n + 1)
                    for c0, t0, m in PSEG:
                        ins = a.activation(up_ext[:, n - 8, c0:c0 + m], bank[n % 4][:, t0:t0 + m], ACT.Copy)
                    ins.then_inc(pu_ready, 1)
            for n in range(2 * KD):
                act.wait_ge(gate_mm, n + 1)
                a.activation(gates[:, n, :], bank[n % 4][:, 0:TOK], ACT.Sigmoid,
                             bias=cols[:, C_GB + n:C_GB + n + 1]).then_inc(gate_ev, 1)
                if n in STATES_AT:
                    for i in range(2 * (n - STATES_AT[0]), 2 * (n - STATES_AT[0]) + 2):
                        act.wait_ge(outT, i + 1)
                        a.activation(out_stage[i], bank[6 + i % 2][0:(POOL_PAD, CONV_PAD)[i // 2], :],
                                     ACT.Copy).then_inc(out_ev, 1)
                elif n == STATES_AT[1] + 1:
                    for i, dst in enumerate((new_pool_p, new_pool_s, new_conv_p, new_conv_s)):
                        act.wait_ge(out_ev, i + 1)
                        act.dma_start(dst[0, 0], out_stage[i]).then_inc(stored, 16)
                elif n == MEAN_AT:
                    act.wait_ge(mean_mm, 1)
                    act.wait_ge(u_ready, CT)
                    a.activation(ln_mean, bank[6][:, 0:CW], ACT.Copy, scale=1.0 / DC).then_inc(mean_ready, 1)
                    act.wait_ge(cen_ready, 1)
                    a.activation(tmp[:, :, :], yc[:, :, :], ACT.Square).then_inc(sq_ready, 1)
                elif n == 9:
                    act.wait_ge(ada_mm, 2)
                    a.activation(rows[:, 1, :], bank[4][:, :], ACT.Copy).then_inc(rows_ready, 1)
                    act.wait_ge(rows_ready, 2)
                    for j in range(4):
                        act.dma_start(mod_rows[0][:, HALF * j:HALF * (j + 1)], rows[32 * j:32 * j + 2, 1, :]) \
                            .then_inc(rows_out[0], 16)
                elif n == VAR_AT:
                    act.wait_ge(chain_a, 1)
                    a.activation(ln_mean, ln_var, ACT.Sqrt).then_inc(std_ready, 1)
                elif n == VAR_AT + 1:
                    act.wait_ge(yn_ready, 1)
                    for c in range(CT):
                        a.activation(tmp[:, c, :], yc[:, c, :], ACT.Sigmoid, scale=cols[:, C_LG + c:C_LG + c + 1],
                                     bias=cols[:, C_LB + c:C_LB + c + 1]).then_inc(zsig_ready, 1)
            act.wait_ge(ada_mm, 3)
            a.activation(rows[:, 2, :], bank[5][:, :], ACT.Copy).then_inc(rows_ready, 1)

            def spread(buf, b, at, done):
                for gg, r in ((0, P), (1, NS_TOK)):
                    act.dma_start(buf[0:r, gg, :], mod_rows[b][gg:gg + 1, D * at:D * (at + 1)].broadcast_to([r, D])) \
                        .then_inc(done, 16)

            act.wait_ge(rows_out[0], 64)
            spread(g1b, 0, 0, spread_ld[0])
            act.wait_ge(a2rows, 1)
            for j in range(4):
                act.dma_start(mod_rows[1][:, HALF * j:HALF * (j + 1)], rows[32 * j:32 * j + 2, 2, :]) \
                    .then_inc(rows_out[1], 16)
            act.wait_ge(merged_ready, KD)
            spread(sh2b, 0, 1, spread_ld[1])
            act.wait_ge(rows_out[1], 64)
            spread(a2b, 1, 0, spread_ld[1])
            spread(g2b, 1, 1, spread_ld[2])
            for i, t in enumerate(OUT_ORDER):
                r = ROWS[t]
                for hh in range(2):
                    act.wait_ge(x2_ready, 2 * i + hh + 1)
                    a.activation(h2[0:r, t, HALF * hh:HALF * (hh + 1)], x[0:r, t, HALF * hh:HALF * (hh + 1)],
                                 ACT.Square, accum_out=stat[0:r, 12 + 3 * hh + t:13 + 3 * hh + t]).then_inc(ssq2, 1)
                act.wait_ge(mean2, 2 + i)
                a.activation(stat[:, 4 + t:5 + t], stat[:, 8 + t:9 + t], ACT.Sqrt).then_inc(sqrt_ready, 1)
                if i == 0:
                    act.wait_ge(stored, 64)
                else:
                    turned(act, i - 1, OUT_ORDER[i - 1], 0)
            turned(act, 2, OUT_ORDER[2], 0)
            act.wait_ge(work_zero, 1)
            for hh in range(2):
                act.dma_start(ysb[64 * hh:64 * hh + E, :], exp_b_down[0][:, HALF * hh:HALF * (hh + 1)]).then_inc(bd_ld, 16)
            act.wait_ge(logit_mm, 1)
            for j, src in enumerate((exp_b_gate, exp_b_up)):
                act.dma_start(bias_table[:, j, :], src[0]).then_inc(bias_ld, 16)
            act.wait_ge(shifted, 1)
            a.activation(rt[:, 5, :, :], rt[:, 4, :, :], ACT.Exp).then_inc(exp_ready, 1)
            act.wait_ge(ohwT_mm, 1)
            a.activation(ohwT, bank[1][:, 0:TT * P], ACT.Copy).then_inc(ohwT_ev, 1)
            act.wait_ge(xg_mm, 1)
            a.activation(xg, bank[0][:, :], ACT.Copy).then_inc(xg_ev, 1)
            act.wait_ge(xgT_mm, 1)
            a.activation(xgT, bank[1][:, :], ACT.Copy).then_inc(xgT_ev, 1)
            act.sem_inc(y_ev, 1)
            act.wait_ge(base_ready, 1)
            items = act.value_load(base_i[0:1, E:E + 1], min_val=E, max_val=MAX_ITEMS)
            with act.Fori(0, items) as n:
                act.wait_ge(gate_read, n + 2)
                a.activation(gsig, gmin, ACT.Sigmoid, scale=ALPHA).then_inc(gsig_ready, 1)
                act.wait_ge(xg_mm, n + 2)
                a.activation(xg, bank[0][:, :], ACT.Copy).then_inc(xg_ev, 1)
                act.wait_ge(xgT_mm, n + 2)
                a.activation(xgT, bank[1][:, :], ACT.Copy).then_inc(xgT_ev, 1)
                act.wait_ge(ohwT_mm, n + 2)
                a.activation(ohwT, bank[1][:, 0:TT * P], ACT.Copy).then_inc(ohwT_ev, 1)
                act.wait_ge(y_mm, n + 1)
                a.activation(ysb, bank[5][:, :], ACT.Copy).then_inc(y_ev, 1)
            for i, t in enumerate(LAST_ORDER):
                r = ROWS[t]
                for hh in range(2):
                    act.wait_ge(x3_ready, 2 * i + hh + 1)
                    a.activation(ring[0:r, t, HALF * hh:HALF * (hh + 1)], x[0:r, t, HALF * hh:HALF * (hh + 1)],
                                 ACT.Square, accum_out=stat[0:r, 18 + 3 * hh + t:19 + 3 * hh + t]).then_inc(ssq3, 1)
                act.wait_ge(mean2, 2 + TT + i)
                a.activation(stat[:, 4 + t:5 + t], stat[:, 8 + t:9 + t], ACT.Sqrt).then_inc(sqrt_ready, 1)

        @block.vector
        def _(dve):
            v = nc.vector
            n = [0]

            def step(ins):
                n[0] += 1
                ins.then_inc(chain_v, 1)
                dve.wait_ge(chain_v, n[0])

            def rstd(sums, count):
                ins = v.tensor_scalar(stat[:, 8:11], sums, 1.0 / D, EPS, ALU.mult, ALU.add)
                ins.then_inc(mean2, 1)
                dve.wait_ge(sqrt_ready, count)
                step(v.reciprocal(stat[:, 4:7], stat[:, 4:7]))

            step(v.memset(stat[:, :], 0.0))
            v.memset(n2rows[:, :], 0.0).then_inc(zeroed, 1)
            dve.wait_ge(cT1, 1)
            v.tensor_copy(c_cols[:, :], bank[5][:, 0:2 * KD]).then_inc(c_cols_ready, 1)
            dve.wait_ge(csig_ready, 1)
            dve.wait_ge(c_cols_ready, 1)
            dve.wait_ge(const, 3)
            v.tensor_tensor(cT[:, :, 0:2], c_cols[:, :].rearrange("p (g k) -> p k g", g=2),
                            csig[:, :].rearrange("p (g k) -> p k g", g=2), ALU.mult).then_inc(cT_ready, 1)
            dve.wait_ge(ssq, TT)
            rstd(stat[:, 0:3], 1)
            for t in range(TT):
                r = ROWS[t]
                v.tensor_scalar(h2[0:r, t, :], x[0:r, t, :], stat[0:r, 4 + t:5 + t], None, ALU.mult).then_inc(xn_ready, 1)
            for k in range(KD):
                dve.wait_ge(xT, k + 1)
                v.tensor_copy(hT[:, k, :], bank[k % 4][:, 0:TOK]).then_inc(xT_ev, 1)
            dve.wait_ge(colT, 1)
            v.tensor_copy(cols[:, :], bank[5][:, 0:N_COLS]).then_inc(cols_ready, 1)
            dve.wait_ge(cols_ready, 1)
            v.memset(uc_ext[:, :, 0:CONV_PAD], 0.0).then_inc(hist0_ready, 1)
            dve.wait_ge(const, 7)
            v.reciprocal(invc[:, :, :], invc[:, :, :]).then_inc(mod_ready, 1)
            dve.wait_ge(modT, 1)
            modv = bank[7][:, :].rearrange("p (r j m) -> p j r m", r=4, m=32)
            four = "p (j r g) -> p j r g"
            step(v.tensor_copy(shc[:, :].rearrange(four, j=2, g=2), modv[:, 0:2, :, 0:2]))
            step(v.tensor_copy(scc[:, :].rearrange(four, j=2, g=2), modv[:, 2:4, :, 0:2]))
            for gg in range(2):
                s = scc[:, :].rearrange("p (k g) -> p g k", g=2)[:, gg, :]
                ins = v.scalar_tensor_tensor(out=s, in0=s, scalar=1.0, in1=cols[:, C_N1:C_N1 + KD],
                                             op0=ALU.add, op1=ALU.mult)
                step(ins) if gg == 0 else ins.then_inc(mod_ready, 1)
            dve.wait_ge(mod_ready, 2)
            dve.wait_ge(xT_ev, KD)
            for k in range(KD):
                for gg, (t0, m) in enumerate(((0, NP_TOK), (NP_TOK, NS_TOK))):
                    ins = v.tensor_scalar(hT[:, k, t0:t0 + m], hT[:, k, t0:t0 + m], scc[:, 2 * k + gg:2 * k + gg + 1],
                                          shc[:, 2 * k + gg:2 * k + gg + 1], ALU.mult, ALU.add)
                ins.then_inc(hT_ready, 1)
            dve.wait_ge(dwT, 1)
            dve.wait_ge(const, 7)
            v.tensor_copy(dwc[:, :, 0:WIDTH], bank[5][:, 0:CT * 32].rearrange("p (c n) -> p c n", n=32)[:, :, 0:WIDTH]) \
                .then_inc(dw_ready, 1)
            dve.wait_ge(hist_ready, 2)
            dve.wait_ge(hist0_ready, 1)
            steps = [0]

            def glu(tiles):
                for c in tiles:
                    m_in = c + 2 if c < 2 else c + 4
                    dve.wait_ge(in_mm, m_in + 1)
                    dve.wait_ge(sig_ready, c + 1)
                    for c0, t0, m in CSEG:
                        ins = v.tensor_tensor(uc_ext[:, c, c0:c0 + m], bank[m_in % 4][:, t0:t0 + m],
                                              sig_g[:, c, t0:t0 + m], ALU.mult)
                    ins.then_inc(u_ready, 1)

            def conv(tiles, k0, k1):
                for k in range(k0, k1):
                    for c in tiles:
                        if k:
                            dve.wait_ge(conv_step, steps[0] - 1)
                        tap = dwc[:, c, k:k + 1]
                        if k == 0:
                            ins = v.tensor_scalar(yc[:, c, :], uc_ext[:, c, 0:CW], tap, cols[:, C_CB + c:C_CB + c + 1],
                                                  ALU.mult, ALU.add)
                        else:
                            ins = v.scalar_tensor_tensor(out=yc[:, c, :], in0=uc_ext[:, c, k:k + CW], scalar=tap,
                                                         in1=yc[:, c, :], op0=ALU.mult, op1=ALU.add)
                        ins.then_inc(conv_step, 1)
                        steps[0] += 1

            glu((0, 1))
            dve.wait_ge(u_ready, 2)
            dve.wait_ge(dw_ready, 1)
            conv((0, 1), 0, CONV_SPLIT)
            glu((2, 3))
            conv((0, 1), CONV_SPLIT, WIDTH)
            dve.wait_ge(u_ready, 4)
            conv((2, 3), 0, WIDTH)
            dve.wait_ge(mean_ready, 1)
            for c in range(CT):
                ins = v.tensor_tensor(yc[:, c, :], yc[:, c, :], ln_mean, ALU.subtract)
            ins.then_inc(cen_ready, 1)
            dve.wait_ge(var_mm, 1)
            v.tensor_scalar(ln_var, bank[7][:, 0:CW], 1.0 / DC, EPS, ALU.mult, ALU.add).then_inc(chain_a, 1)
            dve.wait_ge(std_ready, 1)
            step(v.reciprocal(ln_mean, ln_mean))
            for c in range(CT):
                ins = v.tensor_tensor(yc[:, c, :], yc[:, c, :], ln_mean, ALU.mult)
            ins.then_inc(yn_ready, 1)
            dve.wait_ge(yn_ready, 1)
            dve.wait_ge(zsig_ready, CT)
            for c in range(CT):
                ins = v.tensor_scalar(yc[:, c, :], yc[:, c, :], cols[:, C_LG + c:C_LG + c + 1],
                                      cols[:, C_LB + c:C_LB + c + 1], ALU.mult, ALU.add)
                step(ins)
            dve.wait_ge(pooled_ready, CT)
            dve.wait_ge(out_ev, 2)
            for c in range(CT):
                for (c0, t0, m) in ((0, 0, NP_TOK), (NP_TOK + CONV_PAD, NP_TOK, NS_TOK)):
                    ins = v.tensor_tensor(act_c[:, c, t0:t0 + m], yc[:, c, c0:c0 + m], tmp[:, c, c0:c0 + m], ALU.mult)
            ins.then_inc(act_c_ready, 1)
            dve.wait_ge(act_c_ready, 1)
            dve.wait_ge(out_ev, 4)
            v.memset(h2[:, 2, :], 0.0).then_inc(h2_zero, 1)
            dve.wait_ge(rows_ready, 3)
            dve.wait_ge(n2_ld, 64)
            v.scalar_tensor_tensor(out=rows[0:64, 2, :], in0=rows[0:64, 2, :], scalar=1.0, in1=n2rows[:, :],
                                   op0=ALU.add, op1=ALU.mult).then_inc(a2rows, 1)
            dve.wait_ge(gate_ev, 2 * KD)
            for m in range(KD):
                dve.wait_ge(pm_mm, m + 1)
                v.scalar_tensor_tensor(out=merged[:, m, :], in0=bank[m % 4][:, 0:TOK],
                                       scalar=cols[:, C_PS + m:C_PS + m + 1], in1=gates[:, m, :],
                                       op0=ALU.mult, op1=ALU.mult).then_inc(pm_ev, 1)
            dve.wait_ge(pm_ev, KD)
            for m in range(KD):
                dve.wait_ge(cm_mm, m + 1)
                v.tensor_tensor(gates[:, KD + m, :], bank[m % 4][:, 0:TOK], gates[:, KD + m, :], ALU.mult).then_inc(cm_ev, 1)
                dve.wait_ge(cm_ev, m + 1)
                v.tensor_tensor(merged[:, m, :], merged[:, m, :], gates[:, KD + m, :], ALU.add).then_inc(merged_ready, 1)
            dve.wait_ge(h2_zero, 1)
            wo_reads = [0]

            def add_output(t, hh, src, done):
                r, gg, cs = ROWS[t], t // 2, slice(HALF * hh, HALF * (hh + 1))
                part = view(13812 + HALF * hh, HALF)[0:r, :]
                v.tensor_tensor(part, src, g1b[0:r, gg, cs], ALU.mult).then_inc(wo_ev, 1)
                wo_reads[0] += 1
                dve.wait_ge(wo_ev, wo_reads[0])
                v.tensor_tensor(x[0:r, t, cs], x[0:r, t, cs], part, ALU.add).then_inc(done, 1)

            for i, t in enumerate(OUT_ORDER):
                r, gg = ROWS[t], t // 2
                if i == 0:
                    dve.wait_ge(spread_ld[0], 32)
                for hh in range(2):
                    dve.wait_ge(wo_mm, (1 + hh, 3, 4 + hh)[i])
                    if t == 2:
                        add_output(t, hh, bank[6][64 * hh:64 * hh + 32, :], x_part)
                        dve.wait_ge(x_part, hh + 1)
                        add_output(t, hh, bank[6][64 * hh + 32:64 * hh + 64, :], x2_ready)
                    else:
                        add_output(t, hh, bank[WO_BANK[t][hh]][:, :], x2_ready)
                if i == 0:
                    step(v.memset(logit[:, :, :], 0.0))
                elif i == 2:
                    turned(dve, 1, OUT_ORDER[1], 1)
                dve.wait_ge(ssq2, 2 * i + 2)
                step(v.tensor_tensor(stat[:, t:t + 1], stat[:, 12 + t:13 + t], stat[:, 15 + t:16 + t], ALU.add))
                v.tensor_scalar(stat[:, 8 + t:9 + t], stat[:, t:t + 1], 1.0 / D, EPS, ALU.mult, ALU.add).then_inc(mean2, 1)
                dve.wait_ge(sqrt_ready, 2 + i)
                step(v.reciprocal(stat[:, 4 + t:5 + t], stat[:, 4 + t:5 + t]))
                if i == 0:
                    dve.wait_ge(spread_ld[1], 64)
                step(v.scalar_tensor_tensor(out=h2[0:r, t, :], in0=x[0:r, t, :], scalar=stat[0:r, 4 + t:5 + t],
                                            in1=a2b[0:r, gg, :], op0=ALU.mult, op1=ALU.mult))
                v.tensor_tensor(h2[0:r, t, :], h2[0:r, t, :], sh2b[0:r, gg, :], ALU.add).then_inc(h2_ready, 1)
                if i == 1:
                    dve.wait_ge(stored, 64)
                    turned(dve, 0, OUT_ORDER[0], 1)
                elif i == 2:
                    turned(dve, 2, t, 1)

            def wide(ap):
                return ap.broadcast_to([P, TT, E])

            dve.wait_ge(logit_mm, 1)
            v.tensor_copy(logit[:, 0:2, :], bank[6][:, 0:2 * E].rearrange("p (t e) -> p t e", e=E))
            step(v.tensor_copy(logit[0:NS_TOK, 2, :], bank[6][0:NS_TOK, 2 * E:3 * E]))
            for t in range(TT):
                ins = v.max(top[:, t, :], logit[:, t, :])
            step(ins)
            v.tensor_tensor(rt[:, 4, :, :], logit[:, :, :], wide(top[:, :, 0:1]), ALU.subtract).then_inc(shifted, 1)
            step(v.memset(top[:, :, TOPK:8], FAR))
            for t in range(TT):
                ins = v.match_replace(rt[:, 0, t, :], top[:, t, :], logit[:, t, :], -FAR)
            step(ins)
            v.tensor_tensor(rt[:, 7, :, :], rt[:, 0, :, :], logit[:, :, :], ALU.not_equal).then_inc(sel_ready, 1)
            dve.wait_ge(sel_ready, 1)
            dve.wait_ge(exp_ready, 1)
            step(v.tensor_tensor(rt[:, 5, :, :], rt[:, 5, :, :], rt[:, 7, :, :], ALU.mult))
            step(v.tensor_reduce(stat[:, 24:27], rt[:, 5, :, :], AX, ALU.add))
            step(v.reciprocal(stat[:, 27:30], stat[:, 24:27]))
            for t in range(TT):
                ins = v.tensor_scalar(routed[:, 1, t, 0:E], rt[:, 5, t, :], stat[:, 27 + t:28 + t], None, ALU.mult)
            step(ins)
            dve.wait_ge(work_zero, 2)
            v.tensor_copy(ohw[:, :, 0:E], routed[:, 1, :, 0:E])
            v.tensor_copy(ohw[:, :, SLOTS:SLOTS + E], routed[:, 1, :, 0:E]).then_inc(w_ready, 1)
            dve.wait_ge(w_ready, 1)
            v.memset(routed[:, 1, :, E:E + 1], 0.0)
            v.memset(routed[:, 0, :, E:E + 1], -1.0)
            dve.wait_ge(rank_mm, 1)
            step(v.memset(rt[:, 0, :, :], 0.0))
            step(v.tensor_copy(rt[:, 0, 0:2, :], bank[5][:, 0:2 * E].rearrange("p (t e) -> p t e", e=E)))
            v.tensor_copy(rt[:, 1, 0, :], bank[5][:, 3 * E:4 * E])
            step(v.tensor_copy(rt[0:NS_TOK, 0, 2, :], bank[5][0:NS_TOK, 2 * E:3 * E]))
            step(v.scalar_tensor_tensor(out=rt[:, 0, :, :], in0=rt[:, 0, :, :], scalar=1.0, in1=rt[:, 7, :, :],
                                        op0=ALU.add, op1=ALU.mult))
            step(v.tensor_scalar(routed[:, 0, :, 0:E], rt[:, 0, :, :], -1.0, None, ALU.add))
            both = slot_no[:, :, :].rearrange("p a b -> p (a b)")

            def one_hot():
                for t in range(TT):
                    ins = v.tensor_scalar(oh[:, t, :], slot_no[:, 0, :], item_col[:, 0, t:t + 1], None, ALU.is_equal)
                ins.then_inc(oh_ready, 1)

            for free in (gate_read, up_read, scat_add, actT_ev):
                dve.sem_inc(free, 1)
            step(v.tensor_copy(item_col[:, :, :], routed[:, :, :, 0]))
            one_hot()
            v.tensor_scalar(mine[:, :], part_no[:, :], 0.0, None, ALU.is_equal).then_inc(mine_ready, 1)
            step(v.tensor_scalar(rt[:, 2, 0, :], rt[:, 1, 0, :], float(SLOTS), 1.0, ALU.is_gt, ALU.add))
            for m in range(2, MAX_ITEMS_E):
                step(v.scalar_tensor_tensor(out=rt[:, 2, 0, :], in0=rt[:, 1, 0, :], scalar=float(m * SLOTS),
                                            in1=rt[:, 2, 0, :], op0=ALU.is_gt, op1=ALU.add))
            v.memset(base[:, :, 0:1], 0.0)
            step(v.tensor_copy(base[:, 1, 1:E + 1], rt[:, 2, 0, :]))
            src = 1
            for d in (1, 2, 4, 8, 16):
                v.tensor_copy(base[:, 1 - src, 1:1 + d], base[:, src, 1:1 + d])
                step(v.tensor_tensor(base[:, 1 - src, 1 + d:], base[:, src, 1 + d:], base[:, src, 1:E + 1 - d], ALU.add))
                src = 1 - src
            base_f = base[:, src, :]
            v.tensor_copy(base_i[:, :], base_f[0:1, :]).then_inc(base_ready, 1)

            item_no = slot_no[:, 0, 0:N_TAB].unsqueeze(2).broadcast_to([P, N_TAB, E])
            ends = base_f[:, 1:E + 1].unsqueeze(1).broadcast_to([P, N_TAB, E])
            step(v.tensor_tensor(cmp, item_no, ends, ALU.is_ge))
            step(v.tensor_reduce(owner, cmp, AX, ALU.add))
            step(v.tensor_tensor(cmp, cmp, ends, ALU.mult))
            step(v.tensor_reduce(first[:, :], cmp, AX, ALU.max))
            step(v.tensor_tensor(first[:, :], slot_no[:, 0, 0:N_TAB], first[:, :], ALU.subtract))
            step(v.tensor_scalar(first[:, :], first[:, :], float(SLOTS), None, ALU.mult))
            v.tensor_copy(owner_i[:, :], owner[0:1, :]).then_inc(owner_ready, 1)
            dve.wait_ge(owner_ready, 1)
            items = dve.value_load(base_i[0:1, E:E + 1], min_val=E, max_val=MAX_ITEMS)

            def add_back(tiles, count):
                dve.wait_ge(scat_mm, count)
                for t in tiles:
                    r = ROWS[t]
                    for hh in range(2):
                        cs = slice(HALF * hh, HALF * (hh + 1))
                        src = bank[5][32 * hh:32 * hh + 32, :] if t == 2 else bank[6 + hh][:, :]
                        ins = v.tensor_tensor(acc[0:r, t, cs], acc[0:r, t, cs], src, ALU.add)
                ins.then_inc(scat_add, 1)

            dve.wait_ge(acc_zero, 1)
            with dve.Fori(0, items) as n_e:
                nxt = dve.value_load(owner_i[0:1, bass.ds(n_e + 1, 1)], min_val=0, max_val=E)
                dve.wait_ge(ohwT_mm, n_e + 1)
                for t in range(TT):
                    ins = v.tensor_scalar(ohw[:, t, :], both, item_col[:, 0, t:t + 1], item_col[:, 1, t:t + 1],
                                          ALU.is_equal, ALU.mult)
                ins.then_inc(ohw_ready, 1)
                dve.wait_ge(ohw_ready, n_e + 1)
                v.tensor_scalar(item_col[:, 0, :].unsqueeze(2), routed[:, 0, :, bass.ds(nxt, 1)],
                                first[:, bass.ds(n_e + 1, 1)], None, ALU.subtract)
                v.tensor_copy(item_col[:, 1, :].unsqueeze(2), routed[:, 1, :, bass.ds(nxt, 1)]).then_inc(col_ready, 1)
                dve.wait_ge(col_ready, n_e + 1)
                dve.wait_ge(xg_mm, n_e + 1)
                one_hot()
                dve.wait_ge(gate_done, n_e + 1)
                v.tensor_scalar(gmin, bank[3][:, :], LIMIT, None, ALU.min).then_inc(gate_read, 1)
                add_back((0, 2), n_e * 2 + 1)
                dve.wait_ge(gsig_ready, n_e + 1)
                dve.wait_ge(gate_read, n_e + 2)
                v.tensor_tensor(gsig, gmin, gsig, ALU.mult).then_inc(gs_ready, 1)
                add_back((1,), n_e * 2 + 2)
                dve.wait_ge(up_done, n_e + 1)
                v.tensor_scalar(ucl, bank[4][:, :], LIMIT, -LIMIT, ALU.min, ALU.max).then_inc(up_read, 1)
                dve.wait_ge(up_read, n_e + 2)
                dve.wait_ge(gs_ready, n_e + 1)
                v.scalar_tensor_tensor(out=acts, in0=ucl, scalar=1.0, in1=gsig,
                                       op0=ALU.add, op1=ALU.mult).then_inc(act_ready, 1)
                dve.wait_ge(actT_mm, n_e + 1)
                v.tensor_copy(actT, bank[2][:, :]).then_inc(actT_ev, 1)
                v.tensor_scalar(mine[:, :], part_no[:, :], owner[0:E, bass.ds(n_e + 1, 1)], None,
                                ALU.is_equal).then_inc(mine_ready, 1)

            dve.wait_ge(spread_ld[2], 32)
            dve.wait_ge(scat_add, items * 2 + 1)
            for t in range(TT):
                v.tensor_tensor(acc[0:ROWS[t], t, :], acc[0:ROWS[t], t, :], g2b[0:ROWS[t], t // 2, :],
                                ALU.mult).then_inc(u_mul, 1)
            for t in range(TT):
                dve.wait_ge(u_mul, t + 1)
                v.tensor_tensor(x[0:ROWS[t], t, :], x[0:ROWS[t], t, :], acc[0:ROWS[t], t, :], ALU.add).then_inc(u_done, 1)
            dve.wait_ge(u_done, TT)

            def last_results(i, t):
                r = ROWS[t]
                dve.wait_ge(last_mm, i + 1)
                for hh in range(2):
                    cs = slice(HALF * hh, HALF * (hh + 1))
                    v.tensor_tensor(acc[0:r, t, cs], last_bank(t, hh), g2b[0:r, t // 2, cs], ALU.mult).then_inc(last_mul, 1)
                for hh in range(2):
                    cs = slice(HALF * hh, HALF * (hh + 1))
                    dve.wait_ge(last_mul, 2 * i + hh + 1)
                    v.tensor_tensor(x[0:r, t, cs], x[0:r, t, cs], acc[0:r, t, cs], ALU.add).then_inc(x3_ready, 1)

            def finish(i, t):
                r = ROWS[t]
                dve.wait_ge(ssq3, 2 * i + 2)
                step(v.tensor_tensor(stat[:, t:t + 1], stat[:, 18 + t:19 + t], stat[:, 21 + t:22 + t], ALU.add))
                v.tensor_scalar(stat[:, 8 + t:9 + t], stat[:, t:t + 1], 1.0 / D, EPS, ALU.mult, ALU.add).then_inc(mean2, 1)
                dve.wait_ge(sqrt_ready, 2 + TT + i)
                step(v.reciprocal(stat[:, 4 + t:5 + t], stat[:, 4 + t:5 + t]))
                if i == 0:
                    dve.wait_ge(fg_ld, 16)
                v.scalar_tensor_tensor(out=ybuf[0:r, t, :], in0=x[0:r, t, :], scalar=stat[0:r, 4 + t:5 + t],
                                       in1=fgb[0:r, :], op0=ALU.mult, op1=ALU.mult).then_inc(y_ready, 1)

            for i, t in enumerate(LAST_ORDER):
                last_results(i, t)
                if i:
                    finish(i - 1, LAST_ORDER[i - 1])
            finish(TT - 1, LAST_ORDER[-1])

        @block.tensor
        def _(pe):
            mm, tr = nc.tensor.matmul, nc.tensor.transpose

            def keep_warm(count, out, src):
                for _ in range(count):
                    mm(out, ident[:, :], src, start=True, stop=True)

            pe.wait_ge(const, 4)
            pe.wait_ge(c_ld, 32)
            tr(bank[5][:, 0:2 * KD], c_stage[:, :], ident[0:2 * KD, 0:2 * KD]).then_inc(cT1, 1)

            def modulation(b, out, ks, used_before=0):
                for k in ks:
                    f = ada_piece[(b, k)]
                    front_ready(pe, f)
                    for j in range(4):
                        ins = mm(out[32 * j:32 * j + 32, :], cT[:, k, :], ring[:, f % RING, HALF * j:HALF * (j + 1)],
                                 start=(k == 0), stop=(k == KD - 1), skip_group_check=True)
                        if k == ks[0] and j == 0 and used_before:
                            ins.then_inc(piece_used, used_before)
                    ins.then_inc(ada_mm if k == KD - 1 else piece_used, 1)
                    if k == KD - 3:
                        for j in range(4):
                            mm(out[32 * j:32 * j + 32, :], ada_sel[:, 4 * b + j, :], bada[:, :], start=False, stop=False,
                               skip_group_check=True)

            pe.wait_ge(cT_ready, 1)
            modulation(0, bank[4], range(0, 4))
            pe.wait_ge(xn_ready, TT)
            for k in range(KD):
                if k >= 4:
                    pe.wait_ge(xT_ev, k - 3)
                for t in range(TT):
                    r = ROWS[t]
                    ins = tr(bank[k % 4][:, P * t:P * t + r], h2[0:r, t, P * k:P * (k + 1)], ident[0:r, 0:r])
                ins.then_inc(xT, 1)
            modulation(0, bank[4], range(4, 5))
            pe.wait_ge(ada_ld, 16)
            modulation(0, bank[4], range(5, 6))
            pe.wait_ge(c_cols_ready, 1)
            pe.wait_ge(cols_ld, 16 * 6)
            tr(bank[5][:, 0:N_COLS], stage[:, :], ident[0:N_COLS, 0:N_COLS]).then_inc(colT, 1)
            modulation(0, bank[4], range(6, KD))
            pe.wait_ge(rows_ready, 1)
            for r in range(4):
                ins = tr(bank[7][:, P * r:P * (r + 1)], rows[:, 0, P * r:P * (r + 1)], ident[:, :])
            ins.then_inc(modT, 1)
            pe.wait_ge(xT_ev, KD)
            keep_warm(3, bank[3][:, :], rows[:, 0, :])

            pe.wait_ge(xT_ev, KD)
            for n in range(12):
                f = first_of[("in", (4, 2, 5, 3, 0, 1)[n // 2])]
                w = front_piece(f)[1]
                front_ready(pe, f)
                if n >= 4:
                    m = n - 4
                    if m in (0, 1, 4, 5):
                        pe.wait_ge(sig_ready, (m if m < 2 else m - 2) + 1)
                    elif m < 8:
                        pe.wait_ge(u_ready, (m - 2 if m < 4 else m - 4) + 1)
                for k in range(KD):
                    if n == 0:
                        pe.wait_ge(hT_ready, k + 1)
                    ins = mm(bank[n % 4][:, 0:TOK], w[:, k, P * (n % 2):P * (n % 2 + 1)], hT[:, k, :],
                             start=(k == 0), stop=(k == KD - 1))
                    if k == 0 and n % 2 == 0:
                        ins.then_inc(piece_used, 1)
                ins.then_inc(in_mm, 1)
                if n == 1:
                    pe.wait_ge(cols_ready, 1)
                    pe.wait_ge(dw_ld, 16)
                    for c in range(CT):
                        ins = tr(bank[5][:, 32 * c:32 * c + WIDTH], dw_stage[:, P * c:P * (c + 1)], ident[0:WIDTH, 0:WIDTH])
                    ins.then_inc(dwT, 1)
                    pe.wait_ge(st_ld, 32)
                    for c in range(CT):
                        tr(bank[6][:, 32 * c:32 * c + POOL_PAD], pool_stage[0][:, P * c:P * (c + 1)], ident[0:POOL_PAD, 0:POOL_PAD])
                    for c in range(CT):
                        ins = tr(bank[6][:, 128 + 32 * c:128 + 32 * c + CONV_PAD], pool_stage[1][:, P * c:P * (c + 1)],
                                 ident[0:CONV_PAD, 0:CONV_PAD])
                    ins.then_inc(stT, 1)
            for n in range(2 * KD):
                f = first_of[("gate", n // 2)]
                w = front_piece(f)[1]
                front_ready(pe, f)
                if n < 4:
                    pe.wait_ge(pu_ready, n + 1)
                else:
                    pe.wait_ge(gate_ev, n - 3)
                for k in range(KD):
                    ins = mm(bank[n % 4][:, 0:TOK], w[:, k, P * (n % 2):P * (n % 2 + 1)], hT[:, k, :],
                             start=(k == 0), stop=(k == KD - 1))
                    if k == 0 and n in (0, 8):
                        ins.then_inc(piece_used, 1)
                ins.then_inc(gate_mm, 1)
                if n % 2:
                    b = 1 + n // 8
                    if n == 9:
                        pe.wait_ge(dw_ready, 1)
                    modulation(b, bank[3 + b], range(n % 8 - 1, n % 8 + 1), used_before=1)
                if n in STATES_AT:
                    pe.wait_ge(hist_ready, 2)
                    pe.wait_ge(mod_ready, 2)
                    pe.wait_ge(u_ready, 4)
                    pe.wait_ge(pu_ready, 4)
                    src, width, r = ((up_ext, PEXT, POOL_PAD), (uc_ext, CEXT, CONV_PAD))[n - STATES_AT[0]]
                    for i, c0 in enumerate((NP_TOK, width - r)):
                        if n == STATES_AT[1]:
                            pe.wait_ge(out_ev, i + 1)
                        for c in range(CT):
                            ins = tr(bank[6 + i][0:r, P * c:P * (c + 1)], src[:, c, c0:c0 + r], ident[:, :])
                        ins.then_inc(outT, 1)
                elif n == MEAN_AT:
                    pe.wait_ge(conv_step, CT * WIDTH)
                    pe.wait_ge(out_ev, 4)
                    for c in range(CT):
                        ins = mm(bank[6][:, 0:CW], ones[:, :], yc[:, c, :], start=(c == 0), stop=(c == CT - 1))
                    ins.then_inc(mean_mm, 1)
                elif n == VAR_AT:
                    pe.wait_ge(sq_ready, 1)
                    for c in range(CT):
                        ins = mm(bank[7][:, 0:CW], ones[:, :], tmp[:, c, :], start=(c == 0), stop=(c == CT - 1))
                    ins.then_inc(var_mm, 1)
            f = first_of[("pool", 0)]
            w = front_piece(f)[1]
            front_ready(pe, f)
            for m in range(KD):
                pe.wait_ge(pooled_ready, m // 2 + 1)
                if m >= 4:
                    pe.wait_ge(pm_ev, m - 3)
                else:
                    pe.wait_ge(gate_ev, 2 * KD - 3 + m)
                mm(bank[m % 4][:, 0:TOK], w[:, m // 2, P * (m % 2):P * (m % 2 + 1)], pooled[:, m // 2, :],
                   start=True, stop=True).then_inc(pm_mm, 1)
            pe.wait_ge(act_c_ready, 1)
            for m in range(KD):
                f = first_of[("conv", m // 4)]
                w = front_piece(f)[1]
                front_ready(pe, f)
                if m >= 4:
                    pe.wait_ge(cm_ev, m - 3)
                else:
                    pe.wait_ge(pm_ev, m + 5)
                for c in range(CT):
                    ins = mm(bank[m % 4][:, 0:TOK], w[:, c, P * (m % 4):P * (m % 4 + 1)], act_c[:, c, :],
                             start=(c == 0), stop=(c == CT - 1))
                    if c == 0 and m == 0:
                        ins.then_inc(piece_used, 2)
                    elif c == 0 and m == 4:
                        ins.then_inc(piece_used, 1)
                ins.then_inc(cm_mm, 1)
            def piece(hh, k):
                f = first_of[("out", 0)] + 2 * hh + k // 4
                front_ready(pe, f)
                return front_piece(f)[1][:, k % 4, :]

            def out_half(t, hh, used_before):
                for k in range(KD):
                    w = piece(hh, k)
                    if t == 0 and hh == 0:
                        pe.wait_ge(merged_ready, k + 1)
                    ins = mm(bank[WO_BANK[t][hh]][:, :], merged[:, k, P * t:P * (t + 1)], w, start=(k == 0), stop=(k == KD - 1))
                    if k == 0 and used_before:
                        ins.then_inc(piece_used, used_before)
                ins.then_inc(wo_mm, 1)

            def turn(i, t):
                r = ROWS[t]
                pe.wait_ge(h2_ready, i + 1)
                for half in range(2):
                    if t == 1:
                        pe.wait_ge(h2T_ev[half], 1)
                    for k in range(4 * half, 4 * half + 4):
                        ins = tr(bank[H2T_BANK[t][half]][:, r * (k % 4):r * (k % 4 + 1)], h2[0:r, t, P * k:P * (k + 1)],
                                 ident[0:r, 0:r])
                        if t == 1 and k == 0:
                            ins.then_inc(piece_used, 2 + F_END - N_FRONT - 1)
                    ins.then_inc(h2T_mm, 1)

            pe.wait_ge(rows_ready, 3)
            out_half(0, 0, 1)
            out_half(0, 1, 0)
            for k in range(0, KD, 2):
                for hh in range(2):
                    for odd in range(2):
                        q = 2 * hh + odd
                        w = piece(hh, k + odd)
                        ins = mm(bank[6][32 * q:32 * q + 32, :], merged[:, k + odd, 2 * P:TOK], w,
                                 start=(k == 0), stop=(k == KD - 2), skip_group_check=True)
            ins.then_inc(wo_mm, 1)
            out_half(1, 0, 0)
            pe.wait_ge(cm_ev, KD)
            turn(0, 0)
            pe.wait_ge(wo_ev, 1)
            out_half(1, 1, 2)
            turn(1, 2)

            def logits(i, t):
                r = ROWS[t]
                out = bank[6][0:r, E * t:E * (t + 1)]
                for half in range(2):
                    pe.wait_ge(h2T_ev[half], i + 1)
                for k in range(KD):
                    lhs = h2T[:, k, P * t:P * t + r] if t < 2 else h2T_s[:, k, :]
                    mm(out, lhs, rw[:, k, :], start=(k == 0), stop=False)
                return mm(out, ones[0:1, 0:r], rb[:, :], start=False, stop=True)

            pe.wait_ge(router_ld, 32)
            pe.wait_ge(wo_ev, 6)
            logits(0, 0)
            logits(1, 2)
            keep_warm(3, bank[2][:, :], h2[:, 0, 0:HALF])
            turn(2, 1)
            logits(2, 1).then_inc(logit_mm, 1)
            keep_warm(2, bank[2][:, :], h2[:, 0, 0:HALF])
            pe.wait_ge(sel_ready, 1)
            for t in range(TT):
                r = ROWS[t]
                out = bank[5][0:r, E * t:E * (t + 1)]
                for s in range(t):
                    mm(out, ones[:, 0:r], rt[:, 7, s, :], start=(s == 0), stop=False)
                mm(out, before[0:r, 0:r], rt[0:r, 7, t, :], start=(t == 0), stop=True)
            for s in range(TT):
                ins = mm(bank[5][:, 3 * E:4 * E], ones[0:ROWS[s], :], rt[0:ROWS[s], 7, s, :], start=(s == 0), stop=(s == 2))
            ins.then_inc(rank_mm, 1)
            keep_warm(1, bank[2][:, :], h2[:, 0, 0:HALF])
            pe.wait_ge(w_ready, 1)
            for t in range(TT):
                ins = tr(bank[1][:, P * t:P * (t + 1)], ohw[:, t, :], ident[:, :])
            ins.then_inc(ohwT_mm, 1)
            keep_warm(1, bank[2][:, :], h2[:, 0, 0:HALF])

            def gather(n_next, before_used=None):
                pe.wait_ge(oh_ready, n_next + 1)
                if not isinstance(n_next, int):
                    pe.wait_ge(xg_ev, n_next)
                for t in range(TT):
                    for hh in range(2):
                        ins = mm(bank[0][64 * hh:64 * hh + 64, :], oh[:, t, :],
                                 h2[:, t, HALF * hh:HALF * (hh + 1)], start=(t == 0), stop=(t == TT - 1),
                                 skip_group_check=True)
                        if t == 0 and hh == 0 and before_used:
                            ins.then_inc(before_used, 1)
                ins.then_inc(xg_mm, 1)

            def turn_tokens(n_next):
                pe.wait_ge(xg_ev, n_next + 1)
                for j in range(4):
                    ins = tr(bank[1][:, P * j:P * (j + 1)], xg[:, P * j:P * (j + 1)], ident[:, :])
                ins.then_inc(xgT_mm, 1)

            def product(out, lhs, n_i, c0, done, mid=None):
                for k in range(KD):
                    s = c0 + k // 2
                    if k % 2 == 0:
                        pe.wait_ge(weights_ready, n_i * PIECES + (s + 1))
                    for hh in range(2):
                        ins = mm(out[64 * hh:64 * hh + 64, :], lhs(k),
                                 ring[:, s, D * (k % 2) + HALF * hh:D * (k % 2) + HALF * (hh + 1)],
                                 start=(done is y_mm and k == 0), stop=(done is y_mm and k == KD - 1) or k == KD - 1,
                                 skip_group_check=True)
                    if k % 2 and k != KD - 1:
                        ins.then_inc(piece_used, 1)
                    if k == 3 and mid:
                        mid()
                ins.then_inc(done, 1)

            def bias(out, row, before_used=None):
                for hh in range(2):
                    ins = mm(out[64 * hh:64 * hh + 64, :], mine[:, :],
                             bias_table[:, row, HALF * hh:HALF * (hh + 1)], start=True, stop=False, skip_group_check=True)
                    if hh == 0 and before_used:
                        ins.then_inc(before_used, 1)

            def half_of(buf, k):
                return buf[:, P * (k % 4) + 64 * (k // 4):P * (k % 4) + 64 * (k // 4) + 64]

            def scatter(tiles, group, before_used=None):
                if not isinstance(group, int):
                    pe.wait_ge(scat_add, group + 1)
                for t in tiles:
                    for hh in range(2):
                        out = bank[5][32 * hh:32 * hh + 32, :] if t == 2 else bank[6 + hh][:, :]
                        ins = mm(out, ohwT[64 * hh:64 * hh + 64, P * t:P * t + ROWS[t]],
                                 ysb[64 * hh:64 * hh + 64, :], start=True, stop=True, skip_group_check=True)
                        if hh == 0 and t == tiles[0] and before_used:
                            ins.then_inc(before_used, 1)
                ins.then_inc(scat_mm, 1)

            gather(0)
            keep_warm(1, bank[2][:, :], h2[:, 0, 0:HALF])
            pe.wait_ge(ohwT_ev, 1)
            turn_tokens(0)
            keep_warm(2, bank[2][:, :], h2[:, 0, 0:HALF])
            pe.wait_ge(base_ready, 1)

            items = pe.value_load(base_i[0:1, E:E + 1], min_val=E, max_val=MAX_ITEMS)
            with pe.Fori(0, items) as n:
                pe.wait_ge(xgT_ev, n + 1)
                pe.wait_ge(gate_read, n + 1)
                pe.wait_ge(bias_ld, 32)
                pe.wait_ge(mine_ready, n + 1)
                bias(bank[3], 0, piece_used)
                product(bank[3], lambda k: half_of(xgT, k), n, 0, gate_done)
                pe.wait_ge(bd_ld, 32)
                pe.wait_ge(y_ev, n + 1)
                pe.wait_ge(ohwT_ev, n + 1)
                scatter((0, 2), n * 2, piece_used)
                pe.wait_ge(up_read, n + 1)
                bias(bank[4], 1)
                product(bank[4], lambda k: half_of(xgT, k), n, 4, up_done, lambda: scatter((1,), n * 2 + 1))
                gather(n + 1, piece_used)
                pe.wait_ge(act_ready, n + 1)
                pe.wait_ge(actT_ev, n + 1)
                for j in range(4):
                    ins = tr(bank[2][:, P * j:P * (j + 1)], acts[:, P * j:P * (j + 1)], ident[:, :])
                ins.then_inc(actT_mm, 1)
                turn_tokens(n + 1)
                pe.wait_ge(actT_ev, n + 2)
                pe.wait_ge(scat_add, n * 2 + 2)

                def turn_ohw():
                    pe.wait_ge(ohw_ready, n + 1)
                    pe.wait_ge(xgT_ev, n + 2)
                    for t in range(TT):
                        ins = tr(bank[1][:, P * t:P * (t + 1)], ohw[:, t, :], ident[:, :])
                    ins.then_inc(ohwT_mm, 1)

                product(bank[5], lambda k: half_of(actT, k), n, 8, y_mm, turn_ohw)
            pe.wait_ge(y_ev, items + 1)
            pe.wait_ge(ohwT_ev, items + 1)
            pe.wait_ge(scat_add, items * 2 + 1)
            pe.wait_ge(up_read, items + 1)
            for t in LAST_ORDER:
                for hh in range(2):
                    ins = mm(last_bank(t, hh), ohwT[64 * hh:64 * hh + 64, P * t:P * t + ROWS[t]],
                             ysb[64 * hh:64 * hh + 64, :], start=True, stop=True, skip_group_check=True)
                ins.then_inc(last_mm, 1)


_INS = ["x_prompt", "x_sample", "state_pool", "state_conv", "c_prompt", "c_sample", "norm1_g", "norm2_g", "final_g",
        "w_ada", "b_ada", "w_in", "pool_w", "pool_scale", "conv_dw", "conv_b", "conv_ln_g", "conv_ln_b", "conv_w_out",
        "gate_w", "gate_b", "w_out", "router_w", "router_b", "exp_w_gate", "exp_b_gate", "exp_w_up", "exp_b_up",
        "exp_w_down", "exp_b_down"]
_OUTS = [(1, 256, 1024), (1, 32, 1024), (1, 1, 15, 512), (1, 1, 30, 512), (1, 1, 15, 512), (1, 1, 30, 512)]


def kernel(**inputs):
    import numpy as _np
    import concourse.bacc as _bacc
    from concourse import mybir as _mybir
    from concourse.bass_utils import run_bass_kernel_spmd as _run

    nc = _bacc.Bacc("TRN2", target_bir_lowering=False, num_devices=1)
    arrays, args = {}, []
    for name in _INS:
        a = _np.ascontiguousarray(inputs[name])
        arrays[f"in_{name}"] = a
        args.append(nc.dram_tensor(f"in_{name}", a.shape, _mybir.dt.from_np(a.dtype), kind="ExternalInput").ap())
    for i, shape in enumerate(_OUTS):
        args.append(nc.dram_tensor(f"out_{i}", shape, _mybir.dt.float32, kind="ExternalOutput").ap())
    build(nc, *args)
    r = _run(nc, [arrays], core_ids=[0])
    return tuple(r.results[0][f"out_{i}"] for i in range(len(_OUTS)))
```
